# Optimizing a Trainium2 kernel written in Bass

```python
import jax
import jax.numpy as jnp
from jax import lax
import numpy as np
import math
import jax, jax.numpy as jnp

D_MODEL = 1024
BATCH = 1
SEQ = 2048
DEPTH = 1

N_GROUPS = 5
HEAD_DIM = 64
GROUP_HEADS = 4
GROUP_W = GROUP_HEADS * HEAD_DIM
MIX_W = N_GROUPS * GROUP_W
N_MEM = 256
CHUNK = 128
CONV_K = 4
RWKV_DECAY_RANK = 16
RWKV_A_RANK = 16
EPS = 1e-6

A_COLS = (GROUP_W, GROUP_W, GROUP_W)
B_COLS = (GROUP_W, GROUP_W, GROUP_W, GROUP_HEADS, GROUP_W)
C_COLS = (2 * GROUP_W, GROUP_W, GROUP_HEADS, GROUP_HEADS, GROUP_W, GROUP_W)
D_COLS = (GROUP_W, RWKV_DECAY_RANK, GROUP_W, GROUP_W, RWKV_A_RANK, GROUP_W)
M_COLS = (GROUP_W, GROUP_W)
GROUP_COLS = (sum(A_COLS), sum(B_COLS), sum(C_COLS), sum(D_COLS), sum(M_COLS))
D_W = sum(D_COLS)
IN_COLS = sum(GROUP_COLS)


def rms_norm(x, g):
    xf = x.astype(jnp.float32)
    y = xf * lax.rsqrt(jnp.mean(xf * xf, axis=-1, keepdims=True) + EPS)
    return (y * g.astype(jnp.float32)).astype(x.dtype)

def split_cols(x, widths):
    return jnp.split(x, np.cumsum(widths)[:-1].tolist(), axis=-1)

def to_heads(t):
    return t.reshape(t.shape[:-1] + (GROUP_HEADS, HEAD_DIM))

def causal_dwconv(x, w, b):
    y = lax.conv_general_dilated(
        x, w[:, None, :].astype(x.dtype), (1,), [(CONV_K - 1, 0)],
        dimension_numbers=("NWC", "WIO", "NWC"), feature_group_count=x.shape[-1])
    return y + b

def token_shift(x, mu):
    prev = jnp.pad(x, ((0, 0), (1, 0), (0, 0)))[:, :-1]
    return x + mu * (prev - x)

def spatial_gating(u, v, norm_g, w_s, b_s):
    bsz, seq, _ = u.shape
    nc = seq // CHUNK
    u = jax.nn.gelu(u)
    v = rms_norm(to_heads(jax.nn.gelu(v)), norm_g.reshape(GROUP_HEADS, HEAD_DIM))
    v = v.reshape(bsz, nc, CHUNK, GROUP_HEADS, HEAD_DIM)
    w = jnp.where(jnp.tril(jnp.ones((CHUNK, CHUNK), bool)), w_s, jnp.zeros_like(w_s))
    mixed = jnp.einsum("gts,bcsgd->bctgd", w, v) + b_s.T[:, :, None]
    return u * mixed.reshape(bsz, seq, GROUP_W)

def forgetting_attention(q, k, v, f_logit, q_g, k_g):
    bsz, seq, _ = q.shape
    nb = seq // CHUNK
    q = rms_norm(to_heads(q), q_g)
    k = rms_norm(to_heads(k), k_g)
    v = to_heads(v)
    big_f = jnp.cumsum(jax.nn.log_sigmoid(f_logit.astype(jnp.float32)), axis=1)
    big_f = big_f.transpose(0, 2, 1)
    q_blocks = q.reshape(bsz, nb, CHUNK, GROUP_HEADS, HEAD_DIM).swapaxes(0, 1)
    f_blocks = big_f.reshape(bsz, GROUP_HEADS, nb, CHUNK).transpose(2, 0, 1, 3)
    k_pos = jnp.arange(seq)
    scale = HEAD_DIM ** -0.5

    def one_block(args):
        qb, fb, start = args
        s = jnp.einsum("bthd,bshd->bhts", qb, k).astype(jnp.float32) * scale
        s = s + fb[..., :, None] - big_f[..., None, :]
        q_pos = start + jnp.arange(CHUNK)
        s = jnp.where(k_pos[None, :] <= q_pos[:, None], s, -jnp.inf)
        p = jax.nn.softmax(s, axis=-1).astype(v.dtype)
        return jnp.einsum("bhts,bshd->bthd", p, v)

    out = lax.map(one_block, (q_blocks, f_blocks, jnp.arange(nb) * CHUNK))
    return out.swapaxes(0, 1).reshape(bsz, seq, GROUP_W)

def mlstm(qk, v, i_logit, f_logit, o_logit, conv_w, conv_b, out_g):
    f32 = jnp.float32
    bsz, seq, _ = v.shape
    nc = seq // CHUNK
    q, k = jnp.split(jax.nn.silu(causal_dwconv(qk, conv_w, conv_b)), 2, axis=-1)
    q = to_heads(q).astype(f32)
    k = to_heads(k).astype(f32) * HEAD_DIM ** -0.5
    vh = to_heads(v).astype(f32)
    log_i = i_logit.astype(f32)
    log_f = jax.nn.log_sigmoid(f_logit.astype(f32))

    def chunks(t):
        return t.reshape((bsz, nc, CHUNK) + t.shape[2:]).swapaxes(0, 1)

    causal = jnp.tril(jnp.ones((CHUNK, CHUNK), bool))

    def step(carry, inp):
        c_state, n_state, m_state = carry
        qc, kc, vc, ic, fc = inp
        b = jnp.cumsum(fc, axis=1).swapaxes(1, 2)
        ic = ic.swapaxes(1, 2)
        g = b[..., -1]
        log_d = jnp.where(causal, b[..., :, None] - b[..., None, :] + ic[..., None, :], -jnp.inf)
        inter = b + m_state[..., None]
        m_t = jnp.maximum(jnp.max(log_d, axis=-1), inter)
        s = jnp.einsum("bthd,bshd->bhts", qc, kc) * jnp.exp(log_d - m_t[..., None])
        w_inter = jnp.exp(inter - m_t)
        num = (jnp.einsum("bhts,bshd->bhtd", s, vc)
               + w_inter[..., None] * jnp.einsum("bthk,bhkd->bhtd", qc, c_state))
        den = jnp.sum(s, axis=-1) + w_inter * jnp.einsum("bthk,bhk->bht", qc, n_state)
        h = num / jnp.maximum(jnp.abs(den), jnp.exp(-m_t))[..., None]
        log_w = g[..., None] - b + ic
        m_new = jnp.maximum(g + m_state, jnp.max(log_w, axis=-1))
        w_new = jnp.exp(log_w - m_new[..., None])
        carry_decay = jnp.exp(g + m_state - m_new)
        c_state = carry_decay[..., None, None] * c_state + jnp.einsum("bhs,bshk,bshd->bhkd", w_new, kc, vc)
        n_state = carry_decay[..., None] * n_state + jnp.einsum("bhs,bshk->bhk", w_new, kc)
        return (c_state, n_state, m_new), h.swapaxes(1, 2)

    init = (jnp.zeros((bsz, GROUP_HEADS, HEAD_DIM, HEAD_DIM), f32),
            jnp.zeros((bsz, GROUP_HEADS, HEAD_DIM), f32),
            jnp.zeros((bsz, GROUP_HEADS), f32))
    _, h = lax.scan(step, init, (chunks(q), chunks(k), chunks(vh), chunks(log_i), chunks(log_f)))
    h = h.swapaxes(0, 1).reshape(bsz, seq, GROUP_HEADS, HEAD_DIM)
    h = jax.nn.sigmoid(to_heads(o_logit).astype(f32)) * h
    return rms_norm(h, out_g.reshape(GROUP_HEADS, HEAD_DIM)).reshape(bsz, seq, GROUP_W)

def rwkv7_time_mix(r, w_lo, k, v, a_lo, w0, w2, a0, a2, k_k, k_a, r_k, ln_g):
    f32 = jnp.float32
    bsz, seq, _ = r.shape
    r, w_lo, k, v, a_lo = (t.astype(f32) for t in (r, w_lo, k, v, a_lo))
    w_log = -jax.nn.softplus(-(w0 + jnp.tanh(w_lo) @ w2)) - 0.5
    decay = jnp.exp(-jnp.exp(w_log))
    a = jax.nn.sigmoid(a0 + a_lo @ a2)
    kk = to_heads(k * k_k)
    kk = kk / jnp.maximum(jnp.linalg.norm(kk, axis=-1, keepdims=True), 1e-12)
    k = k * (1 + (a - 1) * k_a)
    rh, dh, kh, vh, ah = (to_heads(t) for t in (r, decay, k, v, a))

    def step(state, inp):
        r_t, w_t, k_t, v_t, kk_t, a_t = inp
        sa = jnp.einsum("bhvk,bhk->bhv", state, -kk_t)
        state = (state * w_t[:, :, None, :] + sa[..., None] * (kk_t * a_t)[:, :, None, :]
                 + v_t[..., None] * k_t[:, :, None, :])
        return state, jnp.einsum("bhvk,bhk->bhv", state, r_t)

    init = jnp.zeros((bsz, GROUP_HEADS, HEAD_DIM, HEAD_DIM), f32)
    _, y = lax.scan(step, init, tuple(t.swapaxes(0, 1) for t in (rh, dh, kh, vh, kk, ah)))
    y = rms_norm(y.swapaxes(0, 1), ln_g.reshape(GROUP_HEADS, HEAD_DIM))
    y = y + jnp.sum(rh * kh * r_k, axis=-1, keepdims=True) * vh
    return y.reshape(bsz, seq, GROUP_W)

def memory_attention(q, mem_n, w_kv, q_g, k_g):
    bsz, seq, _ = q.shape
    k, v = jnp.split(mem_n @ w_kv, 2, axis=-1)
    q = rms_norm(to_heads(q), q_g)
    k = rms_norm(to_heads(k), k_g)
    v = to_heads(v)
    s = jnp.einsum("bthd,bmhd->bhtm", q, k).astype(jnp.float32) * HEAD_DIM ** -0.5
    p = jax.nn.softmax(s, axis=-1).astype(v.dtype)
    return jnp.einsum("bhtm,bmhd->bthd", p, v).reshape(bsz, seq, GROUP_W)

def hybrid_layer(x, mem, norm_g, w_in, w_out, sgu_norm_g, sgu_w, sgu_b,
                 fox_q_g, fox_k_g, fox_f_b,
                 mlstm_conv_w, mlstm_conv_b, mlstm_i_b, mlstm_f_b, mlstm_out_g,
                 rwkv_mu, rwkv_w0, rwkv_w2, rwkv_a0, rwkv_a2, rwkv_k_k, rwkv_k_a, rwkv_r_k, rwkv_ln_g,
                 mem_norm_g, mem_w_kv, mem_q_g, mem_k_g):
    h = rms_norm(x, norm_g)
    proj = h @ w_in
    pa, pb, pc, pd, pm = split_cols(proj, GROUP_COLS)

    a_u, a_v, a_z = split_cols(pa, A_COLS)
    ya = spatial_gating(a_u, a_v, sgu_norm_g, sgu_w, sgu_b)

    b_q, b_k, b_v, b_f, b_z = split_cols(pb, B_COLS)
    yb = forgetting_attention(b_q, b_k, b_v, b_f + fox_f_b, fox_q_g, fox_k_g)

    c_qk, c_v, c_i, c_f, c_o, c_z = split_cols(pc, C_COLS)
    yc = mlstm(c_qk, c_v, c_i + mlstm_i_b, c_f + mlstm_f_b, c_o, mlstm_conv_w, mlstm_conv_b, mlstm_out_g)

    d_r, d_wlo, d_k, d_v, d_alo, d_z = split_cols(token_shift(pd, rwkv_mu), D_COLS)
    yd = rwkv7_time_mix(d_r, d_wlo, d_k, d_v, d_alo, rwkv_w0, rwkv_w2, rwkv_a0, rwkv_a2,
                        rwkv_k_k, rwkv_k_a, rwkv_r_k, rwkv_ln_g)

    m_q, m_z = split_cols(pm, M_COLS)
    ym = memory_attention(m_q, rms_norm(mem, mem_norm_g), mem_w_kv, mem_q_g, mem_k_g)

    branches = [(ya, a_z), (yb, b_z), (yc, c_z), (yd, d_z), (ym, m_z)]
    mixed = jnp.concatenate([y.astype(x.dtype) * jax.nn.silu(z) for y, z in branches], axis=-1)
    return x + mixed @ w_out

def first_inputs(seed: int = 0) -> dict:
    key = jax.random.key(seed)
    ks = iter(jax.random.split(key, 32))
    f32 = jnp.float32

    def nrm(shape, scale):
        return jax.random.normal(next(ks), shape, f32) * scale

    def uni(shape, lo, hi):
        return jax.random.uniform(next(ks), shape, f32, lo, hi)

    def gain(shape):
        return 1.0 + nrm(shape, 0.1)

    L = DEPTH
    return {
        "x": nrm((BATCH, SEQ, D_MODEL), 1.0),
        "mem": nrm((BATCH, N_MEM, D_MODEL), 1.0),
        "norm_g": gain((L, D_MODEL)),
        "w_in": nrm((L, D_MODEL, IN_COLS), D_MODEL ** -0.5),
        "w_out": nrm((L, MIX_W, D_MODEL), MIX_W ** -0.5),
        "sgu_norm_g": gain((L, GROUP_W)),
        "sgu_w": nrm((L, GROUP_HEADS, CHUNK, CHUNK), 0.5 * CHUNK ** -0.5),
        "sgu_b": gain((L, GROUP_HEADS, CHUNK)),
        "fox_q_g": gain((L, HEAD_DIM)),
        "fox_k_g": gain((L, HEAD_DIM)),
        "fox_f_b": uni((L, GROUP_HEADS), 1.0, 5.0),
        "mlstm_conv_w": nrm((L, CONV_K, 2 * GROUP_W), CONV_K ** -0.5),
        "mlstm_conv_b": nrm((L, 2 * GROUP_W), 0.02),
        "mlstm_i_b": nrm((L, GROUP_HEADS), 0.1),
        "mlstm_f_b": uni((L, GROUP_HEADS), 3.0, 6.0),
        "mlstm_out_g": gain((L, GROUP_W)),
        "rwkv_mu": uni((L, D_W), 0.0, 1.0),
        "rwkv_w0": uni((L, GROUP_W), -4.0, 0.0),
        "rwkv_w2": nrm((L, RWKV_DECAY_RANK, GROUP_W), 0.5 * RWKV_DECAY_RANK ** -0.5),
        "rwkv_a0": nrm((L, GROUP_W), 0.1),
        "rwkv_a2": nrm((L, RWKV_A_RANK, GROUP_W), 0.5 * RWKV_A_RANK ** -0.5),
        "rwkv_k_k": 0.85 + nrm((L, GROUP_W), 0.05),
        "rwkv_k_a": gain((L, GROUP_W)),
        "rwkv_r_k": nrm((L, GROUP_HEADS, HEAD_DIM), 0.1),
        "rwkv_ln_g": gain((L, GROUP_W)),
        "mem_norm_g": gain((L, D_MODEL)),
        "mem_w_kv": nrm((L, D_MODEL, 2 * GROUP_W), D_MODEL ** -0.5),
        "mem_q_g": gain((L, HEAD_DIM)),
        "mem_k_g": gain((L, HEAD_DIM)),
    }

def first_block(x, mem, norm_g, w_in, w_out, sgu_norm_g, sgu_w, sgu_b,
              fox_q_g, fox_k_g, fox_f_b,
              mlstm_conv_w, mlstm_conv_b, mlstm_i_b, mlstm_f_b, mlstm_out_g,
              rwkv_mu, rwkv_w0, rwkv_w2, rwkv_a0, rwkv_a2, rwkv_k_k, rwkv_k_a, rwkv_r_k, rwkv_ln_g,
              mem_norm_g, mem_w_kv, mem_q_g, mem_k_g):
    stacked = (norm_g, w_in, w_out, sgu_norm_g, sgu_w, sgu_b,
               fox_q_g, fox_k_g, fox_f_b,
               mlstm_conv_w, mlstm_conv_b, mlstm_i_b, mlstm_f_b, mlstm_out_g,
               rwkv_mu, rwkv_w0, rwkv_w2, rwkv_a0, rwkv_a2, rwkv_k_k, rwkv_k_a, rwkv_r_k, rwkv_ln_g,
               mem_norm_g, mem_w_kv, mem_q_g, mem_k_g)
    for layer in range(DEPTH):
        x = hybrid_layer(x, mem, *[p[layer] for p in stacked])
    return x


CHUNK_2 = 64
Q_BLOCK = 128

A_HEADS = 4
A_HEAD_DIM = 128
A_WIDTH = A_HEADS * A_HEAD_DIM
A_KV_RANK = 128
IDX_HEADS = 8
IDX_DIM = 64
TOPK_MAX = 256

B_HEADS = 4
B_KEY_DIM = 128
B_VAL_DIM = 128
B_WIDTH = B_HEADS * B_VAL_DIM
B_FORGET = B_HEADS * B_KEY_DIM

D_MIX = A_WIDTH + B_WIDTH

REL_BUCKETS = 32
REL_MAX_DIST = 256

DEEPNORM_ALPHA = (2.0 * DEPTH) ** 0.25
DEEPNORM_BETA = (8.0 * DEPTH) ** -0.25
LN_EPS = 1e-5
RMS_EPS = 1e-6

_SPLITS = (
    ('a_q', A_WIDTH),
    ('a_ckv', A_KV_RANK),
    ('a_iq', IDX_HEADS * IDX_DIM),
    ('a_ik', IDX_DIM),
    ('a_iw', IDX_HEADS),
    ('a_gate', A_WIDTH),
    ('b_q', B_FORGET),
    ('b_f', B_FORGET),
    ('b_i', B_WIDTH),
    ('b_gate', B_WIDTH),
)
D_IN_PROJ = int(sum(n for _, n in _SPLITS))
SPLIT_POINTS = tuple(int(v) for v in np.cumsum([n for _, n in _SPLITS])[:-1])


def _rms_norm(x, g):
    xf = x.astype(jnp.float32)
    y = xf * lax.rsqrt(jnp.mean(xf * xf, axis=-1, keepdims=True) + RMS_EPS)
    return (y * g.astype(jnp.float32)).astype(x.dtype)

def _layer_norm(x, g, b):
    xf = x.astype(jnp.float32)
    mu = jnp.mean(xf, axis=-1, keepdims=True)
    var = jnp.mean(jnp.square(xf - mu), axis=-1, keepdims=True)
    y = (xf - mu) * lax.rsqrt(var + LN_EPS) * g.astype(jnp.float32) + b.astype(jnp.float32)
    return y.astype(x.dtype)

def _t5_bucket(rel):
    nb = REL_BUCKETS // 2
    max_exact = nb // 2
    ret = jnp.where(rel > 0, nb, 0).astype(jnp.int32)
    n = jnp.abs(rel)
    nf = jnp.maximum(n, 1).astype(jnp.float32)
    large = max_exact + (jnp.log(nf / max_exact) / math.log(REL_MAX_DIST / max_exact)
                         * (nb - max_exact)).astype(jnp.int32)
    large = jnp.minimum(large, nb - 1)
    return ret + jnp.where(n < max_exact, n, large)

def _dsa_mixer(q, c, iq, ik, iw, w_uk, rel_bias):
    bsz, seq = q.shape[0], q.shape[1]
    k_sel = min(TOPK_MAX, seq // 4)
    n_blk = seq // Q_BLOCK
    q_lat = jnp.einsum('bshd,hdr->bshr', q, w_uk)
    scale = A_HEAD_DIM ** -0.5
    idx_scale = IDX_DIM ** -0.5
    w_scale = IDX_HEADS ** -0.5
    pos = jnp.arange(seq, dtype=jnp.int32)
    key_chunk = pos // CHUNK_2

    def blockify(t):
        return jnp.moveaxis(t.reshape(bsz, n_blk, Q_BLOCK, *t.shape[2:]), 1, 0)

    xs = (blockify(q_lat), blockify(iq), blockify(iw), pos.reshape(n_blk, Q_BLOCK))

    def one_block(args):
        ql, iqb, iwb, qpos = args
        q_chunk = qpos // CHUNK_2
        admissible = key_chunk[None, :] <= q_chunk[:, None]
        dots = jnp.einsum('bqhd,bsd->bqhs', iqb, ik) * idx_scale
        score = jnp.einsum('bqh,bqhs->bqs', iwb * w_scale, jax.nn.relu(dots))
        score = jnp.where(admissible[None], score.astype(jnp.float32), -jnp.inf)
        _, sel = lax.top_k(score, k_sel)
        valid = (sel // CHUNK_2) <= q_chunk[None, :, None]
        c_sel = jax.vmap(lambda cb, ib: cb[ib])(c, sel)
        bias = rel_bias[_t5_bucket(sel - qpos[None, :, None])]
        logits = (jnp.einsum('bqhr,bqkr->bqhk', ql, c_sel).astype(jnp.float32) * scale
                  + jnp.swapaxes(bias, -1, -2).astype(jnp.float32))
        logits = jnp.where(valid[:, :, None, :], logits, -jnp.inf)
        p = jax.nn.softmax(logits, axis=-1).astype(c.dtype)
        return jnp.einsum('bqhk,bqkr->bqhr', p, c_sel)

    o = lax.map(one_block, xs)
    return jnp.moveaxis(o, 0, 1).reshape(bsz, seq, A_HEADS, A_KV_RANK)

def _hgrn2_mixer(q, f_raw, v, lb):
    bsz, seq = q.shape[0], q.shape[1]
    n_chunk = seq // CHUNK_2
    q = jax.nn.silu(q.astype(jnp.float32))
    lbh = lb.reshape(B_HEADS, B_KEY_DIM).astype(jnp.float32)
    f = lbh + (1.0 - lbh) * jax.nn.sigmoid(f_raw.astype(jnp.float32))
    k = 1.0 - f
    log_f = jnp.log(f)

    def chunkify(t):
        return jnp.transpose(t.reshape(bsz, n_chunk, CHUNK_2, B_HEADS, t.shape[-1]), (1, 0, 3, 2, 4))

    qc, kc, vc = chunkify(q), chunkify(k), chunkify(v.astype(jnp.float32))
    bc = jnp.cumsum(chunkify(log_f), axis=3)
    causal = jnp.tril(jnp.ones((CHUNK_2, CHUNK_2), dtype=bool))

    def step(state, inp):
        qn, kn, vn, bn = inp
        diff = bn[:, :, :, None, :] - bn[:, :, None, :, :]
        decay = jnp.exp(jnp.where(causal[:, :, None], diff, -jnp.inf))
        scores = jnp.einsum('bhtk,bhsk,bhtsk->bhts', qn, kn, decay)
        o = (jnp.einsum('bhts,bhsv->bhtv', scores, vn)
             + jnp.einsum('bhtk,bhkv->bhtv', qn * jnp.exp(bn), state))
        b_last = bn[:, :, -1:, :]
        state = (jnp.exp(b_last[:, :, 0, :])[..., None] * state
                 + jnp.einsum('bhsk,bhsv->bhkv', kn * jnp.exp(b_last - bn), vn))
        return state, o

    s0 = jnp.zeros((bsz, B_HEADS, B_KEY_DIM, B_VAL_DIM), jnp.float32)
    _, o = lax.scan(step, s0, (qc, kc, vc, bc))
    return jnp.transpose(o, (1, 0, 3, 2, 4)).reshape(bsz, seq, B_HEADS, B_VAL_DIM)

def second_inputs(seed: int = 0) -> dict:
    key = jax.random.key(seed)
    ks = jax.random.split(key, 12)
    x = jax.random.normal(ks[0], (BATCH, SEQ, D_MODEL), jnp.float32)
    col_scale = jnp.concatenate([
        jnp.full((n,), DEEPNORM_BETA if name == 'b_i' else 1.0, jnp.float32) for name, n in _SPLITS])
    w_in = jax.random.normal(ks[1], (DEPTH, D_MODEL, D_IN_PROJ), jnp.float32) * (D_MODEL ** -0.5) * col_scale
    w_uk = jax.random.normal(ks[2], (DEPTH, A_HEADS, A_HEAD_DIM, A_KV_RANK), jnp.float32) * (A_HEAD_DIM ** -0.5)
    w_uv = (jax.random.normal(ks[3], (DEPTH, A_HEADS, A_KV_RANK, A_HEAD_DIM), jnp.float32)
            * (A_KV_RANK ** -0.5) * DEEPNORM_BETA)
    kv_norm_g = 1.0 + 0.05 * jax.random.normal(ks[4], (DEPTH, A_KV_RANK), jnp.float32)
    rel_bias = 0.2 * jax.random.normal(ks[5], (REL_BUCKETS, A_HEADS), jnp.float32)
    lb_logits = 0.5 * jax.random.normal(ks[6], (DEPTH + 1, B_FORGET), jnp.float32)
    hgrn_norm_g = 1.0 + 0.05 * jax.random.normal(ks[7], (DEPTH, B_WIDTH), jnp.float32)
    w_o = jax.random.normal(ks[8], (DEPTH, D_MIX, D_MODEL), jnp.float32) * (D_MIX ** -0.5) * DEEPNORM_BETA
    ln_g = 1.0 + 0.05 * jax.random.normal(ks[9], (DEPTH, D_MODEL), jnp.float32)
    ln_b = 0.02 * jax.random.normal(ks[10], (DEPTH, D_MODEL), jnp.float32)
    return {'x': x, 'w_in': w_in, 'w_uk': w_uk, 'w_uv': w_uv, 'kv_norm_g': kv_norm_g,
            'rel_bias': rel_bias, 'lb_logits': lb_logits, 'hgrn_norm_g': hgrn_norm_g,
            'w_o': w_o, 'ln_g': ln_g, 'ln_b': ln_b}

def second_block(x, w_in, w_uk, w_uv, kv_norm_g, rel_bias, lb_logits, hgrn_norm_g, w_o, ln_g, ln_b):
    bsz, seq, _ = x.shape
    lb_all = jnp.cumsum(jax.nn.softmax(lb_logits.astype(jnp.float32), axis=0), axis=0)
    for layer in range(DEPTH):
        h = jnp.einsum('bsd,dc->bsc', x, w_in[layer])
        a_q, a_ckv, a_iq, a_ik, a_iw, a_gate, b_q, b_f, b_i, b_gate = jnp.split(h, SPLIT_POINTS, axis=-1)

        c = _rms_norm(a_ckv, kv_norm_g[layer])
        o_lat = _dsa_mixer(a_q.reshape(bsz, seq, A_HEADS, A_HEAD_DIM), c,
                           a_iq.reshape(bsz, seq, IDX_HEADS, IDX_DIM), a_ik, a_iw,
                           w_uk[layer], rel_bias)
        o_a = jnp.einsum('bshr,hrv->bshv', o_lat, w_uv[layer]).reshape(bsz, seq, A_WIDTH)
        o_a = o_a * jax.nn.silu(a_gate)

        o_b = _hgrn2_mixer(b_q.reshape(bsz, seq, B_HEADS, B_KEY_DIM),
                           b_f.reshape(bsz, seq, B_HEADS, B_KEY_DIM),
                           b_i.reshape(bsz, seq, B_HEADS, B_VAL_DIM), lb_all[layer])
        o_b = _rms_norm(o_b, hgrn_norm_g[layer].reshape(B_HEADS, B_VAL_DIM)).reshape(bsz, seq, B_WIDTH)
        o_b = o_b.astype(x.dtype) * jax.nn.silu(b_gate)

        y = jnp.einsum('bsc,cd->bsd', jnp.concatenate([o_a.astype(x.dtype), o_b], axis=-1), w_o[layer])
        x = _layer_norm(DEEPNORM_ALPHA * x + y, ln_g[layer], ln_b[layer])
    return x


def setup_inputs(seed=0):
    out = dict(first_inputs(seed))
    for name, value in second_inputs(seed + 1).items():
        if name != "x":
            out[name + "_2"] = value
    return out


def reference(
    x, mem, norm_g, w_in, w_out, sgu_norm_g, sgu_w, sgu_b, fox_q_g, fox_k_g, fox_f_b,
    mlstm_conv_w, mlstm_conv_b, mlstm_i_b, mlstm_f_b, mlstm_out_g, rwkv_mu, rwkv_w0, rwkv_w2,
    rwkv_a0, rwkv_a2, rwkv_k_k, rwkv_k_a, rwkv_r_k, rwkv_ln_g, mem_norm_g, mem_w_kv, mem_q_g,
    mem_k_g, w_in_2, w_uk_2, w_uv_2, kv_norm_g_2, rel_bias_2, lb_logits_2, hgrn_norm_g_2, w_o_2,
    ln_g_2, ln_b_2,
):
    x = first_block(
        x, mem, norm_g, w_in, w_out, sgu_norm_g, sgu_w, sgu_b, fox_q_g, fox_k_g, fox_f_b,
        mlstm_conv_w, mlstm_conv_b, mlstm_i_b, mlstm_f_b, mlstm_out_g, rwkv_mu, rwkv_w0,
        rwkv_w2, rwkv_a0, rwkv_a2, rwkv_k_k, rwkv_k_a, rwkv_r_k, rwkv_ln_g, mem_norm_g,
        mem_w_kv, mem_q_g, mem_k_g,
    )
    return second_block(
        x, w_in_2, w_uk_2, w_uv_2, kv_norm_g_2, rel_bias_2, lb_logits_2, hgrn_norm_g_2, w_o_2,
        ln_g_2, ln_b_2,
    )


_drawn_inputs = setup_inputs


def setup_inputs(seed=0):
    import zlib

    import numpy as np

    out = dict(_drawn_inputs(seed))
    spreads = {}
    factors = {'sgu_norm_g': 8.0,
     'sgu_b': 3.395,
     'fox_q_g': 8.0,
     'fox_k_g': 7.457,
     'mlstm_conv_b': 8.0,
     'mlstm_i_b': 200.0,
     'rwkv_w2': 6.671,
     'rwkv_a0': 6.269,
     'rwkv_k_k': 8.0,
     'rwkv_k_a': 2.684,
     'mem_norm_g': 8.0,
     'mem_q_g': 8.0,
     'mem_k_g': 8.0,
     'w_uk_2': 3.327,
     'w_uv_2': 2.875,
     'kv_norm_g_2': 8.0,
     'rel_bias_2': 8.0,
     'lb_logits_2': 4.684,
     'hgrn_norm_g_2': 17.855,
     'ln_b_2': 2.87}
    for name, (base, spread) in spreads.items():
        noise = np.random.default_rng([zlib.crc32(name.encode()), seed]).standard_normal(out[name].shape)
        drawn = base * np.exp(spread * noise) if base else spread * noise
        out[name] = jnp.asarray(drawn.astype(out[name].dtype))
    for name, factor in factors.items():
        out[name] = (out[name] * factor).astype(out[name].dtype)
    return out
```

```python
from contextlib import ExitStack, contextmanager

import numpy as np

import concourse.bass as bass
from concourse import mybir

F32 = mybir.dt.float32
U32 = mybir.dt.uint32
ALU = mybir.AluOpType
ACT = mybir.ActivationFunctionType
AX = mybir.AxisListType

P = 128
SEQ = 2048
TILES = SEQ // P
D_MODEL = 1024
KD = D_MODEL // P
HEADS = 4
HD = 64
GW = HEADS * HD
N_MEM = 256
RANK = 16
MIX1 = 5 * GW
EPS = 1e-6
LN_EPS = 1e-5
NEG = -1e30

A_U, A_V, A_Z = 0, 256, 512
B_Q, B_K, B_V, B_F, B_Z = 768, 1024, 1280, 1536, 1540
C_QK, C_V, C_I, C_F, C_O, C_Z = 1796, 2308, 2564, 2568, 2572, 2828
D_0 = 3084
D_R, D_WLO, D_K, D_V, D_ALO, D_Z = 0, 256, 272, 528, 784, 800
D_W = 1056
M_Q, M_Z = 4140, 4396
COLS1 = 4652
E_Q, E_C, E_IQ, E_IK, E_IW, E_G = 0, 512, 640, 1152, 1216, 1224
H_Q, H_F, H_I, H_G = 1736, 2248, 2760, 3272
COLS2 = 3784
IDX_HEADS = 8
IDX_DIM = 64
TOPK = 256
BH = 4
BD = 128
PAD = 4
GROUP = 512
LEVELS = 7
BUCKETS = 32
TAB = 2560
SKEW = 2432


def shape_constants():
    p = np.arange(P)[:, None]
    f = np.arange(P)[None, :]
    cols = [p == f, p <= f, p < f, p > f]
    for l in range(LEVELS):
        half = 1 << l
        cols.append((p // (2 * half) == f // (2 * half)) & (p // half % 2 == 0) & (f // half % 2 == 1))
    cols.append(np.ones((P, P)))
    cols += [(p == h) & (f >= 0) for h in range(HEADS)]
    cols += [p == 2 * j + f // HD for j in range(2)]
    cols += [(p <= f) * 1.0 - (p < P // 2), (p < f) * 1.0 - (p < P // 2)]
    cols += [cols[4 + l].T for l in range(LEVELS)]
    cols += [p + f == P - 1]
    x = np.arange(GROUP + 3 * P)[None, :] - 3 * P
    cols += [(x > p) * NEG, (x > p // 64 * 64 + 63) * NEG]
    return np.concatenate([c.astype(np.float32) for c in cols], axis=1)


IDENT, UPTO, BEFORE, AFTER = (slice(P * k, P * k + P) for k in range(4))
LEVEL = [slice(P * (4 + l), P * (5 + l)) for l in range(LEVELS)]
ONES = slice(P * 11, P * 12)
ROW = [slice(P * (12 + h), P * (13 + h)) for h in range(HEADS)]
PAIR = [slice(P * (16 + j), P * (17 + j)) for j in range(2)]
CENTRED, CENTRED_BEFORE = (slice(P * k, P * k + P) for k in (18, 19))
LEVEL_T = [slice(P * (20 + l), P * (21 + l)) for l in range(LEVELS)]
FLIP = slice(P * 27, P * 28)
WIN = GROUP + 3 * P
CAUSAL0 = P * 28
CHUNKED0 = P * 28 + WIN
CONST_COLS = P * 28 + 2 * WIN


def bucket_table():
    rel = np.arange(TAB) - (SEQ - 1)
    nb, max_dist = BUCKETS // 2, 256
    exact = nb // 2
    n = np.abs(rel)
    nf = np.maximum(n, 1).astype(np.float32)
    large = exact + (np.log(nf / np.float32(exact)) / np.float32(np.log(max_dist / exact))
                     * np.float32(nb - exact)).astype(np.int32)
    bucket = np.where(rel > 0, nb, 0) + np.where(n < exact, n, np.minimum(large, nb - 1))
    return (np.arange(BUCKETS)[:, None] == bucket[None, :]).astype(np.float32)


@contextmanager
def step(nc, names):
    with ExitStack() as ctx:
        sems = {n: ctx.enter_context(nc.semaphore(n)) for n in names.split()}
        with nc.Block() as block:
            yield block, type("Signals", (), sems)
        for sem in sems.values():
            nc.sync.sem_clear(sem)
        nc.all_engine_barrier()


class Buffers:

    def __init__(self, nc, ctx, phase):
        self._nc, self._ctx, self._phase = nc, ctx, phase

    def sb(self, name, shape, dt=F32):
        t = self._ctx.enter_context(self._nc.sbuf_tensor(f"{self._phase}_{name}", shape, dt))
        return t

    def ps(self, name, shape):
        t = self._ctx.enter_context(self._nc.psum_tensor(f"{self._phase}_{name}", shape, F32))
        return t


def spread(ap, axis, n):
    shape = list(ap.shape)
    v = ap.unsqueeze(axis)
    shape.insert(axis, n)
    return v.broadcast_to(shape)


def row(ap, n=P):
    return ap.partition_broadcast(n)


def load(nc, name, pairs):
    with step(nc, "arrived") as (block, s):
        arrived = s.arrived

        @block.sync
        def _(sp):
            for dst, src in pairs:
                sp.dma_start(dst, src, allow_slow_non_contiguous=True).then_inc(arrived, 16)
            sp.wait_ge(arrived, 16 * len(pairs))


def gemm(nc, c, hT, w, out, cols, name, pad):
    w_v = w.rearrange("(k p) n -> p k n", p=P)
    with ExitStack() as ctx:
        B = Buffers(nc, ctx, name)
        wt = B.sb("w", [P, 2, KD, 512])
        stage = B.sb("stage", [P, 4, 512])
        acc = B.ps("acc", [P, 4, 512])

        def group(n0s, width):
            with step(nc, "w_in0 w_in1 product act_copied dve_copied stored0 stored1 stored2 stored3") as (block, s):
                mm, act_cp, dve_cp = s.product, s.act_copied, s.dve_copied
                w_in = (s.w_in0, s.w_in1)
                stored = (s.stored0, s.stored1, s.stored2, s.stored3)

                @block.sync
                def _(sp):
                    for j, n0 in enumerate(n0s):
                        for k in range(KD):
                            sp.dma_start(wt[:, j, k, 0:width], w_v[:, k, bass.ds(n0, width)]).then_inc(w_in[j], 16)
                    for j, n0 in enumerate(n0s):
                        for t in range(TILES):
                            m = j * TILES + t
                            sp.wait_ge(dve_cp if m % 2 else act_cp, m // 2 + 1)
                            sp.dma_start(out[pad + t * P:pad + (t + 1) * P, bass.ds(n0, width)],
                                         stage[:, m % 4, 0:width]).then_inc(stored[m % 4], 16)
                    for slot in range(4):
                        sp.wait_ge(stored[slot], 16 * TILES * len(n0s) // 4)

                @block.tensor
                def _(pe):
                    for j in range(len(n0s)):
                        for t in range(TILES):
                            m = j * TILES + t
                            if m >= 4:
                                pe.wait_ge(dve_cp if m % 2 else act_cp, (m - 4) // 2 + 1)
                            if t == 0:
                                pe.wait_ge(w_in[j], 16 * KD)
                            for k in range(KD):
                                mm_ = pe.matmul(acc[:, m % 4, 0:width], hT[:, k, t * P:(t + 1) * P],
                                                wt[:, j, k, 0:width], start=(k == 0), stop=(k == KD - 1))
                            mm_.then_inc(mm, 1)

                def copies(eng, op, parity, done):
                    for m in range(parity, TILES * len(n0s), 2):
                        eng.wait_ge(mm, m + 1)
                        if m >= 4:
                            eng.wait_ge(stored[m % 4], 16 * (m // 4))
                        op(stage[:, m % 4, 0:width], acc[:, m % 4, 0:width]).then_inc(done, 1)

                @block.scalar
                def _(act):
                    copies(act, lambda o, i: act.activation(o, i, ACT.Copy), 0, act_cp)

                @block.vector
                def _(dve):
                    copies(dve, dve.tensor_copy, 1, dve_cp)

        pairs = cols // 1024
        with nc.Fori(0, pairs) as g:
            group([g * 1024, g * 1024 + 512], 512)
        n = pairs * 1024
        while n < cols:
            group([n], min(512, cols - n))
            n += 512


def norm_transpose(nc, c, x, gain, hT, name, tiles=TILES):
    U = min(4, tiles)
    with ExitStack() as ctx:
        B = Buffers(nc, ctx, name)
        xt = B.sb("xt", [P, U, D_MODEL])
        sq = B.sb("sq", [P, U, D_MODEL])
        ss = B.sb("ss", [P, U])
        g = B.sb("g", [P, KD])
        tp = B.ps("tp", [P, 4, KD // 2, P])
        load(nc, f"{name}_g", [(g[:], gain.rearrange("(k p) -> p k", p=P))])
        with nc.Fori(0, tiles // U) as i:
            with step(nc, "x_in rs normed turned copied") as (block, s):
                x_in, rs, xn, tr, cp = s.x_in, s.rs, s.normed, s.turned, s.copied

                @block.sync
                def _(sp):
                    for u in range(U):
                        sp.dma_start(xt[:, u], x[bass.ds(i * (U * P) + u * P, P), :]).then_inc(x_in, 16)

                @block.scalar
                def _(act):
                    act.wait_ge(x_in, 16 * U)
                    for u in range(U):
                        act.activation(sq[:, u], xt[:, u], ACT.Square, accum_out=ss[:, u:u + 1])
                    act.drain()
                    act.activation(ss[:], ss[:], ACT.Ln, scale=1.0 / D_MODEL, bias=c.eps[:, 0:1])
                    act.drain()
                    act.activation(ss[:], ss[:], ACT.Exp, scale=-0.5).then_inc(rs, 1)

                @block.vector
                def _(dve):
                    dve.wait_ge(rs, 1)
                    for u in range(U):
                        dve.tensor_scalar(xt[:, u], xt[:, u], ss[:, u:u + 1], None, ALU.mult).then_inc(xn, 1)
                    for v in range(2 * U):
                        u, half = v // 2, v % 2
                        dve.wait_ge(tr, v + 1)
                        dve.tensor_tensor(hT[:, 4 * half:4 * half + 4, bass.ds(i * (U * P) + u * P, P)],
                                          tp[:, v % 4], spread(g[:, 4 * half:4 * half + 4], 2, P),
                                          ALU.mult).then_inc(cp, 1)

                @block.tensor
                def _(pe):
                    for v in range(2 * U):
                        u, half = v // 2, v % 2
                        pe.wait_ge(xn, u + 1)
                        if v >= 4:
                            pe.wait_ge(cp, v - 3)
                        for k in range(4):
                            kk = 4 * half + k
                            t = pe.transpose(tp[:, v % 4, k], xt[:, u, kk * P:(kk + 1) * P], c.ident)
                        t.then_inc(tr, 1)


class Constants:
    pass


def load_constants(nc, ctx, consts):
    c = Constants()
    t = ctx.enter_context(nc.sbuf_tensor("consts_sb", [P, CONST_COLS], F32))
    e = ctx.enter_context(nc.sbuf_tensor("eps_sb", [P, 2], F32))
    c.all, c.eps = t, e
    c.ident, c.upto, c.before, c.after, c.ones = (t[:, k] for k in (IDENT, UPTO, BEFORE, AFTER, ONES))
    with step(nc, "const_in eps_set") as (block, s):

        @block.sync
        def _(sp):
            sp.dma_start(t[:], consts).then_inc(s.const_in, 16)
            sp.wait_ge(s.const_in, 16)

        @block.vector
        def _(dve):
            dve.memset(e[:, 0:1], EPS).then_inc(s.eps_set, 1)
            dve.memset(e[:, 1:2], LN_EPS).then_inc(s.eps_set, 1)
            dve.wait_ge(s.eps_set, 2)
    return c


def tokens(ap, i, n, c0, c1, pad=0):
    return ap[bass.ds(i * P + pad, n * P), c0:c1].rearrange("(u p) c -> p u c", p=P)


def rstd(act, c, ss, width):
    act.drain()
    act.activation(ss, ss, ACT.Ln, scale=1.0 / width, bias=c.eps[:, 0:1])
    act.drain()
    return act.activation(ss, ss, ACT.Exp, scale=-0.5)


def sgu(nc, c, w, proj, mixed):
    U = 4
    with ExitStack() as ctx:
        B = Buffers(nc, ctx, "sgu")
        wt = B.sb("wt", [P, HEADS, P])
        wT = B.sb("wT", [P, HEADS, P])
        b = B.sb("b", [P, HEADS])
        g = B.sb("g", [P, GW])
        x = B.sb("x", [P, U, 3 * GW])
        sq = B.sb("sq", [P, U, GW])
        ss = B.sb("ss", [P, U * HEADS])
        tp = B.ps("tp", [P, HEADS, P])
        mx = B.ps("mx", [P, HEADS, U * HD])
        load(nc, "sgu_w", [(wt[:], w['sgu_w'].rearrange("g t s -> t g s")),
                           (b[:], w['sgu_b'].rearrange("g t -> t g")), (g[:], row(w['sgu_norm_g']))])
        with step(nc, "turned masked") as (block, s):

            @block.tensor
            def _(pe):
                for h in range(HEADS):
                    t = pe.transpose(tp[:, h], wt[:, h], c.ident)
                t.then_inc(s.turned, 1)

            @block.vector
            def _(dve):
                dve.wait_ge(s.turned, 1)
                dve.tensor_tensor(wT[:], tp[:], spread(c.upto, 1, HEADS), ALU.mult).then_inc(s.masked, 1)

        with nc.Fori(0, TILES // U) as i:
            with step(nc, "x_in gelus squares rs normed mixes y_done silus stored") as (block, s):

                @block.sync
                def _(sp):
                    sp.dma_start(x[:], tokens(proj, i * U, U, A_U, A_U + 3 * GW, PAD)).then_inc(s.x_in, 16)
                    sp.wait_ge(s.y_done, 1)
                    sp.dma_start(tokens(mixed, i * U, U, 0, GW), x[:, :, 0:GW]).then_inc(s.stored, 16)
                    sp.wait_ge(s.stored, 16)

                @block.scalar
                def _(act):
                    act.wait_ge(s.x_in, 16)
                    act.activation(x[:, :, 0:2 * GW], x[:, :, 0:2 * GW], ACT.Gelu_apprx_tanh).then_inc(s.gelus, 1)
                    act.activation(x[:, :, 2 * GW:], x[:, :, 2 * GW:], ACT.Silu).then_inc(s.silus, 1)
                    act.wait_ge(s.squares, 1)
                    rstd(act, c, ss[:], HD).then_inc(s.rs, 1)

                @block.vector
                def _(dve):
                    u, v, z = (x[:, :, k * GW:(k + 1) * GW] for k in range(3))
                    vh = v.rearrange("p u (h d) -> p u h d", h=HEADS)
                    dve.wait_ge(s.gelus, 1)
                    dve.tensor_tensor(sq[:], v, v, ALU.mult)
                    dve.drain()
                    dve.tensor_reduce(ss[:], sq[:].rearrange("p u (h d) -> p (u h) d", h=HEADS), AX.X,
                                      ALU.add).then_inc(s.squares, 1)
                    dve.tensor_tensor(v, v, spread(g[:], 1, U), ALU.mult)
                    dve.wait_ge(s.rs, 1)
                    dve.drain()
                    dve.tensor_tensor(vh, vh, spread(ss[:].rearrange("p (u h) -> p u h", u=U), 3, HD),
                                      ALU.mult).then_inc(s.normed, 1)
                    dve.wait_ge(s.mixes, 1)
                    for h in range(HEADS):
                        cols = slice(h * HD, (h + 1) * HD)
                        dve.scalar_tensor_tensor(out=u[:, :, cols],
                                                 in0=mx[:, h].rearrange("p (u d) -> p u d", u=U),
                                                 scalar=b[:, h:h + 1], in1=u[:, :, cols], op0=ALU.add, op1=ALU.mult)
                    dve.wait_ge(s.silus, 1)
                    dve.drain()
                    dve.tensor_tensor(u, u, z, ALU.mult).then_inc(s.y_done, 1)

                @block.tensor
                def _(pe):
                    v = x[:, :, GW:2 * GW].rearrange("p u (h d) -> p h u d", h=HEADS)
                    pe.wait_ge(s.normed, 1)
                    for h in range(HEADS):
                        m = pe.matmul(mx[:, h].rearrange("p (u d) -> p u d", u=U), wT[:, h], v[:, h],
                                      start=True, stop=True)
                    m.then_inc(s.mixes, 1)


def memory_attention(nc, c, w, proj, mixed):
    MT = N_MEM // P
    with ExitStack() as ctx:
        B = Buffers(nc, ctx, "mem")
        kT = B.sb("kT", [HD, HEADS, N_MEM])
        vm = B.sb("vm", [P, MT, GW])
        gq = B.sb("gq", [P, HD])
        gk = B.sb("gk", [P, HD])
        load(nc, "mem_g", [(gq[:], row(w['mem_q_g'])), (gk[:], row(w['mem_k_g']))])
        with ExitStack() as early:
            E = Buffers(nc, early, "memkv")
            hT = E.sb("hT", [P, KD, N_MEM])
            norm_transpose(nc, c, w['mem'], w['mem_norm_g'], hT, "nm", tiles=MT)
            wk = E.sb("wk", [P, KD, 2 * GW])
            k = E.sb("k", [P, MT, HEADS, HD])
            sq = E.sb("sq", [P, MT, HEADS, HD])
            ss = E.sb("ss", [P, MT, HEADS])
            acc = E.ps("acc", [P, MT, 2 * GW])
            tp = E.ps("tp", [P, HEADS, N_MEM])
            with step(nc, "w_in prods split squares rs normed turned kept") as (block, s):

                @block.sync
                def _(sp):
                    sp.dma_start(wk[:], w['mem_w_kv'].rearrange("(k p) n -> p k n", p=P)).then_inc(s.w_in, 16)

                @block.tensor
                def _(pe):
                    pe.wait_ge(s.w_in, 16)
                    for t in range(MT):
                        for j in range(KD):
                            m = pe.matmul(acc[:, t], hT[:, j, t * P:(t + 1) * P], wk[:, j], start=(j == 0),
                                          stop=(j == KD - 1))
                    m.then_inc(s.prods, 1)
                    pe.wait_ge(s.normed, 1)
                    for t in range(MT):
                        for h in range(HEADS):
                            m = pe.transpose(tp[0:HD, h, t * P:(t + 1) * P], k[:, t, h], c.ident)
                    m.then_inc(s.turned, 1)

                @block.scalar
                def _(act):
                    act.wait_ge(s.squares, 1)
                    rstd(act, c, ss[:], HD).then_inc(s.rs, 1)

                @block.vector
                def _(dve):
                    dve.wait_ge(s.prods, 1)
                    dve.tensor_copy(k[:], acc[:, :, 0:GW].rearrange("p t (h d) -> p t h d", h=HEADS))
                    dve.tensor_copy(vm[:], acc[:, :, GW:2 * GW])
                    dve.drain()
                    dve.tensor_tensor(sq[:], k[:], k[:], ALU.mult)
                    dve.drain()
                    dve.tensor_reduce(ss[:], sq[:], AX.X, ALU.add).then_inc(s.squares, 1)
                    dve.wait_ge(s.rs, 1)
                    dve.tensor_tensor(k[:], k[:], spread(ss[:], 3, HD), ALU.mult)
                    dve.drain()
                    kk = k[:].rearrange("p t h d -> p (t h) d")
                    dve.tensor_tensor(kk, kk, spread(gk[:], 1, MT * HEADS), ALU.mult).then_inc(s.normed, 1)
                    dve.wait_ge(s.turned, 1)
                    dve.tensor_copy(kT[:], tp[0:HD]).then_inc(s.kept, 1)

        U = 2
        qz = B.sb("qz", [P, U, 2 * GW])
        sq = B.sb("sqq", [P, U, GW])
        ss = B.sb("ss", [P, U * HEADS])
        qT = B.sb("qT", [HD, U, HEADS, P])
        pr = B.sb("pr", [P, HEADS, N_MEM])
        mx = B.sb("mx", [P, U, HEADS])
        den = B.sb("den", [P, U, HEADS])
        pT = B.sb("pT", [P, HEADS, MT, P])
        tq = B.ps("tq", [P, HEADS, P])
        sc = B.ps("sc", [P, HEADS, N_MEM])
        tp = B.ps("tp", [P, HEADS, MT, P])
        o = B.ps("o", [P, HEADS, HD])
        with nc.Fori(0, TILES // U) as i:
            with step(nc, "x_in squares rs normed q_turned q_kept scored maxed exps turned kept weighed "
                          "divided silus y_done stored") as (block, s):

                @block.sync
                def _(sp):
                    sp.dma_start(qz[:], tokens(proj, i * U, U, M_Q, M_Q + 2 * GW, PAD)).then_inc(s.x_in, 16)
                    sp.wait_ge(s.y_done, 1)
                    sp.dma_start(tokens(mixed, i * U, U, 4 * GW, 5 * GW), qz[:, :, 0:GW]).then_inc(s.stored, 16)
                    sp.wait_ge(s.stored, 16)

                @block.scalar
                def _(act):
                    act.wait_ge(s.x_in, 16)
                    act.activation(qz[:, :, GW:], qz[:, :, GW:], ACT.Silu).then_inc(s.silus, 1)
                    act.wait_ge(s.squares, 1)
                    rstd(act, c, ss[:], HD).then_inc(s.rs, 1)
                    for u in range(U):
                        act.wait_ge(s.maxed, u + 1)
                        if u:
                            act.wait_ge(s.turned, u)
                        for h in range(HEADS):
                            act.activation(pr[:, h], sc[:, h], ACT.Exp, bias=mx[:, u, h:h + 1],
                                           accum_out=den[:, u, h:h + 1]).then_inc(s.exps, 1)

                @block.vector
                def _(dve):
                    q, z = qz[:, :, 0:GW], qz[:, :, GW:]
                    q64 = q.rearrange("p u (h d) -> p u h d", h=HEADS)
                    dve.wait_ge(s.x_in, 16)
                    dve.tensor_tensor(sq[:], q, q, ALU.mult)
                    dve.drain()
                    dve.tensor_reduce(ss[:], sq[:].rearrange("p u (h d) -> p (u h) d", h=HEADS), AX.X,
                                      ALU.add).then_inc(s.squares, 1)
                    dve.wait_ge(s.rs, 1)
                    dve.tensor_tensor(q64, q64, spread(ss[:].rearrange("p (u h) -> p u h", u=U), 3, HD), ALU.mult)
                    dve.drain()
                    for u in range(U):
                        dve.scalar_tensor_tensor(out=q64[:, u], in0=q64[:, u], scalar=HD ** -0.5,
                                                 in1=spread(gq[:], 1, HEADS), op0=ALU.mult,
                                                 op1=ALU.mult).then_inc(s.normed, 1)
                    for u in range(U):
                        dve.wait_ge(s.q_turned, u + 1)
                        dve.tensor_copy(qT[:, u], tq[0:HD]).then_inc(s.q_kept, 1)
                        dve.wait_ge(s.scored, u + 1)
                        dve.tensor_reduce(mx[:, u], sc[:], AX.X, ALU.max)
                        dve.drain()
                        dve.tensor_scalar(mx[:, u], mx[:, u], -1.0, None, ALU.mult).then_inc(s.maxed, 1)
                        dve.wait_ge(s.turned, u + 1)
                        dve.tensor_copy(pT[:], tp[:]).then_inc(s.kept, 1)
                        dve.reciprocal(den[:, u], den[:, u])
                        dve.wait_ge(s.weighed, u + 1)
                        if u == 0:
                            dve.wait_ge(s.silus, 1)
                        dve.drain()
                        dve.tensor_tensor(q64[:, u], o[:], spread(den[:, u], 2, HD), ALU.mult).then_inc(s.divided, 1)
                        dve.drain()
                        d = dve.tensor_tensor(q[:, u], q[:, u], z[:, u], ALU.mult)
                    d.then_inc(s.y_done, 1)

                @block.tensor
                def _(pe):
                    q = qz[:, :, 0:GW].rearrange("p u (h d) -> p u h d", h=HEADS)
                    for u in range(U):
                        pe.wait_ge(s.normed, U)
                        for h in range(HEADS):
                            m = pe.transpose(tq[0:HD, h], q[:, u, h], c.ident)
                        m.then_inc(s.q_turned, 1)
                        pe.wait_ge(s.q_kept, u + 1)
                        for h in range(HEADS):
                            m = pe.matmul(sc[:, h], qT[:, u, h], kT[:, h], start=True, stop=True)
                        m.then_inc(s.scored, 1)
                        pe.wait_ge(s.exps, HEADS * (u + 1))
                        for h in range(HEADS):
                            for t in range(MT):
                                m = pe.transpose(tp[:, h, t], pr[:, h, t * P:(t + 1) * P], c.ident)
                        m.then_inc(s.turned, 1)
                        pe.wait_ge(s.kept, u + 1)
                        if u:
                            pe.wait_ge(s.divided, u)
                        for h in range(HEADS):
                            for t in range(MT):
                                m = pe.matmul(o[:, h], pT[:, h, t], vm[:, t, h * HD:(h + 1) * HD],
                                              start=(t == 0), stop=(t == MT - 1))
                        m.then_inc(s.weighed, 1)


def zero_rows(nc, buf, proj):
    with step(nc, "zeroed stored") as (block, s):

        @block.vector
        def _(dve):
            dve.memset(buf[0:PAD, 0:3, :], 0.0).then_inc(s.zeroed, 1)

        @block.sync
        def _(sp):
            sp.wait_ge(s.zeroed, 1)
            for n0 in range(0, COLS1, SEQ):
                n = min(SEQ, COLS1 - n0)
                sp.dma_start(proj[0:PAD, n0:n0 + n], buf[0:PAD, n0 // SEQ, 0:n]).then_inc(s.stored, 16)
            sp.wait_ge(s.stored, 16 * 3)


def fox(nc, c, w, proj, mixed):
    A = HD + 1
    with ExitStack() as ctx:
        B = Buffers(nc, ctx, "fox")
        qT = B.sb("qT", [A, HEADS, SEQ])
        kT = B.sb("kT", [A, HEADS, SEQ])
        v = B.sb("v", [P, TILES, GW])
        gq = B.sb("gq", [P, 2, HD])
        fb = B.sb("fb", [P, HEADS])
        carry = B.sb("carry", [1, HEADS])
        load(nc, "fox_g", [(gq[:, 0], row(w['fox_q_g'])), (gq[:, 1], row(w['fox_k_g'])), (fb[:], row(w['fox_f_b'])),
                           (v[:], proj[PAD:, B_V:B_V + GW].rearrange("(t p) c -> p t c", p=P))])
        with step(nc, "scaled cleared") as (block, s):

            @block.vector
            def _(dve):
                dve.tensor_scalar(gq[:, 0], gq[:, 0], HD ** -0.5, None, ALU.mult).then_inc(s.scaled, 1)
                dve.memset(carry[:], 0.0).then_inc(s.cleared, 1)

        with ExitStack() as early:
            E = Buffers(nc, early, "foxq")
            U = 2
            x = E.sb("x", [P, U, 2, HEADS, HD])
            f = E.sb("f", [P, U, HEADS])
            aug = E.sb("aug", [P, U, 2, HEADS, A])
            sq = E.sb("sq", [P, U, 2 * GW])
            ss = E.sb("ss", [P, U, 2, HEADS])
            cum = E.ps("cum", [P, U, HEADS])
            tot = E.ps("tot", [1, U, HEADS])
            tp = E.ps("tp", [P, 2, HEADS, P])
            with nc.Fori(0, TILES // U) as i:
                with step(nc, "x_in f_in squares rs logf sums carried aug_done turned q_kept k_kept biased") as (block, s):

                    @block.sync
                    def _(sp):
                        sp.dma_start(x[:].rearrange("p u a h d -> p u (a h d)"),
                                     tokens(proj, i * U, U, B_Q, B_Q + 2 * GW, PAD)).then_inc(s.x_in, 16)
                        sp.dma_start(f[:], tokens(proj, i * U, U, B_F, B_F + HEADS, PAD)).then_inc(s.f_in, 16)

                    @block.scalar
                    def _(act):
                        act.wait_ge(s.biased, 1)
                        act.activation(f[:], f[:], ACT.Exp, scale=-1.0)
                        act.drain()
                        act.activation(f[:], f[:], ACT.Ln, bias=c.ones[:, 0:1]).then_inc(s.logf, 1)
                        act.wait_ge(s.squares, 1)
                        rstd(act, c, ss[:], HD).then_inc(s.rs, 1)
                        for u in range(U):
                            act.wait_ge(s.turned, u + 1)
                            act.activation(qT[:, :, bass.ds((i * U + u) * P, P)], tp[0:A, 0],
                                           ACT.Copy).then_inc(s.q_kept, 1)

                    @block.vector
                    def _(dve):
                        dve.wait_ge(s.f_in, 16)
                        dve.tensor_tensor(f[:], f[:], spread(fb[:], 1, U), ALU.add).then_inc(s.biased, 1)
                        dve.wait_ge(s.x_in, 16)
                        x2 = x[:].rearrange("p u a h d -> p u (a h d)")
                        dve.tensor_tensor(sq[:], x2, x2, ALU.mult)
                        dve.memset(aug[:, :, 0, :, HD:A], 1.0)
                        dve.drain()
                        dve.tensor_reduce(ss[:].rearrange("p u a h -> p (u a h)"),
                                          sq[:].rearrange("p u (x d) -> p (u x) d", d=HD), AX.X,
                                          ALU.add).then_inc(s.squares, 1)
                        for u in range(U):
                            for a in range(2):
                                dve.tensor_tensor(x[:, u, a], x[:, u, a], spread(gq[:, a], 1, HEADS), ALU.mult)
                        for u in range(U):
                            dve.wait_ge(s.sums, u + 1)
                            dve.tensor_copy(aug[:, u, 1, :, HD:A].rearrange("p h o -> p (h o)"), cum[:, u])
                            dve.tensor_tensor(carry[:], carry[:], tot[:, u], ALU.add)
                            dve.drain().then_inc(s.carried, 1)
                        dve.wait_ge(s.rs, 1)
                        dve.drain()
                        for u in range(U):
                            for a in range(2):
                                dve.tensor_tensor(aug[:, u, a, :, 0:HD], x[:, u, a], spread(ss[:, u, a], 2, HD),
                                                  ALU.mult)
                        dve.drain().then_inc(s.aug_done, 1)
                        for u in range(U):
                            dve.wait_ge(s.turned, u + 1)
                            dve.tensor_copy(kT[:, :, bass.ds((i * U + u) * P, P)], tp[0:A, 1]).then_inc(s.k_kept, 1)

                    @block.tensor
                    def _(pe):
                        pe.wait_ge(s.logf, 1)
                        for u in range(U):
                            if u:
                                pe.wait_ge(s.carried, u)
                            pe.matmul(cum[:, u], c.upto, f[:, u], start=True, stop=False)
                            pe.matmul(cum[:, u], c.ones[0:1], carry[:], start=False, stop=True)
                            pe.matmul(tot[:, u], c.ones[:, 0:1], f[:, u], start=True, stop=True).then_inc(s.sums, 1)
                        pe.wait_ge(s.aug_done, 1)
                        for u in range(U):
                            if u:
                                pe.wait_ge(s.q_kept, u)
                                pe.wait_ge(s.k_kept, u)
                            for a in range(2):
                                for h in range(HEADS):
                                    m = pe.transpose(tp[0:A, a, h], aug[:, u, a, h], c.ident)
                            m.then_inc(s.turned, 1)

        z = B.sb("z", [P, GW])
        qb = B.sb("qb", [A, HEADS, P])
        pr = B.sb("pr", [P, 2, SEQ])
        mx = B.sb("mx", [P, HEADS])
        m2 = B.sb("m2", [P, HEADS, 4])
        den = B.sb("den", [P, HEADS])
        pT = B.sb("pT", [P, 2, 4, P])
        y = B.sb("y", [P, HEADS, HD])
        sc = B.ps("sc", [P, 4, GROUP])
        tp = B.ps("tp2", [P, 2, 4, P])
        o = B.ps("o", [P, HEADS, HD])
        for g in range(TILES // 4):
            W = (g + 1) * GROUP
            NG = g + 1
            with nc.Fori(0, 4) as j:
                with step(nc, "z_in q_here silus scored maxed exps turned kept_v weighed y_done stored") \
                        as (block, s):

                    @block.sync
                    def _(sp):
                        sp.dma_start(z[:], proj[bass.ds(j * P + (4 * g * P + PAD), P), B_Z:B_Z + GW]).then_inc(s.z_in, 16)
                        sp.wait_ge(s.y_done, 1)
                        sp.dma_start(mixed[bass.ds(j * P + 4 * g * P, P), GW:2 * GW],
                                     y[:].rearrange("p h d -> p (h d)")).then_inc(s.stored, 16)
                        sp.wait_ge(s.stored, 16)

                    @block.gpsimd
                    def _(pool):
                        pool.tensor_copy(qb[:], qT[:, :, bass.ds(j * P + 4 * g * P, P)]).then_inc(s.q_here, 1)

                    @block.scalar
                    def _(act):
                        act.wait_ge(s.z_in, 16)
                        act.activation(z[:], z[:], ACT.Silu).then_inc(s.silus, 1)

                        for h in range(HEADS):
                            act.wait_ge(s.maxed, h + 1)
                            if h >= 2:
                                act.wait_ge(s.turned, (h - 1) * NG)
                            act.activation(pr[:, h % 2, 0:W], sc[:].rearrange("p a b -> p (a b)")[:, 0:W], ACT.Exp,
                                           bias=mx[:, h:h + 1], accum_out=den[:, h:h + 1]).then_inc(s.exps, 1)

                    @block.vector
                    def _(dve):
                        def keep(h):
                            for k in range(NG):
                                n = h * NG + k
                                dve.wait_ge(s.turned, n + 1)
                                if n >= 2:
                                    dve.wait_ge(s.weighed, n - 1)
                                dve.tensor_copy(pT[:, n % 2], tp[:, n % 2]).then_inc(s.kept_v, 1)

                        for h in range(HEADS):
                            dve.wait_ge(s.scored, h + 1)
                            dve.tensor_reduce(mx[:, h:h + 1], sc[:].rearrange("p a b -> p (a b)")[:, 0:W], AX.X,
                                              ALU.max)
                            dve.drain()
                            dve.tensor_scalar(mx[:, h:h + 1], mx[:, h:h + 1], -1.0, None, ALU.mult)\
                               .then_inc(s.maxed, 1)
                            if h:
                                keep(h - 1)
                        keep(HEADS - 1)
                        dve.wait_ge(s.exps, HEADS)
                        dve.reciprocal(den[:], den[:])
                        dve.wait_ge(s.weighed, HEADS * NG)
                        dve.wait_ge(s.silus, 1)
                        dve.drain()
                        dve.tensor_tensor(y[:], o[:], spread(den[:], 2, HD), ALU.mult)
                        dve.drain()
                        y2 = y[:].rearrange("p h d -> p (h d)")
                        dve.tensor_tensor(y2, y2, z[:], ALU.mult).then_inc(s.y_done, 1)

                    @block.tensor
                    def _(pe):
                        def score(h):
                            for k in range(NG):
                                last = k == NG - 1
                                m = pe.matmul(sc[:, k], qb[:, h], kT[:, h, k * GROUP:(k + 1) * GROUP], start=True,
                                              stop=not last)
                                if last:
                                    m = pe.matmul(sc[:, k], c.ident, c.all[:, bass.ds(CAUSAL0 + 3 * P - j * P, GROUP)],
                                                  start=False, stop=True)
                            m.then_inc(s.scored, 1)

                        def turn(n):
                            h, k = n // NG, n % NG
                            if n >= 2:
                                pe.wait_ge(s.kept_v, n - 1)
                            for b in range(4):
                                m = pe.transpose(tp[:, n % 2, b], pr[:, h % 2, (4 * k + b) * P:(4 * k + b + 1) * P],
                                                 c.ident)
                            m.then_inc(s.turned, 1)

                        def weigh(n):
                            h, k = n // NG, n % NG
                            pe.wait_ge(s.kept_v, n + 1)
                            for b in range(4):
                                m = pe.matmul(o[:, h], pT[:, n % 2, b], v[:, 4 * k + b, h * HD:(h + 1) * HD],
                                              start=(k == 0 and b == 0), stop=(k == NG - 1 and b == 3))
                            m.then_inc(s.weighed, 1)

                        pe.wait_ge(s.q_here, 1)
                        score(0)
                        for h in range(HEADS):
                            pe.wait_ge(s.exps, h + 1)
                            if h + 1 < HEADS:
                                score(h + 1)
                            turn(h * NG)
                            for k in range(1, NG):
                                turn(h * NG + k)
                                weigh(h * NG + k - 1)
                            weigh(h * NG + NG - 1)


def mlstm(nc, c, w, proj, mixed):
    V1 = HD + 1
    with ExitStack() as ctx:
        B = Buffers(nc, ctx, "ml")
        cw = B.sb("cw", [P, 4, 2 * GW])
        cb = B.sb("cb", [P, 2 * GW])
        gb = B.sb("gb", [P, 2 * HEADS])
        og = B.sb("og", [P, GW])
        state = B.sb("state", [P, 2, 2 * V1])
        m_prev = B.sb("m_prev", [HEADS, 1])
        x = B.sb("x", [P, 4, 2 * GW])
        vx = B.sb("vx", [P, HEADS, V1])
        vin = B.sb("vin", [P, GW])
        gi = B.sb("gi", [P, 2 * HEADS])
        oz = B.sb("oz", [P, 2, GW])
        qk = B.sb("qk", [P, 2 * GW])
        a_tok = B.sb("a_tok", [P, HEADS])
        nb = B.sb("nb", [P, HEADS])
        a_row = B.sb("a_row", [HEADS, P])
        M = B.sb("M", [HEADS, P])
        nM = B.sb("nM", [HEADS, P])
        rows = B.sb("rows", [HEADS, 3, P])
        tok = B.sb("tok", [P, 3, HEADS])
        cd = B.sb("cd", [P, 2])
        qkT = B.sb("qkT", [P, 4, P])
        E = B.sb("E", [P, HEADS, P])
        kw = B.sb("kw", [P, HEADS, HD])
        num = B.sb("num", [P, HEADS, V1])
        h = B.sb("h", [P, HEADS, HD])
        sq = B.sb("sq", [P, HEADS, HD])
        ss = B.sb("ss", [P, HEADS])
        small = B.ps("small", [P, 512])
        p_nb, p_ar, p_nr = small[:, 0:4], small[0:HEADS, 64:192], small[0:HEADS, 192:320]
        p_tok, p_cd = small[:, 320:332].rearrange("p (a h) -> p a h", a=3), small[:, 340:342]
        p_qk = B.ps("p_qk", [P, 4, P])
        p_M = B.ps("p_M", [P, HEADS, P])
        both = B.ps("both", [P, 2, 512])
        p_s = both[:, :, 0:2 * P].rearrange("p r (j t) -> p j r t", j=2)
        p_int = both[:, :, 2 * P:2 * P + 2 * V1].rearrange("p r (j e) -> p j r e", j=2)
        p_in = B.ps("p_in", [P, HEADS, V1])
        p_up = B.ps("p_up", [P, 2, 2 * V1])
        load(nc, "ml_w", [(cw[:, j], row(w['mlstm_conv_w'][j])) for j in range(4)]
             + [(cb[:], row(w['mlstm_conv_b'])), (gb[:, 0:HEADS], row(w['mlstm_i_b'])),
                (gb[:, HEADS:], row(w['mlstm_f_b'])), (og[:], row(w['mlstm_out_g']))])
        with step(nc, "cleared") as (block, s):

            @block.vector
            def _(dve):
                dve.memset(state[:], 0.0).then_inc(s.cleared, 1)
                dve.memset(m_prev[:], 0.0).then_inc(s.cleared, 1)
                dve.memset(vx[:, :, HD:V1], 1.0).then_inc(s.cleared, 1)
                dve.wait_ge(s.cleared, 3)

        with nc.Fori(0, TILES) as i:
            with step(nc, "x_in v_in g_in oz_in conv_late conved qk_done gates_in logf sums a_done rows_t "
                          "M_done exps_r spread_M toks tok_done cd_ps Ein Eexp turned qkT_done scores "
                          "weighted num_ps kw_done up_ps sqd rs y_done stored tanhs") as (block, s):

                @block.sync
                def _(sp):
                    for j in range(4):
                        sp.dma_start(x[:, j], proj[bass.ds(i * P + (PAD - 3 + j), P), C_QK:C_QK + 2 * GW])\
                          .then_inc(s.x_in, 16)
                    sp.dma_start(gi[:], proj[bass.ds(i * P + PAD, P), C_I:C_I + 2 * HEADS]).then_inc(s.g_in, 16)
                    sp.dma_start(vin[:], proj[bass.ds(i * P + PAD, P), C_V:C_V + GW]).then_inc(s.v_in, 16)
                    sp.dma_start(oz[:].rearrange("p a c -> p (a c)"),
                                 proj[bass.ds(i * P + PAD, P), C_O:C_O + 2 * GW]).then_inc(s.oz_in, 16)
                    sp.wait_ge(s.y_done, 1)
                    sp.dma_start(mixed[bass.ds(i * P, P), 2 * GW:3 * GW], h[:].rearrange("p h d -> p (h d)"))\
                      .then_inc(s.stored, 16)
                    sp.wait_ge(s.stored, 16)

                @block.gpsimd
                def _(pool):
                    pool.wait_ge(s.x_in, 64)
                    pool.tensor_tensor(x[:, 2:4], x[:, 2:4], cw[:, 2:4], ALU.mult).then_inc(s.conv_late, 1)

                @block.scalar
                def _(act):
                    act.wait_ge(s.oz_in, 16)
                    act.activation(oz[:, 1], oz[:, 1], ACT.Silu)
                    act.activation(oz[:, 0], oz[:, 0], ACT.Tanh, scale=0.5).then_inc(s.tanhs, 1)
                    act.wait_ge(s.conved, 1)
                    act.activation(qk[:], qk[:], ACT.Silu).then_inc(s.qk_done, 1)
                    act.wait_ge(s.gates_in, 1)
                    act.activation(gi[:, HEADS:], gi[:, HEADS:], ACT.Exp, scale=-1.0)
                    act.drain()
                    act.activation(gi[:, HEADS:], gi[:, HEADS:], ACT.Ln, bias=c.ones[:, 0:1]).then_inc(s.logf, 1)
                    act.wait_ge(s.turned, 1)
                    act.activation(qkT[:, 0:2], p_qk[:, 0:2], ACT.Copy)
                    act.activation(qkT[:, 2:4], p_qk[:, 2:4], ACT.Copy, scale=HD ** -0.5).then_inc(s.qkT_done, 1)
                    act.wait_ge(s.M_done, 1)
                    act.activation(rows[:, 0], nM[:], ACT.Exp, bias=m_prev[:, 0:1])
                    act.activation(rows[:, 1], rows[:, 1], ACT.Exp)
                    act.activation(rows[:, 2], a_row[:], ACT.Exp, bias=nM[:, P - 1:P]).then_inc(s.exps_r, 1)
                    act.wait_ge(s.Ein, 1)
                    act.activation(E[:], E[:], ACT.Exp).then_inc(s.Eexp, 1)
                    act.wait_ge(s.sqd, 1)
                    rstd(act, c, ss[:], HD).then_inc(s.rs, 1)

                @block.vector
                def _(dve):
                    dve.wait_ge(s.g_in, 16)
                    dve.tensor_tensor(gi[:], gi[:], gb[:], ALU.add).then_inc(s.gates_in, 1)
                    dve.wait_ge(s.x_in, 64)
                    dve.tensor_tensor(x[:, 0:2], x[:, 0:2], cw[:, 0:2], ALU.mult)
                    dve.drain()
                    dve.tensor_tensor(qk[:], x[:, 0], x[:, 1], ALU.add)
                    dve.drain()
                    dve.tensor_tensor(qk[:], qk[:], cb[:], ALU.add)
                    dve.wait_ge(s.conv_late, 1)
                    dve.tensor_tensor(x[:, 2], x[:, 2], x[:, 3], ALU.add)
                    dve.drain()
                    dve.tensor_tensor(qk[:], qk[:], x[:, 2], ALU.add).then_inc(s.conved, 1)
                    dve.wait_ge(s.v_in, 16)
                    dve.tensor_copy(vx[:, :, 0:HD], vin[:].rearrange("p (h d) -> p h d", h=HEADS))
                    dve.wait_ge(s.sums, 1)
                    dve.tensor_copy(nb[:], p_nb)
                    dve.tensor_tensor(a_tok[:], gi[:, 0:HEADS], p_nb, ALU.add)
                    dve.drain().then_inc(s.a_done, 1)
                    dve.wait_ge(s.rows_t, 1)
                    dve.tensor_copy(a_row[:], p_ar)
                    dve.drain()
                    dve.tensor_tensor_scan(M[:], a_row[:], a_row[:], m_prev[:, 0:1], ALU.max, ALU.max)
                    dve.drain()
                    dve.tensor_scalar(nM[:], M[:], -1.0, None, ALU.mult)
                    dve.tensor_tensor(rows[:, 1], p_nr, M[:], ALU.subtract)
                    dve.drain().then_inc(s.M_done, 1)
                    dve.wait_ge(s.spread_M, 1)
                    for k in range(HEADS):
                        dve.tensor_scalar(E[:, k], p_M[:, k], a_tok[:, k:k + 1], 0.0, ALU.add, ALU.min)
                    dve.drain().then_inc(s.Ein, 1)
                    dve.wait_ge(s.toks, 1)
                    dve.tensor_scalar(m_prev[:], M[:, P - 1:P], p_nr[:, P - 1:P], None, ALU.subtract)
                    dve.tensor_copy(tok[:], p_tok)
                    dve.tensor_copy(cd[:], p_cd)
                    dve.drain()
                    dve.wait_ge(s.qk_done, 1)
                    k3 = qk[:, GW:].rearrange("p (h d) -> p h d", h=HEADS)
                    dve.tensor_tensor(kw[:], k3, spread(tok[:, 2], 2, HD), ALU.mult)
                    dve.drain()
                    dve.tensor_scalar(kw[:], kw[:], HD ** -0.5, None, ALU.mult).then_inc(s.kw_done, 1)
                    dve.wait_ge(s.Eexp, 1)
                    dve.tensor_tensor(E[:], E[:], spread(c.upto, 1, HEADS), ALU.mult)
                    dve.wait_ge(s.scores, 1)
                    dve.drain()
                    E4 = E[:].rearrange("p (j r) t -> p j r t", j=2)
                    dve.tensor_tensor(E4, E4, p_s, ALU.mult).then_inc(s.weighted, 1)
                    dve.wait_ge(s.num_ps, 1)
                    for j in range(2):
                        dve.tensor_tensor(num[:, 2 * j:2 * j + 2], p_int[:, j], spread(tok[:, 0, 2 * j:2 * j + 2], 2, V1),
                                          ALU.mult)
                    dve.drain()
                    dve.tensor_tensor(num[:], num[:], p_in[:], ALU.add)
                    dve.drain()
                    d = num[:, :, HD:V1].rearrange("p h o -> p (h o)")
                    dve.scalar_tensor_tensor(out=ss[:], in0=d, scalar=-1.0, in1=d, op0=ALU.mult, op1=ALU.max)
                    dve.drain()
                    dve.tensor_tensor(ss[:], ss[:], tok[:, 1], ALU.max)
                    dve.drain()
                    dve.reciprocal(ss[:], ss[:])
                    dve.wait_ge(s.tanhs, 1)
                    oh = oz[:, 0].rearrange("p (h d) -> p h d", h=HEADS)
                    dve.tensor_scalar(oh, oh, 0.5, 0.5, ALU.mult, ALU.add)
                    dve.drain()
                    dve.tensor_tensor(h[:], num[:, :, 0:HD], spread(ss[:], 2, HD), ALU.mult)
                    dve.drain()
                    dve.tensor_tensor(h[:], h[:], oh, ALU.mult)
                    dve.drain()
                    dve.tensor_tensor(sq[:], h[:], h[:], ALU.mult)
                    dve.drain()
                    dve.tensor_reduce(ss[:], sq[:], AX.X, ALU.add).then_inc(s.sqd, 1)
                    h2 = h[:].rearrange("p h d -> p (h d)")
                    dve.tensor_tensor(h2, h2, og[:], ALU.mult)
                    dve.drain()
                    dve.tensor_tensor(h2, h2, oz[:, 1], ALU.mult)
                    dve.wait_ge(s.up_ps, 1)
                    for j in range(2):
                        dve.scalar_tensor_tensor(out=state[:, j], in0=state[:, j], scalar=cd[:, j:j + 1],
                                                 in1=p_up[:, j], op0=ALU.mult, op1=ALU.add)
                    dve.wait_ge(s.rs, 1)
                    dve.drain()
                    dve.tensor_tensor(h[:], h[:], spread(ss[:], 2, HD), ALU.mult).then_inc(s.y_done, 1)

                @block.tensor
                def _(pe):
                    pe.wait_ge(s.logf, 1)
                    pe.matmul(p_nb, c.upto, gi[:, HEADS:], start=True, stop=True).then_inc(s.sums, 1)
                    pe.wait_ge(s.a_done, 1)
                    pe.transpose(p_ar, a_tok[:], c.ident)
                    pe.transpose(p_nr, nb[:], c.ident).then_inc(s.rows_t, 1)
                    pe.wait_ge(s.qk_done, 1)
                    for j in range(4):
                        m = pe.transpose(p_qk[:, j], qk[:, j * P:(j + 1) * P], c.ident)
                    m.then_inc(s.turned, 1)
                    pe.wait_ge(s.M_done, 1)
                    for k in range(HEADS):
                        m = pe.matmul(p_M[:, k], c.all[0:HEADS, ROW[k]], nM[:], start=True, stop=True)
                    m.then_inc(s.spread_M, 1)
                    pe.wait_ge(s.exps_r, 1)
                    for k in range(3):
                        pe.transpose(p_tok[:, k], rows[:, k], c.ident[0:HEADS, 0:HEADS])
                    for j in range(2):
                        m = pe.matmul(p_cd[:, j:j + 1], c.all[0:HEADS, PAIR[j]], rows[:, 0, P - 1:P], start=True,
                                      stop=True)
                    m.then_inc(s.toks, 1)
                    pe.wait_ge(s.qkT_done, 1)
                    for k in range(HEADS):
                        off, j = HD * (k % 2), k // 2
                        m = pe.matmul(p_s[:, j, k % 2], qkT[off:off + HD, 2 + j], qkT[off:off + HD, j], start=True, stop=True)
                    for k in range(HEADS):
                        off, j = HD * (k % 2), k // 2
                        m = pe.matmul(p_int[:, j, k % 2], qkT[off:off + HD, j],
                                  state[off:off + HD, j, (k % 2) * V1:(k % 2 + 1) * V1], start=True, stop=True)
                    m.then_inc(s.scores, 1)
                    pe.wait_ge(s.weighted, 1)
                    for k in range(HEADS):
                        m = pe.matmul(p_in[:, k], E[:, k], vx[:, k], start=True, stop=True)
                    m.then_inc(s.num_ps, 1)
                    pe.wait_ge(s.kw_done, 1)
                    for j in range(2):
                        m = pe.matmul(p_up[:, j], kw[:, 2 * j:2 * j + 2].rearrange("p h d -> p (h d)"),
                                      vx[:, 2 * j:2 * j + 2].rearrange("p h d -> p (h d)"), start=True, stop=True)
                    m.then_inc(s.up_ps, 1)


def rwkv(nc, c, w, proj, mixed):
    R_E = float(np.exp(-0.5))
    with ExitStack() as ctx:
        B = Buffers(nc, ctx, "rw")
        mu = B.sb("mu", [P, D_W])
        par = B.sb("par", [P, 6, GW])
        lo2 = B.sb("lo2", [RANK, 2, GW])
        state = B.sb("state", [P, 2, HD])
        load(nc, "rw_w", [(mu[:], row(w['rwkv_mu'])), (lo2[:, 0], w['rwkv_w2']), (lo2[:, 1], w['rwkv_a2'])]
             + [(par[:, k], row(w[n])) for k, n in enumerate(['rwkv_w0', 'rwkv_a0', 'rwkv_k_k', 'rwkv_k_a'])]
             + [(par[:, 4], row(w['rwkv_r_k'].rearrange("h d -> (h d)"))), (par[:, 5], row(w['rwkv_ln_g']))])
        with step(nc, "cleared") as (block, s):

            @block.vector
            def _(dve):
                dve.memset(state[:], 0.0).then_inc(s.cleared, 1)
                dve.wait_ge(s.cleared, 1)

        x = B.sb("x", [P, D_W])
        pv = B.sb("pv", [P, D_W])
        loT = B.sb("loT", [RANK, 2, P])
        wa = B.sb("wa", [P, 2, GW])
        kk = B.sb("kk", [P, HEADS, HD])
        kn = B.sb("kn", [P, GW])
        sq = B.sb("sq", [P, HEADS, HD])
        ss = B.sb("ss", [P, HEADS])
        bon = B.sb("bon", [P, HEADS])
        ex = B.sb("ex", [P, 3, GW])
        em = B.sb("em", [P, 2, 2])
        tl = B.sb("tl", [P, 4, GW])
        XT4 = B.sb("XT4", [P, 2, 4, P])
        G = B.sb("G", [P, 2, HEADS, 2, P])
        X = B.sb("X", [P, HEADS, P])
        XT = B.sb("XT", [P, HEADS, P])
        Pm = B.sb("Pm", [P, HEADS, P])
        R = B.sb("R", [P, HEADS, HD])
        U = B.sb("U", [P, HEADS, HD])
        S0 = B.sb("S0", [P, 2, HD])
        y = B.sb("y", [P, HEADS, HD])
        big = B.ps("big", [P, 8, 512])
        b0, b1, b2, b3, b4, b5, b6, b7 = (big[:, k] for k in range(8))
        with nc.Fori(0, TILES) as i:
            with step(nc, "x_in p_in shifted mixed_x lows low_ps low_kept wa_ps wa_in tanhs la_done cums exps kksq "
                          "norms kk_ready tilde turned_a turned_b kept_a kept_v s0_done grams g_done p1 p1c dx dxc "
                          "r_ps r_done u_ps u_done y_ps st_ps sqd rs y_done stored silus bonus_in xT_done") as (block, s):

                @block.sync
                def _(sp):
                    sp.dma_start(x[:], proj[bass.ds(i * P + PAD, P), D_0:D_0 + D_W]).then_inc(s.x_in, 16)
                    sp.dma_start(pv[:], proj[bass.ds(i * P + (PAD - 1), P), D_0:D_0 + D_W]).then_inc(s.p_in, 16)
                    sp.wait_ge(s.y_done, 1)
                    sp.dma_start(mixed[bass.ds(i * P, P), 3 * GW:4 * GW], y[:].rearrange("p h d -> p (h d)"))\
                      .then_inc(s.stored, 16)
                    sp.wait_ge(s.stored, 16)

                @block.scalar
                def _(act):
                    act.wait_ge(s.shifted, 1)
                    act.activation(x[:, D_WLO:D_WLO + RANK], x[:, D_WLO:D_WLO + RANK], ACT.Tanh).then_inc(s.lows, 1)
                    act.activation(x[:, D_Z:D_Z + GW], x[:, D_Z:D_Z + GW], ACT.Silu).then_inc(s.silus, 1)
                    act.wait_ge(s.wa_in, 1)
                    act.activation(wa[:], wa[:], ACT.Tanh, scale=0.5).then_inc(s.tanhs, 1)
                    act.wait_ge(s.kksq, 1)
                    act.activation(ss[:], ss[:], ACT.Sqrt).then_inc(s.norms, 1)
                    act.wait_ge(s.cums, 1)
                    cps = b0.rearrange("p (a c) -> p a c", a=2)
                    act.activation(ex[:, 0:2], cps, ACT.Exp)
                    act.activation(ex[:, 2], cps[:, 0], ACT.Exp, scale=-1.0)
                    act.activation(em[:], b1[:, 0:4].rearrange("p (j e) -> p j e", j=2), ACT.Exp).then_inc(s.exps, 1)
                    act.wait_ge(s.turned_a, 1)
                    act.activation(XT4[:, 0], b2.rearrange("p (a t) -> p a t", a=4), ACT.Copy).then_inc(s.kept_a, 1)
                    for l in range(LEVELS):
                        act.wait_ge(s.p1, l + 1)
                        act.activation(Pm[:], b0.rearrange("p (h t) -> p h t", h=HEADS), ACT.Copy).then_inc(s.p1c, 1)
                    act.wait_ge(s.sqd, 1)
                    rstd(act, c, ss[:], HD).then_inc(s.rs, 1)

                @block.vector
                def _(dve):
                    h4 = lambda ap: ap.rearrange("p (h d) -> p h d", h=HEADS)
                    dve.wait_ge(s.x_in, 16)
                    dve.wait_ge(s.p_in, 16)
                    dve.tensor_tensor(pv[:], pv[:], x[:], ALU.subtract)
                    dve.drain()
                    dve.tensor_tensor(pv[:], pv[:], mu[:], ALU.mult)
                    dve.drain()
                    dve.tensor_tensor(x[:], x[:], pv[:], ALU.add).then_inc(s.shifted, 1)
                    dve.wait_ge(s.low_ps, 1)
                    dve.tensor_copy(loT[:], b1[0:RANK, 0:2 * P].rearrange("p (a t) -> p a t", a=2))\
                       .then_inc(s.low_kept, 1)
                    k, v, r = x[:, D_K:D_K + GW], x[:, D_V:D_V + GW], x[:, D_R:D_R + GW]
                    dve.drain()
                    kk2 = kk[:].rearrange("p h d -> p (h d)")
                    dve.tensor_tensor(kk2, k, par[:, 2], ALU.mult)
                    dve.drain()
                    dve.tensor_tensor(sq[:], kk[:], kk[:], ALU.mult)
                    dve.drain()
                    dve.tensor_reduce(ss[:], sq[:], AX.X, ALU.add).then_inc(s.kksq, 1)
                    dve.wait_ge(s.wa_ps, 1)
                    dve.tensor_tensor(wa[:], b2.rearrange("p (a c) -> p a c", a=2), par[:, 0:2], ALU.add)\
                       .then_inc(s.wa_in, 1)
                    dve.wait_ge(s.tanhs, 1)
                    dve.tensor_scalar(wa[:, 0], wa[:, 0], -0.5 * R_E, -0.5 * R_E, ALU.mult, ALU.add)
                    dve.tensor_scalar(wa[:, 1], wa[:, 1], 0.5, 0.5, ALU.mult, ALU.add)
                    dve.drain().then_inc(s.la_done, 1)
                    dve.wait_ge(s.norms, 1)
                    dve.tensor_scalar(ss[:], ss[:], 1e-12, None, ALU.max)
                    dve.drain()
                    dve.reciprocal(ss[:], ss[:])
                    dve.scalar_tensor_tensor(out=kn[:], in0=wa[:, 1], scalar=-1.0, in1=par[:, 3], op0=ALU.add,
                                             op1=ALU.mult)
                    dve.drain()
                    dve.tensor_tensor(kk[:], kk[:], spread(ss[:], 2, HD), ALU.mult)
                    dve.scalar_tensor_tensor(out=kn[:], in0=kn[:], scalar=1.0, in1=k, op0=ALU.add, op1=ALU.mult)
                    dve.drain()
                    dve.tensor_tensor(sq[:].rearrange("p h d -> p (h d)"), r, kn[:], ALU.mult)
                    dve.drain()
                    dve.tensor_tensor(sq[:].rearrange("p h d -> p (h d)"), sq[:].rearrange("p h d -> p (h d)"),
                                      par[:, 4], ALU.mult)
                    dve.drain()
                    dve.tensor_reduce(bon[:], sq[:], AX.X, ALU.add)
                    dve.wait_ge(s.exps, 1)
                    dve.tensor_tensor(tl[:, 0], r, ex[:, 0], ALU.mult)
                    dve.scalar_tensor_tensor(out=tl[:, 1], in0=kk2, scalar=-1.0, in1=ex[:, 1], op0=ALU.mult,
                                             op1=ALU.mult)
                    dve.tensor_tensor(tl[:, 3], kn[:], ex[:, 2], ALU.mult)
                    dve.tensor_tensor(tl[:, 2], kk2, ex[:, 2], ALU.mult)
                    dve.drain()
                    dve.tensor_tensor(tl[:, 2], tl[:, 2], wa[:, 1], ALU.mult).then_inc(s.tilde, 1)
                    for j in range(2):
                        d = dve.tensor_scalar(S0[:, j], state[:, j], em[:, j, 0:1], None, ALU.mult)
                    d.then_inc(s.s0_done, 1)
                    dve.wait_ge(s.turned_b, 1)
                    dve.tensor_copy(XT4[:, 1], b3.rearrange("p (a t) -> p a t", a=4)).then_inc(s.kept_v, 1)
                    masks = c.all[:, 1 * P:3 * P].rearrange("p (a t) -> p a t", a=2)
                    for h in range(HEADS):
                        dve.wait_ge(s.grams, h + 1)
                        ps = big[:, 4 + 2 * (h % 2) + h // 2].rearrange("p (b a t) -> p b a t", b=2, a=2)
                        for b in range(2):
                            d = dve.tensor_tensor(G[:, b, h], ps[:, b], masks, ALU.mult)
                        d.then_inc(s.g_done, 1)
                    dve.tensor_copy(X[:], spread(c.ident, 1, HEADS))
                    dve.tensor_copy(XT[:], spread(c.ident, 1, HEADS))
                    dve.drain().then_inc(s.xT_done, 1)
                    for l in range(LEVELS):
                        dve.wait_ge(s.dx, l + 1)
                        if l < LEVELS - 1:
                            dve.copy_predicated(X[:], spread(c.all[:, LEVEL_T[l]].bitcast(U32), 1, HEADS),
                                                b1.rearrange("p (h t) -> p h t", h=HEADS))
                        dve.copy_predicated(XT[:], spread(c.all[:, LEVEL[l]].bitcast(U32), 1, HEADS),
                                            b2.rearrange("p (h t) -> p h t", h=HEADS))
                        dve.drain().then_inc(s.dxc, 1)
                    par2 = lambda ap, a0: ap.rearrange("p r (j d) -> p j r d", d=HD)
                    dve.wait_ge(s.r_ps, 1)
                    R4 = R[:].rearrange("p (j r) d -> p j r d", j=2)
                    dve.tensor_copy(R4, par2(big[:, 4:8:2, 0:2 * HD], 0)).then_inc(s.r_done, 1)
                    dve.wait_ge(s.u_ps, 1)
                    dve.tensor_copy(U[:], b3[:, 0:GW].rearrange("p (h d) -> p h d", h=HEADS)).then_inc(s.u_done, 1)
                    dve.wait_ge(s.st_ps, 1)
                    for off in (0, HD):
                        o = slice(off, off + HD)
                        dve.tensor_tensor(S0[o], S0[o], b0[o, 0:2 * P].rearrange("p (j c) -> p j c", j=2)[:, :, o],
                                          ALU.add)
                    dve.drain()
                    for j in range(2):
                        dve.tensor_scalar(state[:, j], S0[:, j], em[:, j, 1:2], None, ALU.mult)
                    dve.wait_ge(s.y_ps, 1)
                    y4 = y[:].rearrange("p (j r) d -> p j r d", j=2)
                    dve.tensor_copy(y4, par2(big[:, 5:8:2, 0:2 * HD], 0))
                    dve.drain()
                    dve.tensor_tensor(sq[:], y[:], y[:], ALU.mult)
                    dve.drain()
                    dve.tensor_reduce(ss[:], sq[:], AX.X, ALU.add).then_inc(s.sqd, 1)
                    y2 = y[:].rearrange("p h d -> p (h d)")
                    dve.tensor_tensor(y2, y2, par[:, 5], ALU.mult)
                    dve.drain()
                    dve.tensor_tensor(sq[:], h4(v), spread(bon[:], 2, HD), ALU.mult)
                    dve.wait_ge(s.rs, 1)
                    dve.drain()
                    dve.tensor_tensor(y[:], y[:], spread(ss[:], 2, HD), ALU.mult)
                    dve.drain()
                    dve.tensor_tensor(y[:], y[:], sq[:], ALU.add)
                    dve.wait_ge(s.silus, 1)
                    dve.drain()
                    dve.tensor_tensor(y2, y2, x[:, D_Z:D_Z + GW], ALU.mult).then_inc(s.y_done, 1)

                @block.tensor
                def _(pe):
                    pe.wait_ge(s.lows, 1)
                    pe.transpose(b1[0:RANK, 0:P], x[:, D_WLO:D_WLO + RANK], c.ident)
                    pe.transpose(b1[0:RANK, P:2 * P], x[:, D_ALO:D_ALO + RANK], c.ident).then_inc(s.low_ps, 1)
                    pe.wait_ge(s.low_kept, 1)
                    pe.matmul(b2[:, 0:GW], loT[:, 0], lo2[:, 0], start=True, stop=True)
                    pe.matmul(b2[:, GW:2 * GW], loT[:, 1], lo2[:, 1], start=True, stop=True).then_inc(s.wa_ps, 1)
                    pe.wait_ge(s.la_done, 1)
                    pe.matmul(b0[:, 0:GW], c.all[:, CENTRED], wa[:, 0], start=True, stop=True)
                    pe.matmul(b0[:, GW:2 * GW], c.all[:, CENTRED_BEFORE], wa[:, 0], start=True, stop=True)
                    for j in range(2):
                        lj = wa[:, 0, j * P:(j + 1) * P]
                        pe.matmul(b1[:, 2 * j:2 * j + 1], lj, c.upto[:, P // 2 - 1:P // 2], start=True, stop=True)
                        m = pe.matmul(b1[:, 2 * j + 1:2 * j + 2], lj, c.after[:, P // 2 - 1:P // 2], start=True,
                                      stop=True)
                    m.then_inc(s.cums, 1)
                    pe.wait_ge(s.tilde, 1)
                    for j in range(2):
                        for a in range(4):
                            m = pe.transpose(big[:, 2 + j, a * P:(a + 1) * P], tl[:, a, j * P:(j + 1) * P], c.ident)
                        m.then_inc((s.turned_a, s.turned_b)[j], 1)
                    pe.wait_ge(s.kept_a, 1)
                    for h in range(HEADS):
                        off, j = HD * (h % 2), h // 2
                        if h == 2:
                            pe.wait_ge(s.kept_v, 1)
                        o = slice(off, off + HD)
                        ps = big[:, 4 + 2 * (h % 2) + j]
                        for b in range(2):
                            m = pe.matmul(ps[:, b * GW:(b + 1) * GW], XT4[o, j, 2 + b],
                                          XT4[o, j, 0:2].rearrange("p a t -> p (a t)"), start=True, stop=True)
                        m.then_inc(s.grams, 1)
                    pe.wait_ge(s.g_done, HEADS)
                    pe.wait_ge(s.xT_done, 1)
                    for l in range(LEVELS):
                        if l:
                            pe.wait_ge(s.dxc, l)
                        for h in range(HEADS):
                            m = pe.matmul(b0[:, h * P:(h + 1) * P], G[:, 0, h, 1], X[:, h], start=True, stop=True)
                        m.then_inc(s.p1, 1)
                        pe.wait_ge(s.p1c, l + 1)
                        for h in range(HEADS):
                            if l < LEVELS - 1:
                                pe.matmul(b1[:, h * P:(h + 1) * P], XT[:, h], Pm[:, h], start=True, stop=True)
                            m = pe.matmul(b2[:, h * P:(h + 1) * P], Pm[:, h], XT[:, h], start=True, stop=True)
                        m.then_inc(s.dx, 1)
                    v = x[:, D_V:D_V + GW].rearrange("p (h d) -> p h d", h=HEADS)
                    pe.wait_ge(s.s0_done, 1)
                    for h in range(HEADS):
                        off, j = HD * (h % 2), h // 2
                        o = slice(off, off + HD)
                        dst = big[:, 4 + 2 * (h % 2), j * HD:(j + 1) * HD]
                        pe.matmul(dst, XT4[o, j, 1], S0[o, j], start=True, stop=False)
                        m = pe.matmul(dst, G[:, 1, h, 1], v[:, h], start=False, stop=True)
                    m.then_inc(s.r_ps, 1)
                    pe.wait_ge(s.r_done, 1)
                    pe.wait_ge(s.dxc, LEVELS)
                    for h in range(HEADS):
                        m = pe.matmul(b3[:, h * HD:(h + 1) * HD], XT[:, h], R[:, h], start=True, stop=True)
                    m.then_inc(s.u_ps, 1)
                    pe.wait_ge(s.u_done, 1)
                    for h in range(HEADS):
                        off, j = HD * (h % 2), h // 2
                        o = slice(off, off + HD)
                        dst = big[:, 5 + 2 * (h % 2), j * HD:(j + 1) * HD]
                        pe.matmul(dst, XT4[o, j, 0], S0[o, j], start=True, stop=False)
                        pe.matmul(dst, G[:, 0, h, 0], U[:, h], start=False, stop=False)
                        m = pe.matmul(dst, G[:, 1, h, 0], v[:, h], start=False, stop=True)
                    m.then_inc(s.y_ps, 1)
                    for j in range(2):
                        dst = b0[:, j * P:(j + 1) * P]
                        pe.matmul(dst, tl[:, 2, j * P:(j + 1) * P],
                                  U[:, 2 * j:2 * j + 2].rearrange("p h d -> p (h d)"), start=True, stop=False)
                        m = pe.matmul(dst, tl[:, 3, j * P:(j + 1) * P], x[:, D_V + j * P:D_V + (j + 1) * P],
                                      start=False, stop=True)
                    m.then_inc(s.st_ps, 1)


ALPHA = 2.0 ** 0.25


def project_out(nc, c, mix, w_out, x_in, x_out, name, turned_out=None, ln=None):
    K = mix.shape[1] // P
    KB = [(k, min(4, K - k)) for k in range(0, K, 4)]
    U = 4
    with ExitStack() as ctx:
        B = Buffers(nc, ctx, name)
        wo = B.sb("wo", [P, K, D_MODEL])
        m = B.sb("m", [P, 2, K * P])
        x = B.sb("x", [P, U, D_MODEL])
        mT = B.sb("mT", [P, 2, K, P])
        tp = B.ps("tp", [P, 2, 4, P])
        acc = B.ps("acc", [P, 2, 2, 512])
        loads = [(wo[:], w_out.rearrange("(k p) n -> p k n", p=P))]
        if ln:
            gb = B.sb("gb", [P, 2, D_MODEL])
            st = B.sb("st", [P, 2, 6])
            ag = B.sb("ag", [P, 2])
            loads += [(gb[:, 0], row(ln[0])), (gb[:, 1], row(ln[1]))]
        else:
            tq = B.ps("tq", [P, 2, 4, P])
        load(nc, f"{name}_w", loads)
        nb = len(KB)
        with nc.Fori(0, TILES // U) as i:
            with step(nc, "m_in0 m_in1 x_in turned kept prod summed vars rs stored x_turned x_kept") as (block, s):
                m_in = (s.m_in0, s.m_in1)

                @block.sync
                def _(sp):
                    sp.dma_start(x[:], tokens(x_in, i * U, U, 0, D_MODEL)).then_inc(s.x_in, 16)
                    for u in range(U):
                        if u >= 2:
                            sp.wait_ge(s.turned, nb * (u - 1))
                        sp.dma_start(m[:, u % 2], mix[bass.ds((i * U + u) * P, P), :]).then_inc(m_in[u % 2], 16)
                    for u in range(U):
                        sp.wait_ge(s.summed, u + 1)
                        sp.dma_start(x_out[bass.ds((i * U + u) * P, P), :], x[:, u]).then_inc(s.stored, 16)
                    sp.wait_ge(s.stored, 16 * U)

                @block.tensor
                def _(pe):
                    def turn(u):
                        pe.wait_ge(m_in[u % 2], 16 * (u // 2 + 1))
                        for b, (k0, kn) in enumerate(KB):
                            n = u * nb + b
                            if n >= 2:
                                pe.wait_ge(s.kept, n - 1)
                            for k in range(kn):
                                t = pe.transpose(tp[:, n % 2, k], m[:, u % 2, (k0 + k) * P:(k0 + k + 1) * P], c.ident)
                            t.then_inc(s.turned, 1)

                    def multiply(u):
                        pe.wait_ge(s.kept, nb * (u + 1))
                        if u >= 2:
                            pe.wait_ge(s.summed, u - 1)
                        for n in range(2):
                            for k in range(K):
                                t = pe.matmul(acc[:, u % 2, n], mT[:, u % 2, k], wo[:, k, n * 512:(n + 1) * 512],
                                              start=(k == 0), stop=(k == K - 1))
                        t.then_inc(s.prod, 1)

                    def turn_x(u):
                        pe.wait_ge(s.summed, u + 1)
                        for b in range(2):
                            n = 2 * u + b
                            if n >= 2:
                                pe.wait_ge(s.x_kept, n - 1)
                            for k in range(4):
                                t = pe.transpose(tq[:, n % 2, k], x[:, u, (4 * b + k) * P:(4 * b + k + 1) * P],
                                                 c.ident)
                            t.then_inc(s.x_turned, 1)

                    turn(0)
                    for u in range(U):
                        if u + 1 < U:
                            turn(u + 1)
                        multiply(u)
                        if not ln and u:
                            turn_x(u - 1)
                    if not ln:
                        turn_x(U - 1)

                @block.scalar
                def _(act):
                    def keep(u):
                        for b, (k0, kn) in enumerate(KB):
                            n = u * nb + b
                            act.wait_ge(s.turned, n + 1)
                            if u >= 2 and b == 0:
                                act.wait_ge(s.prod, u - 1)
                            act.activation(mT[:, u % 2, k0:k0 + kn], tp[:, n % 2, 0:kn], ACT.Copy)\
                               .then_inc(s.kept, 1)

                    keep(0)
                    for u in range(U):
                        if u + 1 < U:
                            keep(u + 1)
                        if ln:
                            act.wait_ge(s.vars, u + 1)
                            act.activation(ag[:, 1:2], ag[:, 1:2], ACT.Ln, bias=c.eps[:, 1:2])
                            act.drain()
                            act.activation(ag[:, 1:2], ag[:, 1:2], ACT.Exp, scale=-0.5).then_inc(s.rs, 1)

                @block.vector
                def _(dve):
                    def keep_x(u):
                        for b in range(2):
                            n = 2 * u + b
                            dve.wait_ge(s.x_turned, n + 1)
                            dve.tensor_copy(turned_out[:, 4 * b:4 * b + 4, bass.ds((i * U + u) * P, P)],
                                            tq[:, n % 2]).then_inc(s.x_kept, 1)

                    dve.wait_ge(s.x_in, 16)
                    for u in range(U):
                        dve.wait_ge(s.prod, u + 1)
                        xu = x[:, u].rearrange("p (n c) -> p n c", n=2)
                        if not ln:
                            dve.tensor_tensor(xu, xu, acc[:, u % 2], ALU.add).then_inc(s.summed, 1)
                            if u:
                                keep_x(u - 1)
                            continue
                        for n in range(2):
                            dve.scalar_tensor_tensor(out=xu[:, n], in0=xu[:, n], scalar=ALPHA, in1=acc[:, u % 2, n],
                                                     op0=ALU.mult, op1=ALU.add)
                        dve.drain()
                        for n in range(2):
                            dve.bn_stats(st[:, n], xu[:, n])
                        dve.drain()
                        dve.bn_aggr(ag[:], st[:].rearrange("p a b -> p (a b)"))
                        dve.drain().then_inc(s.vars, 1)
                        dve.wait_ge(s.rs, u + 1)
                        dve.tensor_scalar(x[:, u], x[:, u], ag[:, 0:1], ag[:, 1:2], ALU.subtract, ALU.mult)
                        dve.drain()
                        dve.tensor_tensor(x[:, u], x[:, u], gb[:, 0], ALU.mult)
                        dve.drain()
                        dve.tensor_tensor(x[:, u], x[:, u], gb[:, 1], ALU.add).then_inc(s.summed, 1)
                    if not ln:
                        keep_x(U - 1)


def hgrn(nc, c, w, proj, mix):
    H = BH
    with ExitStack() as ctx:
        B = Buffers(nc, ctx, "hg")
        lb = B.sb("lb", [P, 2, H * BD])
        g = B.sb("g", [P, H * BD])
        state = B.sb("state", [P, H, BD])
        x = B.sb("x", [P, 4, H * BD])
        k = B.sb("k", [P, H * BD])
        qT = B.sb("qT", [P, H, P])
        kT = B.sb("kT", [P, H, P])
        bT = B.sb("bT", [P, H, P])
        E = B.sb("E", [P, 2, H, P])
        A = B.sb("A", [P, H, P])
        qe = B.sb("qe", [P, H, P])
        ke = B.sb("ke", [P, H, P])
        ktok = B.sb("ktok", [P, H, P])
        dec = B.sb("dec", [P, H])
        y = B.sb("y", [P, H, BD])
        sq = B.sb("sq", [P, H, BD])
        ss = B.sb("ss", [P, H])
        big = B.ps("big", [P, 8, 512])
        four = lambda n: big[:, n].rearrange("p (h t) -> p h t", h=H)
        load(nc, "hg_w", [(lb[:, 0], row(w['lb_logits_2'][0])), (lb[:, 1], row(w['lb_logits_2'][1])),
                          (g[:], row(w['hgrn_norm_g_2']))])
        with step(nc, "expd diffd cleared lbd") as (block, s):

            @block.vector
            def _(dve):
                dve.memset(state[:], 0.0).then_inc(s.cleared, 1)
                dve.tensor_tensor(E[:, 0].rearrange("p h t -> p (h t)"), lb[:, 0], lb[:, 1], ALU.max)
                dve.drain()
                for n in range(2):
                    dve.tensor_tensor(lb[:, n], lb[:, n], E[:, 0].rearrange("p h t -> p (h t)"), ALU.subtract)
                dve.drain().then_inc(s.diffd, 1)
                dve.wait_ge(s.expd, 1)
                dve.tensor_tensor(lb[:, 1], lb[:, 0], lb[:, 1], ALU.add)
                dve.drain()
                dve.reciprocal(lb[:, 1], lb[:, 1])
                dve.drain()
                dve.tensor_tensor(lb[:, 0], lb[:, 0], lb[:, 1], ALU.mult)
                dve.drain()
                dve.tensor_scalar(lb[:, 1], lb[:, 0], -1.0, 1.0, ALU.mult, ALU.add).then_inc(s.lbd, 1)

            @block.scalar
            def _(act):
                act.wait_ge(s.diffd, 1)
                act.activation(lb[:], lb[:], ACT.Exp).then_inc(s.expd, 1)

        with nc.Fori(0, TILES) as i:
            with step(nc, "x_in silus sigs f_done logf k_done turned_q q_kept turned_k k_kept sums b_kept diffs exps "
                          "tilde pairs picked e_in e_out ee_done ke_t ktok_done o_ps up_ps sqd rs y_done stored "
                          ) as (block, s):

                @block.sync
                def _(sp):
                    sp.dma_start(x[:].rearrange("p a c -> p (a c)"), proj[bass.ds(i * P, P), H_Q:H_Q + 4 * H * BD])\
                      .then_inc(s.x_in, 16)
                    sp.wait_ge(s.y_done, 1)
                    sp.dma_start(mix[bass.ds(i * P, P), 512:1024], y[:].rearrange("p h d -> p (h d)"))\
                      .then_inc(s.stored, 16)
                    sp.wait_ge(s.stored, 16)

                @block.scalar
                def _(act):
                    act.wait_ge(s.x_in, 16)
                    act.activation(x[:, 1], x[:, 1], ACT.Sigmoid).then_inc(s.sigs, 1)
                    act.activation(x[:, 0], x[:, 0], ACT.Silu)
                    act.activation(x[:, 3], x[:, 3], ACT.Silu).then_inc(s.silus, 1)
                    act.wait_ge(s.f_done, 1)
                    act.activation(x[:, 1], x[:, 1], ACT.Ln).then_inc(s.logf, 1)
                    act.wait_ge(s.turned_q, 1)
                    act.activation(qT[:], four(0), ACT.Copy).then_inc(s.q_kept, 1)
                    for l in range(LEVELS):
                        act.wait_ge(s.diffs, l + 1)
                        act.activation(E[:, l % 2], E[:, l % 2], ACT.Exp).then_inc(s.exps, 1)
                    act.wait_ge(s.e_in, 1)
                    act.activation(ke[:], ke[:], ACT.Exp)
                    act.activation(qe[:], bT[:], ACT.Exp)
                    act.activation(dec[:], bT[:, :, P - 1], ACT.Exp).then_inc(s.e_out, 1)
                    act.wait_ge(s.sqd, 1)
                    rstd(act, c, ss[:], BD).then_inc(s.rs, 1)

                @block.vector
                def _(dve):
                    dve.wait_ge(s.sigs, 1)
                    f = x[:, 1]
                    dve.tensor_tensor(f, f, lb[:, 1], ALU.mult)
                    dve.drain()
                    dve.tensor_tensor(f, f, lb[:, 0], ALU.add)
                    dve.drain()
                    dve.tensor_scalar(k[:], f, -1.0, 1.0, ALU.mult, ALU.add)
                    dve.drain().then_inc(s.f_done, 1)
                    dve.wait_ge(s.turned_k, 1)
                    dve.tensor_copy(kT[:], four(1)).then_inc(s.k_kept, 1)
                    dve.wait_ge(s.sums, 1)
                    dve.tensor_copy(bT[:], four(2)).then_inc(s.b_kept, 1)
                    dve.wait_ge(s.pairs, 1)
                    dve.drain()
                    dve.tensor_tensor(A[:], four(3), spread(c.ident, 1, H), ALU.mult)

                    def halves(ap, l):
                        half = 1 << l
                        v = ap.rearrange("p h (n a b) -> p h n a b", a=2, b=half)
                        return v[:, :, :, 0], v[:, :, :, 1]

                    def joint(l):
                        half = 1 << l
                        v = bT[:].rearrange("p h (n a b) -> p h n a b", a=2, b=half)[:, :, :, 0, half - 1]
                        return spread(v, 3, half)

                    def diffs(l):
                        e0, e1 = halves(E[:, l % 2], l)
                        b0, b1 = halves(bT[:], l)
                        if l >= 2:
                            dve.wait_ge(s.pairs, l)
                        dve.tensor_tensor(e1, b1, joint(l), ALU.subtract)
                        dve.tensor_tensor(e0, joint(l), b0, ALU.subtract)
                        dve.drain().then_inc(s.diffs, 1)

                    def tilde(l):
                        e0, e1 = halves(E[:, l % 2], l)
                        dve.wait_ge(s.exps, l + 1)
                        dve.tensor_tensor(e1, e1, halves(qT[:], l)[1], ALU.mult)
                        dve.tensor_tensor(e0, e0, halves(kT[:], l)[0], ALU.mult)
                        dve.drain().then_inc(s.tilde, 1)

                    def pick(l):
                        dve.wait_ge(s.pairs, l + 2)
                        dve.copy_predicated(A[:], spread(c.all[:, LEVEL[l]].bitcast(U32), 1, H), four(4 + l % 2))\
                           .then_inc(s.picked, 1)

                    diffs(0)
                    dve.tensor_tensor(ke[:], spread(bT[:, :, P - 1], 2, P), bT[:], ALU.subtract).then_inc(s.e_in, 1)
                    for l in range(LEVELS):
                        if l + 1 < LEVELS:
                            diffs(l + 1)
                        tilde(l)
                        if l:
                            dve.drain()
                            pick(l - 1)
                    dve.wait_ge(s.q_kept, 1)
                    dve.wait_ge(s.e_out, 1)
                    dve.tensor_tensor(qe[:], qe[:], qT[:], ALU.mult)
                    dve.tensor_tensor(ke[:], ke[:], kT[:], ALU.mult)
                    dve.drain().then_inc(s.ee_done, 1)
                    pick(LEVELS - 1)
                    dve.wait_ge(s.ke_t, 1)
                    dve.tensor_copy(ktok[:], four(6)).then_inc(s.ktok_done, 1)
                    dve.wait_ge(s.o_ps, 1)
                    dve.tensor_copy(y[:], four(7))
                    dve.drain()
                    dve.tensor_tensor(sq[:], y[:], y[:], ALU.mult)
                    dve.drain()
                    dve.tensor_reduce(ss[:], sq[:], AX.X, ALU.add).then_inc(s.sqd, 1)
                    y2 = y[:].rearrange("p h d -> p (h d)")
                    dve.tensor_tensor(y2, y2, g[:], ALU.mult)
                    dve.wait_ge(s.silus, 1)
                    dve.drain()
                    dve.tensor_tensor(y2, y2, x[:, 3], ALU.mult)
                    dve.wait_ge(s.up_ps, 1)
                    for h in range(H):
                        dve.scalar_tensor_tensor(out=state[:, h], in0=state[:, h], scalar=dec[:, h:h + 1],
                                                 in1=big[:, 0, h * BD:(h + 1) * BD], op0=ALU.mult, op1=ALU.add)
                    dve.wait_ge(s.rs, 1)
                    dve.drain()
                    dve.tensor_tensor(y[:], y[:], spread(ss[:], 2, BD), ALU.mult).then_inc(s.y_done, 1)

                @block.tensor
                def _(pe):
                    pe.wait_ge(s.silus, 1)
                    for h in range(H):
                        m = pe.transpose(big[:, 0, h * P:(h + 1) * P], x[:, 0, h * BD:(h + 1) * BD], c.ident)
                    m.then_inc(s.turned_q, 1)
                    pe.wait_ge(s.f_done, 1)
                    for h in range(H):
                        m = pe.transpose(big[:, 1, h * P:(h + 1) * P], k[:, h * BD:(h + 1) * BD], c.ident)
                    m.then_inc(s.turned_k, 1)
                    pe.wait_ge(s.logf, 1)
                    for h in range(H):
                        m = pe.matmul(big[:, 2, h * P:(h + 1) * P], x[:, 1, h * BD:(h + 1) * BD], c.upto, start=True,
                                      stop=True)
                    m.then_inc(s.sums, 1)
                    pe.wait_ge(s.q_kept, 1)
                    pe.wait_ge(s.k_kept, 1)
                    for h in range(H):
                        m = pe.matmul(big[:, 3, h * P:(h + 1) * P], kT[:, h], qT[:, h], start=True, stop=True)
                    m.then_inc(s.pairs, 1)
                    for l in range(LEVELS):
                        pe.wait_ge(s.tilde, l + 1)
                        if l >= 2:
                            pe.wait_ge(s.picked, l - 1)
                        for h in range(H):
                            m = pe.matmul(big[:, 4 + l % 2, h * P:(h + 1) * P], E[:, l % 2, h], E[:, l % 2, h],
                                          start=True, stop=True)
                        m.then_inc(s.pairs, 1)
                    pe.wait_ge(s.ee_done, 1)
                    for h in range(H):
                        m = pe.transpose(big[:, 6, h * P:(h + 1) * P], ke[:, h], c.ident)
                    m.then_inc(s.ke_t, 1)
                    pe.wait_ge(s.picked, LEVELS)
                    for h in range(H):
                        v = x[:, 2, h * BD:(h + 1) * BD]
                        pe.matmul(big[:, 7, h * BD:(h + 1) * BD], qe[:, h], state[:, h], start=True, stop=False)
                        m = pe.matmul(big[:, 7, h * BD:(h + 1) * BD], A[:, h], v, start=False, stop=True)
                    m.then_inc(s.o_ps, 1)
                    pe.wait_ge(s.ktok_done, 1)
                    for h in range(H):
                        m = pe.matmul(big[:, 0, h * BD:(h + 1) * BD], ktok[:, h], x[:, 2, h * BD:(h + 1) * BD],
                                      start=True, stop=True)
                    m.then_inc(s.up_ps, 1)


def sparse_attention(nc, c, w, proj, mix, table, onehot):
    H, R, KEEP = 4, 128, float(TOPK)
    with ExitStack() as ctx:
        B = Buffers(nc, ctx, "ds")
        cT = B.sb("cT", [P, SEQ])
        ct = B.sb("ct", [P, TILES, R])
        ikT = B.sb("ikT", [IDX_DIM, SEQ])
        uk = B.sb("uk", [P, H, R])
        uv = B.sb("uv", [P, H, P])
        bias = B.sb("bias", [P, H, SKEW])
        big = B.ps("big", [P, 8, 512])
        with ExitStack() as early:
            E = Buffers(nc, early, "dp")
            g = E.sb("g", [P, R])
            ik = E.sb("ik", [P, TILES, IDX_DIM])
            sq = E.sb("sq", [P, TILES, R])
            ss = E.sb("ss", [P, TILES])
            rb = E.sb("rb", [BUCKETS, H])
            oh = E.sb("oh", [BUCKETS, TAB])
            tb = E.sb("tb", [H, TAB])
            load(nc, "ds_w", [(uk[:], w['w_uk_2'].rearrange("h d r -> d h r")),
                              (uv[:], w['w_uv_2'].rearrange("h r v -> r h v")), (g[:], row(w['kv_norm_g_2'])),
                              (ik[:], proj[:, E_IK:E_IK + IDX_DIM].rearrange("(t p) c -> p t c", p=P)),
                              (ct[:], proj[:, E_C:E_C + R].rearrange("(t p) c -> p t c", p=P)),
                              (rb[:], w['rel_bias_2']), (oh[:], onehot)])
            with step(nc, "squares rs normed turned kept biases bias_kept table_out bias_in ik_t ik_kept") as (block, s):

                @block.vector
                def _(dve):
                    dve.tensor_tensor(sq[:], ct[:], ct[:], ALU.mult)
                    dve.drain()
                    dve.tensor_reduce(ss[:], sq[:], AX.X, ALU.add).then_inc(s.squares, 1)
                    dve.tensor_tensor(ct[:], ct[:], spread(g[:], 1, TILES), ALU.mult)
                    dve.wait_ge(s.rs, 1)
                    dve.drain()
                    dve.tensor_tensor(ct[:], ct[:], spread(ss[:], 2, R), ALU.mult).then_inc(s.normed, 1)
                    dve.wait_ge(s.biases, 1)
                    dve.tensor_copy(tb[:].rearrange("h (a b) -> h a b", a=5), big[0:H, 0:5]).then_inc(s.bias_kept, 1)
                    dve.wait_ge(s.turned, 1)
                    dve.tensor_copy(cT[:].rearrange("p (a b) -> p a b", a=4), big[:, 0:4]).then_inc(s.kept, 1)
                    dve.wait_ge(s.ik_t, 1)
                    dve.tensor_copy(ikT[:].rearrange("p (a b) -> p a b", a=4), big[0:IDX_DIM, 4:8])\
                       .then_inc(s.ik_kept, 1)

                @block.scalar
                def _(act):
                    act.wait_ge(s.squares, 1)
                    rstd(act, c, ss[:], R).then_inc(s.rs, 1)

                @block.tensor
                def _(pe):
                    for k in range(5):
                        m = pe.matmul(big[0:H, k], rb[:], oh[:, k * 512:(k + 1) * 512], start=True, stop=True)
                    m.then_inc(s.biases, 1)
                    pe.wait_ge(s.bias_kept, 1)
                    pe.wait_ge(s.normed, 1)
                    for t in range(TILES):
                        m = pe.transpose(big[:, t // 4, (t % 4) * P:(t % 4 + 1) * P], ct[:, t], c.ident)
                    m.then_inc(s.turned, 1)
                    for t in range(TILES):
                        m = pe.transpose(big[0:IDX_DIM, 4 + t // 4, (t % 4) * P:(t % 4 + 1) * P], ik[:, t], c.ident)
                    m.then_inc(s.ik_t, 1)

                @block.sync
                def _(sp):
                    sp.wait_ge(s.bias_kept, 1)
                    sp.dma_start(table, tb[:]).then_inc(s.table_out, 16)
                    sp.wait_ge(s.table_out, 16)
                    sp.dma_start(bias[:], bass.AP(tensor=table.tensor, offset=0,
                                                  ap=[[1, P], [TAB, H], [1, SKEW]])).then_inc(s.bias_in, 16)
                    sp.wait_ge(s.bias_in, 16)

        FL = SKEW // 8
        with step(nc, "flipped copied") as (block, s):

            @block.tensor
            def _(pe):
                for n in range(8 * H):
                    if n >= 8:
                        pe.wait_ge(s.copied, n - 7)
                    pe.matmul(big[:, n % 8, 0:FL], c.all[:, FLIP], bias[:, n // 8, n % 8 * FL:(n % 8 + 1) * FL],
                              start=True, stop=True).then_inc(s.flipped, 1)

            @block.vector
            def _(dve):
                for n in range(8 * H):
                    dve.wait_ge(s.flipped, n + 1)
                    dve.tensor_copy(bias[:, n // 8, n % 8 * FL:(n % 8 + 1) * FL], big[:, n % 8, 0:FL])\
                       .then_inc(s.copied, 1)

        q = B.sb("q", [P, H * R])
        iq = B.sb("iq", [P, IDX_HEADS, IDX_DIM])
        iw = B.sb("iw", [P, 3, IDX_HEADS])
        gate = B.sb("gate", [P, H, P])
        qT = B.sb("qT", [P, H, P])
        ql = B.sb("ql", [P, H, P])
        iqT = B.sb("iqT", [IDX_DIM, IDX_HEADS, P])
        rel = B.sb("rel", [P, 2, 1024])
        score = B.sb("score", [P, SEQ])
        t1 = B.sb("t1", [P, SEQ])
        t2 = B.sb("t2", [P, SEQ])
        bm = B.sb("bm", [P, SEQ])
        L = B.sb("L", [P, SEQ])
        L2 = B.sb("L2", [P, SEQ])
        thr = B.sb("thr", [P, 4])
        mx = B.sb("mx", [P, H])
        den = B.sb("den", [P, H])
        pT = B.sb("pT", [P, 2, 4, P])
        oT = B.sb("oT", [P, H, P])
        y = B.sb("y", [P, H, P])
        for g_ in range(TILES // 4):
            W = (g_ + 1) * GROUP
            NG = g_ + 1
            PIECES = [(k, min(1024, W - k)) for k in range(0, W, 1024)]
            base = 4 * g_ * P
            with nc.Fori(0, 4) as j:
                with step(nc, "q_in iq_in iw_in g_in silus scaled q_turned q_kept ql_ps ql_done iq_ps iq_done "
                              "dots relus summed selected biased logits maxed exps turned kept weighed o_kept "
                              "o_ps y_done stored added") as (block, s):
                    tok = bass.ds(j * P + base, P)
                    Lh = (L, L2)

                    @block.sync
                    def _(sp):
                        sp.dma_start(q[:], proj[tok, E_Q:E_Q + H * R]).then_inc(s.q_in, 16)
                        sp.dma_start(iq[:].rearrange("p h d -> p (h d)"), proj[tok, E_IQ:E_IQ + IDX_HEADS * IDX_DIM])\
                          .then_inc(s.iq_in, 16)
                        sp.dma_start(iw[:, 0], proj[tok, E_IW:E_IW + IDX_HEADS]).then_inc(s.iw_in, 16)
                        sp.dma_start(gate[:].rearrange("p h d -> p (h d)"), proj[tok, E_G:E_G + H * P])\
                          .then_inc(s.g_in, 16)
                        sp.wait_ge(s.y_done, 1)
                        sp.dma_start(mix[tok, 0:512], y[:].rearrange("p h d -> p (h d)")).then_inc(s.stored, 16)
                        sp.wait_ge(s.stored, 16)

                    @block.gpsimd
                    def _(pool):
                        for h in range(H):
                            pool.wait_ge(s.selected, 1)
                            if h:
                                pool.wait_ge(s.added, h)
                            pool.tensor_tensor(bm[:, 0:W], t1[:, 0:W],
                                               bias[:, h, bass.ds((TILES - 1) * P - base - j * P, W)], ALU.add)\
                                .then_inc(s.biased, 1)

                    @block.scalar
                    def _(act):
                        act.wait_ge(s.g_in, 16)
                        act.activation(gate[:], gate[:], ACT.Silu).then_inc(s.silus, 1)
                        act.wait_ge(s.q_turned, 1)
                        act.activation(qT[:], big[:, 4].rearrange("p (h t) -> p h t", h=H), ACT.Copy)\
                           .then_inc(s.q_kept, 1)
                        act.wait_ge(s.ql_ps, 1)
                        act.activation(ql[:], big[:, 5].rearrange("p (h t) -> p h t", h=H), ACT.Copy,
                                       scale=P ** -0.5).then_inc(s.ql_done, 1)
                        n = 0
                        for h in range(IDX_HEADS):
                            for k, wd in PIECES:
                                act.wait_ge(s.dots, n + 1)
                                if n >= 2:
                                    act.wait_ge(s.summed, n - 1)
                                act.activation(rel[:, n % 2, 0:wd],
                                               big[:, 2 * (n % 2):2 * (n % 2) + wd // 512].rearrange("p a b -> p (a b)"),
                                               ACT.Relu).then_inc(s.relus, 1)
                                n += 1
                        for h in range(H):
                            act.wait_ge(s.maxed, h + 1)
                            act.activation(Lh[h % 2][:, 0:W], Lh[h % 2][:, 0:W], ACT.Exp, bias=mx[:, h:h + 1],
                                           accum_out=den[:, h:h + 1]).then_inc(s.exps, 1)

                    @block.vector
                    def _(dve):
                        dve.wait_ge(s.iw_in, 16)
                        dve.scalar_tensor_tensor(out=iw[:, 1], in0=iw[:, 0], scalar=-1.0, in1=iw[:, 0], op0=ALU.mult,
                                                 op1=ALU.max)
                        dve.tensor_scalar(iw[:, 2], iw[:, 0], 0.0, 2.0, ALU.is_ge, ALU.mult)
                        dve.drain()
                        dve.tensor_scalar(iw[:, 1], iw[:, 1], float(IDX_HEADS ** -0.5 * IDX_DIM ** -0.5), None, ALU.mult)
                        dve.tensor_scalar(iw[:, 2], iw[:, 2], -1.0, None, ALU.add)
                        dve.wait_ge(s.iq_in, 16)
                        dve.drain()
                        dve.tensor_tensor(iq[:], iq[:], spread(iw[:, 1], 2, IDX_DIM), ALU.mult).then_inc(s.scaled, 1)
                        dve.wait_ge(s.iq_ps, 1)
                        dve.tensor_copy(iqT[:].rearrange("p (a h) t -> p a (h t)", a=2), big[0:IDX_DIM, 6:8])\
                           .then_inc(s.iq_done, 1)
                        n = 0
                        for h in range(IDX_HEADS):
                            for k, wd in PIECES:
                                dve.wait_ge(s.relus, n + 1)
                                sg = iw[:, 2, h:h + 1]
                                if h:
                                    dve.drain()
                                    d = dve.scalar_tensor_tensor(out=score[:, k:k + wd], in0=rel[:, n % 2, 0:wd],
                                                                 scalar=sg, in1=score[:, k:k + wd], op0=ALU.mult,
                                                                 op1=ALU.add)
                                else:
                                    d = dve.tensor_scalar(score[:, k:k + wd], rel[:, n % 2, 0:wd], sg, None, ALU.mult)
                                d.then_inc(s.summed, 1)
                                n += 1
                        dve.drain()
                        window = c.all[:, bass.ds(CHUNKED0 + 3 * P - j * P, GROUP)]
                        dve.tensor_tensor(score[:, W - GROUP:W], score[:, W - GROUP:W], window, ALU.add)
                        thu = thr[:].bitcast(U32)
                        dve.drain()
                        dve.tensor_scalar(t1[:, 0:W], score[:, 0:W], 0.0, 0.0, ALU.is_ge, ALU.add,
                                          accum_out=thr[:, 2:3])
                        dve.memset(thu[:, 0:1], 0xFFFFFFFF)
                        dve.memset(thu[:, 1:2], 0)
                        dve.drain()
                        dve.tensor_scalar(thu[:, 3:4], thr[:, 2:3], KEEP, None, ALU.is_ge)
                        dve.drain()
                        dve.copy_predicated(thu[:, 0:1], thu[:, 3:4], thu[:, 1:2])
                        for bit in range(30, -1, -1):
                            dve.drain()
                            dve.tensor_scalar(thu[:, 1:2], thu[:, 0:1], 1 << bit, None, ALU.bitwise_xor)
                            dve.drain()
                            dve.tensor_scalar(t1[:, 0:W], score[:, 0:W], thr[:, 1:2], 0.0, ALU.is_ge, ALU.add,
                                              accum_out=thr[:, 2:3])
                            dve.drain()
                            dve.tensor_scalar(thu[:, 3:4], thr[:, 2:3], KEEP, None, ALU.is_ge)
                            dve.drain()
                            dve.copy_predicated(thu[:, 0:1], thu[:, 3:4], thu[:, 1:2])
                        dve.drain()
                        dve.tensor_scalar(t1[:, 0:W], score[:, 0:W], thr[:, 0:1], 0.0, ALU.is_gt, ALU.add,
                                          accum_out=thr[:, 2:3])
                        dve.tensor_scalar(t2[:, 0:W], score[:, 0:W], thr[:, 0:1], None, ALU.is_equal)
                        dve.drain()
                        dve.tensor_scalar(thr[:, 3:4], thr[:, 2:3], -1.0, KEEP, ALU.mult, ALU.add)
                        dve.tensor_tensor_scan(score[:, 0:W], t2[:, 0:W], t2[:, 0:W], 0.0, ALU.add, ALU.max)
                        dve.drain()
                        dve.scalar_tensor_tensor(out=t2[:, 0:W], in0=score[:, 0:W], scalar=thr[:, 3:4],
                                                 in1=t2[:, 0:W], op0=ALU.is_le, op1=ALU.mult)
                        dve.drain()
                        dve.scalar_tensor_tensor(out=t1[:, 0:W], in0=t1[:, 0:W], scalar=-1.0, in1=t2[:, 0:W],
                                                 op0=ALU.add, op1=ALU.add)
                        dve.drain()
                        dve.tensor_scalar(t1[:, 0:W], t1[:, 0:W], -NEG, None, ALU.mult)
                        dve.drain()
                        dve.tensor_tensor(t1[:, W - GROUP:W], t1[:, W - GROUP:W], window, ALU.add)
                        dve.drain().then_inc(s.selected, 1)

                        def keep(h):
                            for k in range(NG):
                                n = h * NG + k
                                dve.wait_ge(s.turned, n + 1)
                                if n >= 2:
                                    dve.wait_ge(s.weighed, n - 1)
                                dve.tensor_copy(pT[:, n % 2], big[:, 4 + n % 2].rearrange("p (b t) -> p b t", b=4))\
                                   .then_inc(s.kept, 1)

                        for h in range(H):
                            dve.wait_ge(s.biased, h + 1)
                            dve.wait_ge(s.logits, h + 1)
                            if h >= 2:
                                dve.wait_ge(s.turned, (h - 1) * NG)
                            dve.tensor_tensor_reduce(Lh[h % 2][:, 0:W], big[:, 0:NG].rearrange("p a b -> p (a b)"),
                                                     bm[:, 0:W], 1.0, 4 * NEG, ALU.add, ALU.max, mx[:, h:h + 1])\
                               .then_inc(s.added, 1)
                            dve.drain()
                            dve.tensor_scalar(mx[:, h:h + 1], mx[:, h:h + 1], -1.0, None, ALU.mult)\
                               .then_inc(s.maxed, 1)
                            if h:
                                keep(h - 1)
                        keep(H - 1)
                        dve.wait_ge(s.exps, H)
                        dve.reciprocal(den[:], den[:])
                        dve.wait_ge(s.silus, 1)
                        dve.wait_ge(s.weighed, H * NG)
                        dve.tensor_copy(oT[:], big[:, 6].rearrange("p (h t) -> p h t", h=H)).then_inc(s.o_kept, 1)
                        dve.drain()
                        dve.tensor_tensor(gate[:], gate[:], spread(den[:], 2, P), ALU.mult)
                        dve.drain()
                        dve.wait_ge(s.o_ps, 1)
                        dve.tensor_tensor(y[:], big[:, 7].rearrange("p (h t) -> p h t", h=H), gate[:], ALU.mult)\
                           .then_inc(s.y_done, 1)

                    @block.tensor
                    def _(pe):
                        pe.wait_ge(s.q_in, 16)
                        for h in range(H):
                            m = pe.transpose(big[:, 4, h * P:(h + 1) * P], q[:, h * R:(h + 1) * R], c.ident)
                        m.then_inc(s.q_turned, 1)
                        pe.wait_ge(s.q_kept, 1)
                        for h in range(H):
                            m = pe.matmul(big[:, 5, h * P:(h + 1) * P], uk[:, h], qT[:, h], start=True, stop=True)
                        m.then_inc(s.ql_ps, 1)
                        pe.wait_ge(s.scaled, 1)
                        for h in range(IDX_HEADS):
                            m = pe.transpose(big[0:IDX_DIM, 6 + h // 4, (h % 4) * P:(h % 4 + 1) * P], iq[:, h], c.ident)
                        m.then_inc(s.iq_ps, 1)
                        pe.wait_ge(s.iq_done, 1)
                        n = 0
                        for h in range(IDX_HEADS):
                            for k, wd in PIECES:
                                if n >= 2:
                                    pe.wait_ge(s.relus, n - 1)
                                for b in range(wd // 512):
                                    m = pe.matmul(big[:, 2 * (n % 2) + b], iqT[:, h],
                                                  ikT[:, k + b * 512:k + (b + 1) * 512], start=True, stop=True)
                                m.then_inc(s.dots, 1)
                                n += 1
                        pe.wait_ge(s.relus, n)
                        pe.wait_ge(s.ql_done, 1)

                        def logits(h):
                            if h:
                                pe.wait_ge(s.added, h)
                            for k in range(NG):
                                m = pe.matmul(big[:, k], ql[:, h], cT[:, k * 512:(k + 1) * 512], start=True, stop=True)
                            m.then_inc(s.logits, 1)

                        def turn(n):
                            h, k = n // NG, n % NG
                            if n >= 2:
                                pe.wait_ge(s.kept, n - 1)
                            for b in range(4):
                                m = pe.transpose(big[:, 4 + n % 2, b * P:(b + 1) * P],
                                                 Lh[h % 2][:, (4 * k + b) * P:(4 * k + b + 1) * P], c.ident)
                            m.then_inc(s.turned, 1)

                        def weigh(n):
                            h, k = n // NG, n % NG
                            pe.wait_ge(s.kept, n + 1)
                            for b in range(4):
                                m = pe.matmul(big[:, 6, h * P:(h + 1) * P], ct[:, 4 * k + b], pT[:, n % 2, b],
                                              start=(k == 0 and b == 0), stop=(k == NG - 1 and b == 3))
                            m.then_inc(s.weighed, 1)

                        logits(0)
                        for h in range(H):
                            if h + 1 < H:
                                logits(h + 1)
                            pe.wait_ge(s.exps, h + 1)
                            turn(h * NG)
                            for k in range(1, NG):
                                turn(h * NG + k)
                                weigh(h * NG + k - 1)
                            weigh(h * NG + NG - 1)
                        pe.wait_ge(s.o_kept, 1)
                        for h in range(H):
                            m = pe.matmul(big[:, 7, h * P:(h + 1) * P], oT[:, h], uv[:, h], start=True, stop=True)
                        m.then_inc(s.o_ps, 1)


def program(nc, t, consts, onehot, out):
    w = {n: (v[0] if v.shape[0] == 1 else v) for n, v in t.items()}
    out = out[0]

    def scratch(name, shape):
        return nc.dram_tensor(name, shape, F32, kind="Internal").ap()

    proj1, mixed1 = scratch("proj1", [SEQ + PAD, COLS1]), scratch("mixed1", [SEQ, MIX1])
    x2 = scratch("x2", [SEQ, D_MODEL])
    proj2, mixed2 = scratch("proj2", [SEQ, COLS2]), scratch("mixed2", [SEQ, D_MODEL])
    table = scratch("table", [HEADS, TAB])
    with ExitStack() as ctx:
        c = load_constants(nc, ctx, consts)
        with ExitStack() as own:
            B = Buffers(nc, own, "first")
            hT = B.sb("hT", [P, KD, SEQ])
            zero_rows(nc, hT, proj1)
            norm_transpose(nc, c, w['x'], w['norm_g'], hT, "n1")
            gemm(nc, c, hT, w['w_in'], proj1, COLS1, "g1", PAD)
        sgu(nc, c, w, proj1, mixed1)
        memory_attention(nc, c, w, proj1, mixed1)
        fox(nc, c, w, proj1, mixed1)
        mlstm(nc, c, w, proj1, mixed1)
        rwkv(nc, c, w, proj1, mixed1)
        with ExitStack() as own:
            B = Buffers(nc, own, "second")
            hT = B.sb("hT", [P, KD, SEQ])
            project_out(nc, c, mixed1, w['w_out'], w['x'], x2, "po", turned_out=hT)
            gemm(nc, c, hT, w['w_in_2'], proj2, COLS2, "g2", 0)
        sparse_attention(nc, c, w, proj2, mixed2, table, onehot)
        hgrn(nc, c, w, proj2, mixed2)
        project_out(nc, c, mixed2, w['w_o_2'], x2, out, "pf", ln=(w['ln_g_2'], w['ln_b_2']))


INPUTS = """x mem norm_g w_in w_out sgu_norm_g sgu_w sgu_b fox_q_g fox_k_g fox_f_b mlstm_conv_w mlstm_conv_b
mlstm_i_b mlstm_f_b mlstm_out_g rwkv_mu rwkv_w0 rwkv_w2 rwkv_a0 rwkv_a2 rwkv_k_k rwkv_k_a rwkv_r_k rwkv_ln_g
mem_norm_g mem_w_kv mem_q_g mem_k_g w_in_2 w_uk_2 w_uv_2 kv_norm_g_2 rel_bias_2 lb_logits_2 hgrn_norm_g_2 w_o_2
ln_g_2 ln_b_2""".split()


def kernel(**inputs):
    import concourse.bacc as bacc
    from concourse.bass_utils import run_bass_kernel_spmd

    nc = bacc.Bacc("TRN2", target_bir_lowering=False, num_devices=1)
    arrays, views = {}, {}
    for n in INPUTS:
        a = np.ascontiguousarray(inputs[n])
        arrays[f"in_{n}"] = a
        views[n] = nc.dram_tensor(f"in_{n}", a.shape, F32, kind="ExternalInput").ap()
    made = {"consts": shape_constants(), "onehot": bucket_table()}
    for n, a in made.items():
        arrays[n] = a
        views[n] = nc.dram_tensor(n, a.shape, F32, kind="ExternalInput").ap()
    out = nc.dram_tensor("out", [1, SEQ, D_MODEL], F32, kind="ExternalOutput").ap()
    program(nc, {n: views[n] for n in INPUTS}, views["consts"], views["onehot"], out)
    r = run_bass_kernel_spmd(nc, [arrays], core_ids=[0])
    return r.results[0]["out"]
```

```python
from contextlib import ExitStack, contextmanager

import numpy as np

import concourse.bass as bass
from concourse import mybir

F32 = mybir.dt.float32
U32 = mybir.dt.uint32
I32 = mybir.dt.int32
U16 = mybir.dt.uint16
ALU = mybir.AluOpType
ACT = mybir.ActivationFunctionType
AX = mybir.AxisListType

P = 128
SEQ = 2048
TILES = SEQ // P
D_MODEL = 1024
KD = D_MODEL // P
HEADS = 4
HD = 64
GW = HEADS * HD
N_MEM = 256
RANK = 16
MIX1 = 5 * GW
EPS = 1e-6
LN_EPS = 1e-5
NEG = -1e30

A_U, A_V, A_Z = 0, 256, 512
B_Q, B_K, B_V, B_F, B_Z = 768, 1024, 1280, 1536, 1540
C_QK, C_V, C_I, C_F, C_O, C_Z = 1796, 2308, 2564, 2568, 2572, 2828
D_0 = 3084
D_R, D_WLO, D_K, D_V, D_ALO, D_Z = 0, 256, 272, 528, 784, 800
D_W = 1056
M_Q, M_Z = 4140, 4396
COLS1 = 4652
E_Q, E_C, E_IQ, E_IK, E_IW, E_G = 0, 512, 640, 1152, 1216, 1224
H_Q, H_F, H_I, H_G = 1736, 2248, 2760, 3272
COLS2 = 3784
IDX_HEADS = 8
IDX_DIM = 64
TOPK = 256
BH = 4
BD = 128
PAD = 4
GROUP = 512
LEVELS = 7
BUCKETS = 32
TAB = 2560
SKEW = SEQ


def shape_constants():
    p = np.arange(P)[:, None]
    f = np.arange(P)[None, :]
    cols = [p == f, p <= f, p < f, p > f]
    for l in range(LEVELS):
        half = 1 << l
        cols.append((p // (2 * half) == f // (2 * half)) & (p // half % 2 == 0) & (f // half % 2 == 1))
    cols.append(np.ones((P, P)))
    cols += [(p == h) & (f >= 0) for h in range(HEADS)]
    cols += [p == 2 * j + f // HD for j in range(2)]
    cols += [(p <= f) * 1.0 - (p < P // 2), (p < f) * 1.0 - (p < P // 2)]
    cols += [cols[4 + l].T for l in range(LEVELS)]
    cols += [p + f == P - 1]
    cols += [np.zeros((P, GROUP)), (f > p) * NEG, (f > p // 64 * 64 + 63) * NEG]
    return np.concatenate([c.astype(np.float32) for c in cols], axis=1)


IDENT, UPTO, BEFORE, AFTER = (slice(P * k, P * k + P) for k in range(4))
LEVEL = [slice(P * (4 + l), P * (5 + l)) for l in range(LEVELS)]
ONES = slice(P * 11, P * 12)
ROW = [slice(P * (12 + h), P * (13 + h)) for h in range(HEADS)]
PAIR = [slice(P * (16 + j), P * (17 + j)) for j in range(2)]
CENTRED, CENTRED_BEFORE = (slice(P * k, P * k + P) for k in (18, 19))
LEVEL_T = [slice(P * (20 + l), P * (21 + l)) for l in range(LEVELS)]
FLIP = slice(P * 27, P * 28)
CAUSAL0 = P * 28
CHUNKED = slice(CAUSAL0 + GROUP + P, CAUSAL0 + GROUP + 2 * P)
CONST_COLS = CAUSAL0 + GROUP + 2 * P


def bucket_table():
    rel = np.arange(TAB) - (SEQ - 1)
    nb, max_dist = BUCKETS // 2, 256
    exact = nb // 2
    n = np.abs(rel)
    nf = np.maximum(n, 1).astype(np.float32)
    large = exact + (np.log(nf / np.float32(exact)) / np.float32(np.log(max_dist / exact))
                     * np.float32(nb - exact)).astype(np.int32)
    bucket = np.where(rel > 0, nb, 0) + np.where(n < exact, n, np.minimum(large, nb - 1))
    return (np.arange(BUCKETS)[:, None] == bucket[None, :]).astype(np.float32)


@contextmanager
def step(nc, names):
    with ExitStack() as ctx:
        sems = {n: ctx.enter_context(nc.semaphore(n)) for n in names.split()}
        with nc.Block() as block:
            yield block, type("Signals", (), sems)
        for sem in sems.values():
            nc.sync.sem_clear(sem)
        nc.all_engine_barrier()


class Buffers:

    def __init__(self, nc, ctx, phase):
        self._nc, self._ctx, self._phase = nc, ctx, phase

    def sb(self, name, shape, dt=F32):
        t = self._ctx.enter_context(self._nc.sbuf_tensor(f"{self._phase}_{name}", shape, dt))
        return t

    def ps(self, name, shape):
        t = self._ctx.enter_context(self._nc.psum_tensor(f"{self._phase}_{name}", shape, F32))
        return t


def together(engine, name, branches):
    at = []
    for n, branch in enumerate(branches):
        if name in branch:
            steps = branch[name](engine)
            at.append([next(steps), n, steps])
    while at:
        first = min(at, key=lambda b: (b[0], b[1]))
        place = next(first[2], None)
        assert place is None or place >= first[0], (name, first, place)
        if place is None:
            at.remove(first)
        else:
            first[0] = place




def spread(ap, axis, n):
    shape = list(ap.shape)
    v = ap.unsqueeze(axis)
    shape.insert(axis, n)
    return v.broadcast_to(shape)


def row(ap, n=P):
    return ap.partition_broadcast(n)


def load(nc, name, pairs):
    with step(nc, "arrived") as (block, s):
        arrived = s.arrived

        @block.sync
        def _(sp):
            for dst, src in pairs:
                sp.dma_start(dst, src, allow_slow_non_contiguous=True).then_inc(arrived, 16)
            sp.wait_ge(arrived, 16 * len(pairs))


def gemm(nc, c, hT, w, out, cols, name, pad):
    w_v = w.rearrange("(k p) n -> p k n", p=P)
    with ExitStack() as ctx:
        B = Buffers(nc, ctx, name)
        wt = B.sb("w", [P, 2, KD, 512])
        stage = B.sb("stage", [P, 4, 512])
        acc = B.ps("acc", [P, 4, 512])

        def group(n0s, width):
            with step(nc, "w_in0 w_in1 product act_copied dve_copied stored0 stored1 stored2 stored3") as (block, s):
                mm, act_cp, dve_cp = s.product, s.act_copied, s.dve_copied
                w_in = (s.w_in0, s.w_in1)
                stored = (s.stored0, s.stored1, s.stored2, s.stored3)

                @block.sync
                def _(sp):
                    for j, n0 in enumerate(n0s):
                        for k in range(KD):
                            sp.dma_start(wt[:, j, k, 0:width], w_v[:, k, bass.ds(n0, width)]).then_inc(w_in[j], 16)
                    for j, n0 in enumerate(n0s):
                        for t in range(TILES):
                            m = j * TILES + t
                            sp.wait_ge(dve_cp if m % 2 else act_cp, m // 2 + 1)
                            sp.dma_start(out[pad + t * P:pad + (t + 1) * P, bass.ds(n0, width)],
                                         stage[:, m % 4, 0:width]).then_inc(stored[m % 4], 16)
                    for slot in range(4):
                        sp.wait_ge(stored[slot], 16 * TILES * len(n0s) // 4)

                @block.tensor
                def _(pe):
                    for j in range(len(n0s)):
                        for t in range(TILES):
                            m = j * TILES + t
                            if m >= 4:
                                pe.wait_ge(dve_cp if m % 2 else act_cp, (m - 4) // 2 + 1)
                            if t == 0:
                                pe.wait_ge(w_in[j], 16 * KD)
                            for k in range(KD):
                                mm_ = pe.matmul(acc[:, m % 4, 0:width], hT[:, k, t * P:(t + 1) * P],
                                                wt[:, j, k, 0:width], start=(k == 0), stop=(k == KD - 1))
                            mm_.then_inc(mm, 1)

                def copies(eng, op, parity, done):
                    for m in range(parity, TILES * len(n0s), 2):
                        eng.wait_ge(mm, m + 1)
                        if m >= 4:
                            eng.wait_ge(stored[m % 4], 16 * (m // 4))
                        op(stage[:, m % 4, 0:width], acc[:, m % 4, 0:width]).then_inc(done, 1)

                @block.scalar
                def _(act):
                    copies(act, lambda o, i: act.activation(o, i, ACT.Copy), 0, act_cp)

                @block.vector
                def _(dve):
                    copies(dve, dve.tensor_copy, 1, dve_cp)

        pairs = cols // 1024
        with nc.Fori(0, pairs) as g:
            group([g * 1024, g * 1024 + 512], 512)
        n = pairs * 1024
        while n < cols:
            group([n], min(512, cols - n))
            n += 512


def norm_transpose(nc, c, x, gain, hT, name, tiles=TILES):
    U = min(4, tiles)
    with ExitStack() as ctx:
        B = Buffers(nc, ctx, name)
        xt = B.sb("xt", [P, U, D_MODEL])
        sq = B.sb("sq", [P, U, D_MODEL])
        ss = B.sb("ss", [P, U])
        g = B.sb("g", [P, KD])
        tp = B.ps("tp", [P, 4, KD // 2, P])
        load(nc, f"{name}_g", [(g[:], gain.rearrange("(k p) -> p k", p=P))])
        with nc.Fori(0, tiles // U) as i:
            with step(nc, "x_in rs normed turned copied") as (block, s):
                x_in, rs, xn, tr, cp = s.x_in, s.rs, s.normed, s.turned, s.copied

                @block.sync
                def _(sp):
                    for u in range(U):
                        sp.dma_start(xt[:, u], x[bass.ds(i * (U * P) + u * P, P), :]).then_inc(x_in, 16)

                @block.scalar
                def _(act):
                    act.wait_ge(x_in, 16 * U)
                    for u in range(U):
                        act.activation(sq[:, u], xt[:, u], ACT.Square, accum_out=ss[:, u:u + 1])
                    act.drain()
                    act.activation(ss[:], ss[:], ACT.Ln, scale=1.0 / D_MODEL, bias=c.eps[:, 0:1])
                    act.drain()
                    act.activation(ss[:], ss[:], ACT.Exp, scale=-0.5).then_inc(rs, 1)

                @block.vector
                def _(dve):
                    dve.wait_ge(rs, 1)
                    for u in range(U):
                        dve.tensor_scalar(xt[:, u], xt[:, u], ss[:, u:u + 1], None, ALU.mult).then_inc(xn, 1)
                    for v in range(2 * U):
                        u, half = v // 2, v % 2
                        dve.wait_ge(tr, v + 1)
                        dve.tensor_tensor(hT[:, 4 * half:4 * half + 4, bass.ds(i * (U * P) + u * P, P)],
                                          tp[:, v % 4], spread(g[:, 4 * half:4 * half + 4], 2, P),
                                          ALU.mult).then_inc(cp, 1)

                @block.tensor
                def _(pe):
                    for v in range(2 * U):
                        u, half = v // 2, v % 2
                        pe.wait_ge(xn, u + 1)
                        if v >= 4:
                            pe.wait_ge(cp, v - 3)
                        for k in range(4):
                            kk = 4 * half + k
                            t = pe.transpose(tp[:, v % 4, k], xt[:, u, kk * P:(kk + 1) * P], c.ident)
                        t.then_inc(tr, 1)


class Constants:
    pass


def load_constants(nc, ctx, consts):
    c = Constants()
    t = ctx.enter_context(nc.sbuf_tensor("consts_sb", [P, CONST_COLS], F32))
    e = ctx.enter_context(nc.sbuf_tensor("eps_sb", [P, 2], F32))
    c.all, c.eps = t, e
    c.ident, c.upto, c.before, c.after, c.ones = (t[:, k] for k in (IDENT, UPTO, BEFORE, AFTER, ONES))
    with step(nc, "const_in eps_set") as (block, s):

        @block.sync
        def _(sp):
            sp.dma_start(t[:], consts).then_inc(s.const_in, 16)
            sp.wait_ge(s.const_in, 16)

        @block.vector
        def _(dve):
            dve.memset(e[:, 0:1], EPS).then_inc(s.eps_set, 1)
            dve.memset(e[:, 1:2], LN_EPS).then_inc(s.eps_set, 1)
            dve.wait_ge(s.eps_set, 2)
    return c


def tokens(ap, i, n, c0, c1, pad=0):
    return ap[bass.ds(i * P + pad, n * P), c0:c1].rearrange("(u p) c -> p u c", p=P)


def rstd(act, c, ss, width):
    act.drain()
    act.activation(ss, ss, ACT.Ln, scale=1.0 / width, bias=c.eps[:, 0:1])
    act.drain()
    return act.activation(ss, ss, ACT.Exp, scale=-0.5)


def sgu(nc, c, w, proj, mixed):
    U = 4
    with ExitStack() as ctx:
        B = Buffers(nc, ctx, "sgu")
        wt = B.sb("wt", [P, HEADS, P])
        wT = B.sb("wT", [P, HEADS, P])
        b = B.sb("b", [P, HEADS])
        g = B.sb("g", [P, GW])
        x = B.sb("x", [P, U, 3 * GW])
        sq = B.sb("sq", [P, U, GW])
        ss = B.sb("ss", [P, U * HEADS])
        tp = B.ps("tp", [P, HEADS, P])
        mx = B.ps("mx", [P, HEADS, U * HD])
        load(nc, "sgu_w", [(wt[:], w['sgu_w'].rearrange("g t s -> t g s")),
                           (b[:], w['sgu_b'].rearrange("g t -> t g")), (g[:], row(w['sgu_norm_g']))])
        with step(nc, "turned masked") as (block, s):

            @block.tensor
            def _(pe):
                for h in range(HEADS):
                    t = pe.transpose(tp[:, h], wt[:, h], c.ident)
                t.then_inc(s.turned, 1)

            @block.vector
            def _(dve):
                dve.wait_ge(s.turned, 1)
                dve.tensor_tensor(wT[:], tp[:], spread(c.upto, 1, HEADS), ALU.mult).then_inc(s.masked, 1)

        with nc.Fori(0, TILES // U) as i:
            with step(nc, "x_in gelus squares rs normed mixes y_done silus stored") as (block, s):

                @block.sync
                def _(sp):
                    sp.dma_start(x[:], tokens(proj, i * U, U, A_U, A_U + 3 * GW, PAD)).then_inc(s.x_in, 16)
                    sp.wait_ge(s.y_done, 1)
                    sp.dma_start(tokens(mixed, i * U, U, 0, GW), x[:, :, 0:GW]).then_inc(s.stored, 16)
                    sp.wait_ge(s.stored, 16)

                @block.scalar
                def _(act):
                    act.wait_ge(s.x_in, 16)
                    act.activation(x[:, :, 0:2 * GW], x[:, :, 0:2 * GW], ACT.Gelu_apprx_tanh).then_inc(s.gelus, 1)
                    act.activation(x[:, :, 2 * GW:], x[:, :, 2 * GW:], ACT.Silu).then_inc(s.silus, 1)
                    act.wait_ge(s.squares, 1)
                    rstd(act, c, ss[:], HD).then_inc(s.rs, 1)

                @block.vector
                def _(dve):
                    u, v, z = (x[:, :, k * GW:(k + 1) * GW] for k in range(3))
                    vh = v.rearrange("p u (h d) -> p u h d", h=HEADS)
                    dve.wait_ge(s.gelus, 1)
                    dve.tensor_tensor(sq[:], v, v, ALU.mult)
                    dve.drain()
                    dve.tensor_reduce(ss[:], sq[:].rearrange("p u (h d) -> p (u h) d", h=HEADS), AX.X,
                                      ALU.add).then_inc(s.squares, 1)
                    dve.tensor_tensor(v, v, spread(g[:], 1, U), ALU.mult)
                    dve.wait_ge(s.rs, 1)
                    dve.drain()
                    dve.tensor_tensor(vh, vh, spread(ss[:].rearrange("p (u h) -> p u h", u=U), 3, HD),
                                      ALU.mult).then_inc(s.normed, 1)
                    dve.wait_ge(s.mixes, 1)
                    for h in range(HEADS):
                        cols = slice(h * HD, (h + 1) * HD)
                        dve.scalar_tensor_tensor(out=u[:, :, cols],
                                                 in0=mx[:, h].rearrange("p (u d) -> p u d", u=U),
                                                 scalar=b[:, h:h + 1], in1=u[:, :, cols], op0=ALU.add, op1=ALU.mult)
                    dve.wait_ge(s.silus, 1)
                    dve.drain()
                    dve.tensor_tensor(u, u, z, ALU.mult).then_inc(s.y_done, 1)

                @block.tensor
                def _(pe):
                    v = x[:, :, GW:2 * GW].rearrange("p u (h d) -> p h u d", h=HEADS)
                    pe.wait_ge(s.normed, 1)
                    for h in range(HEADS):
                        m = pe.matmul(mx[:, h].rearrange("p (u d) -> p u d", u=U), wT[:, h], v[:, h],
                                      start=True, stop=True)
                    m.then_inc(s.mixes, 1)


def memory_attention(nc, c, w, proj, mixed):
    MT = N_MEM // P
    with ExitStack() as ctx:
        B = Buffers(nc, ctx, "mem")
        kT = B.sb("kT", [HD, HEADS, N_MEM])
        vm = B.sb("vm", [P, MT, GW])
        gq = B.sb("gq", [P, HD])
        gk = B.sb("gk", [P, HD])
        load(nc, "mem_g", [(gq[:], row(w['mem_q_g'])), (gk[:], row(w['mem_k_g']))])
        with ExitStack() as early:
            E = Buffers(nc, early, "memkv")
            hT = E.sb("hT", [P, KD, N_MEM])
            norm_transpose(nc, c, w['mem'], w['mem_norm_g'], hT, "nm", tiles=MT)
            wk = E.sb("wk", [P, KD, 2 * GW])
            k = E.sb("k", [P, MT, HEADS, HD])
            sq = E.sb("sq", [P, MT, HEADS, HD])
            ss = E.sb("ss", [P, MT, HEADS])
            acc = E.ps("acc", [P, MT, 2 * GW])
            tp = E.ps("tp", [P, HEADS, N_MEM])
            with step(nc, "w_in prods split squares rs normed turned kept") as (block, s):

                @block.sync
                def _(sp):
                    sp.dma_start(wk[:], w['mem_w_kv'].rearrange("(k p) n -> p k n", p=P)).then_inc(s.w_in, 16)

                @block.tensor
                def _(pe):
                    pe.wait_ge(s.w_in, 16)
                    for t in range(MT):
                        for j in range(KD):
                            m = pe.matmul(acc[:, t], hT[:, j, t * P:(t + 1) * P], wk[:, j], start=(j == 0),
                                          stop=(j == KD - 1))
                    m.then_inc(s.prods, 1)
                    pe.wait_ge(s.normed, 1)
                    for t in range(MT):
                        for h in range(HEADS):
                            m = pe.transpose(tp[0:HD, h, t * P:(t + 1) * P], k[:, t, h], c.ident)
                    m.then_inc(s.turned, 1)

                @block.scalar
                def _(act):
                    act.wait_ge(s.squares, 1)
                    rstd(act, c, ss[:], HD).then_inc(s.rs, 1)

                @block.vector
                def _(dve):
                    dve.wait_ge(s.prods, 1)
                    dve.tensor_copy(k[:], acc[:, :, 0:GW].rearrange("p t (h d) -> p t h d", h=HEADS))
                    dve.tensor_copy(vm[:], acc[:, :, GW:2 * GW])
                    dve.drain()
                    dve.tensor_tensor(sq[:], k[:], k[:], ALU.mult)
                    dve.drain()
                    dve.tensor_reduce(ss[:], sq[:], AX.X, ALU.add).then_inc(s.squares, 1)
                    dve.wait_ge(s.rs, 1)
                    dve.tensor_tensor(k[:], k[:], spread(ss[:], 3, HD), ALU.mult)
                    dve.drain()
                    kk = k[:].rearrange("p t h d -> p (t h) d")
                    dve.tensor_tensor(kk, kk, spread(gk[:], 1, MT * HEADS), ALU.mult).then_inc(s.normed, 1)
                    dve.wait_ge(s.turned, 1)
                    dve.tensor_copy(kT[:], tp[0:HD]).then_inc(s.kept, 1)

        U = 2
        qz = B.sb("qz", [P, U, 2 * GW])
        sq = B.sb("sqq", [P, U, GW])
        ss = B.sb("ss", [P, U * HEADS])
        qT = B.sb("qT", [HD, U, HEADS, P])
        pr = B.sb("pr", [P, HEADS, N_MEM])
        mx = B.sb("mx", [P, U, HEADS])
        den = B.sb("den", [P, U, HEADS])
        pT = B.sb("pT", [P, HEADS, MT, P])
        tq = B.ps("tq", [P, HEADS, P])
        sc = B.ps("sc", [P, HEADS, N_MEM])
        tp = B.ps("tp", [P, HEADS, MT, P])
        o = B.ps("o", [P, HEADS, HD])
        with nc.Fori(0, TILES // U) as i:
            with step(nc, "x_in squares rs normed q_turned q_kept scored maxed exps turned kept weighed "
                          "divided silus y_done stored") as (block, s):

                @block.sync
                def _(sp):
                    sp.dma_start(qz[:], tokens(proj, i * U, U, M_Q, M_Q + 2 * GW, PAD)).then_inc(s.x_in, 16)
                    sp.wait_ge(s.y_done, 1)
                    sp.dma_start(tokens(mixed, i * U, U, 4 * GW, 5 * GW), qz[:, :, 0:GW]).then_inc(s.stored, 16)
                    sp.wait_ge(s.stored, 16)

                @block.scalar
                def _(act):
                    act.wait_ge(s.x_in, 16)
                    act.activation(qz[:, :, GW:], qz[:, :, GW:], ACT.Silu).then_inc(s.silus, 1)
                    act.wait_ge(s.squares, 1)
                    rstd(act, c, ss[:], HD).then_inc(s.rs, 1)
                    for u in range(U):
                        act.wait_ge(s.maxed, u + 1)
                        if u:
                            act.wait_ge(s.turned, u)
                        for h in range(HEADS):
                            act.activation(pr[:, h], sc[:, h], ACT.Exp, bias=mx[:, u, h:h + 1],
                                           accum_out=den[:, u, h:h + 1]).then_inc(s.exps, 1)

                @block.vector
                def _(dve):
                    q, z = qz[:, :, 0:GW], qz[:, :, GW:]
                    q64 = q.rearrange("p u (h d) -> p u h d", h=HEADS)
                    dve.wait_ge(s.x_in, 16)
                    dve.tensor_tensor(sq[:], q, q, ALU.mult)
                    dve.drain()
                    dve.tensor_reduce(ss[:], sq[:].rearrange("p u (h d) -> p (u h) d", h=HEADS), AX.X,
                                      ALU.add).then_inc(s.squares, 1)
                    dve.wait_ge(s.rs, 1)
                    dve.tensor_tensor(q64, q64, spread(ss[:].rearrange("p (u h) -> p u h", u=U), 3, HD), ALU.mult)
                    dve.drain()
                    for u in range(U):
                        dve.scalar_tensor_tensor(out=q64[:, u], in0=q64[:, u], scalar=HD ** -0.5,
                                                 in1=spread(gq[:], 1, HEADS), op0=ALU.mult,
                                                 op1=ALU.mult).then_inc(s.normed, 1)
                    for u in range(U):
                        dve.wait_ge(s.q_turned, u + 1)
                        dve.tensor_copy(qT[:, u], tq[0:HD]).then_inc(s.q_kept, 1)
                        dve.wait_ge(s.scored, u + 1)
                        dve.tensor_reduce(mx[:, u], sc[:], AX.X, ALU.max)
                        dve.drain()
                        dve.tensor_scalar(mx[:, u], mx[:, u], -1.0, None, ALU.mult).then_inc(s.maxed, 1)
                        dve.wait_ge(s.turned, u + 1)
                        dve.tensor_copy(pT[:], tp[:]).then_inc(s.kept, 1)
                        dve.reciprocal(den[:, u], den[:, u])
                        dve.wait_ge(s.weighed, u + 1)
                        if u == 0:
                            dve.wait_ge(s.silus, 1)
                        dve.drain()
                        dve.tensor_tensor(q64[:, u], o[:], spread(den[:, u], 2, HD), ALU.mult).then_inc(s.divided, 1)
                        dve.drain()
                        d = dve.tensor_tensor(q[:, u], q[:, u], z[:, u], ALU.mult)
                    d.then_inc(s.y_done, 1)

                @block.tensor
                def _(pe):
                    q = qz[:, :, 0:GW].rearrange("p u (h d) -> p u h d", h=HEADS)
                    for u in range(U):
                        pe.wait_ge(s.normed, U)
                        for h in range(HEADS):
                            m = pe.transpose(tq[0:HD, h], q[:, u, h], c.ident)
                        m.then_inc(s.q_turned, 1)
                        pe.wait_ge(s.q_kept, u + 1)
                        for h in range(HEADS):
                            m = pe.matmul(sc[:, h], qT[:, u, h], kT[:, h], start=True, stop=True)
                        m.then_inc(s.scored, 1)
                        pe.wait_ge(s.exps, HEADS * (u + 1))
                        for h in range(HEADS):
                            for t in range(MT):
                                m = pe.transpose(tp[:, h, t], pr[:, h, t * P:(t + 1) * P], c.ident)
                        m.then_inc(s.turned, 1)
                        pe.wait_ge(s.kept, u + 1)
                        if u:
                            pe.wait_ge(s.divided, u)
                        for h in range(HEADS):
                            for t in range(MT):
                                m = pe.matmul(o[:, h], pT[:, h, t], vm[:, t, h * HD:(h + 1) * HD],
                                              start=(t == 0), stop=(t == MT - 1))
                        m.then_inc(s.weighed, 1)


def zero_rows(nc, buf, proj):
    with step(nc, "zeroed stored") as (block, s):

        @block.vector
        def _(dve):
            dve.memset(buf[0:PAD, 0:3, :], 0.0).then_inc(s.zeroed, 1)

        @block.sync
        def _(sp):
            sp.wait_ge(s.zeroed, 1)
            for n0 in range(0, COLS1, SEQ):
                n = min(SEQ, COLS1 - n0)
                sp.dma_start(proj[0:PAD, n0:n0 + n], buf[0:PAD, n0 // SEQ, 0:n]).then_inc(s.stored, 16)
            sp.wait_ge(s.stored, 16 * 3)


FOX_SIGNALS = "z_in z_silus logits f_added f_maxed f_exps f_turned f_kept f_weighed fy_done f_stored "


def fox_and_rwkv(nc, c, w, proj, mixed):
    A = HD + 1
    with ExitStack() as ctx:
        B = Buffers(nc, ctx, "fox")
        qT = B.sb("qT", [A, HEADS, SEQ])
        kT = B.sb("kT", [A, HEADS, SEQ])
        v = B.sb("v", [P, TILES, GW])
        gq = B.sb("gq", [P, 2, HD])
        fb = B.sb("fb", [P, HEADS])
        carry = B.sb("carry", [1, HEADS])
        load(nc, "fox_g", [(gq[:, 0], row(w['fox_q_g'])), (gq[:, 1], row(w['fox_k_g'])), (fb[:], row(w['fox_f_b'])),
                           (v[:], proj[PAD:, B_V:B_V + GW].rearrange("(t p) c -> p t c", p=P))])
        with step(nc, "scaled cleared") as (block, s):

            @block.vector
            def _(dve):
                dve.tensor_scalar(gq[:, 0], gq[:, 0], HD ** -0.5, None, ALU.mult).then_inc(s.scaled, 1)
                dve.memset(carry[:], 0.0).then_inc(s.cleared, 1)

        with ExitStack() as early:
            E = Buffers(nc, early, "foxq")
            U = 2
            x = E.sb("x", [P, U, 2, HEADS, HD])
            f = E.sb("f", [P, U, HEADS])
            aug = E.sb("aug", [P, U, 2, HEADS, A])
            sq = E.sb("sq", [P, U, 2 * GW])
            ss = E.sb("ss", [P, U, 2, HEADS])
            cum = E.ps("cum", [P, U, HEADS])
            tot = E.ps("tot", [1, U, HEADS])
            tp = E.ps("tp", [P, 2, HEADS, P])
            with nc.Fori(0, TILES // U) as i:
                with step(nc, "x_in f_in squares rs logf sums carried aug_done turned q_kept k_kept biased") as (block, s):

                    @block.sync
                    def _(sp):
                        sp.dma_start(x[:].rearrange("p u a h d -> p u (a h d)"),
                                     tokens(proj, i * U, U, B_Q, B_Q + 2 * GW, PAD)).then_inc(s.x_in, 16)
                        sp.dma_start(f[:], tokens(proj, i * U, U, B_F, B_F + HEADS, PAD)).then_inc(s.f_in, 16)

                    @block.scalar
                    def _(act):
                        act.wait_ge(s.biased, 1)
                        act.activation(f[:], f[:], ACT.Exp, scale=-1.0)
                        act.drain()
                        act.activation(f[:], f[:], ACT.Ln, bias=c.ones[:, 0:1]).then_inc(s.logf, 1)
                        act.wait_ge(s.squares, 1)
                        rstd(act, c, ss[:], HD).then_inc(s.rs, 1)
                        for u in range(U):
                            act.wait_ge(s.turned, u + 1)
                            act.activation(qT[:, :, bass.ds((i * U + u) * P, P)], tp[0:A, 0],
                                           ACT.Copy).then_inc(s.q_kept, 1)

                    @block.vector
                    def _(dve):
                        dve.wait_ge(s.f_in, 16)
                        dve.tensor_tensor(f[:], f[:], spread(fb[:], 1, U), ALU.add).then_inc(s.biased, 1)
                        dve.wait_ge(s.x_in, 16)
                        x2 = x[:].rearrange("p u a h d -> p u (a h d)")
                        dve.tensor_tensor(sq[:], x2, x2, ALU.mult)
                        dve.memset(aug[:, :, 0, :, HD:A], 1.0)
                        dve.drain()
                        dve.tensor_reduce(ss[:].rearrange("p u a h -> p (u a h)"),
                                          sq[:].rearrange("p u (x d) -> p (u x) d", d=HD), AX.X,
                                          ALU.add).then_inc(s.squares, 1)
                        for u in range(U):
                            for a in range(2):
                                dve.tensor_tensor(x[:, u, a], x[:, u, a], spread(gq[:, a], 1, HEADS), ALU.mult)
                        for u in range(U):
                            dve.wait_ge(s.sums, u + 1)
                            dve.tensor_copy(aug[:, u, 1, :, HD:A].rearrange("p h o -> p (h o)"), cum[:, u])
                            dve.tensor_tensor(carry[:], carry[:], tot[:, u], ALU.add)
                            dve.drain().then_inc(s.carried, 1)
                        dve.wait_ge(s.rs, 1)
                        dve.drain()
                        for u in range(U):
                            for a in range(2):
                                dve.tensor_tensor(aug[:, u, a, :, 0:HD], x[:, u, a], spread(ss[:, u, a], 2, HD),
                                                  ALU.mult)
                        dve.drain().then_inc(s.aug_done, 1)
                        for u in range(U):
                            dve.wait_ge(s.turned, u + 1)
                            dve.tensor_copy(kT[:, :, bass.ds((i * U + u) * P, P)], tp[0:A, 1]).then_inc(s.k_kept, 1)

                    @block.tensor
                    def _(pe):
                        pe.wait_ge(s.logf, 1)
                        for u in range(U):
                            if u:
                                pe.wait_ge(s.carried, u)
                            pe.matmul(cum[:, u], c.upto, f[:, u], start=True, stop=False)
                            pe.matmul(cum[:, u], c.ones[0:1], carry[:], start=False, stop=True)
                            pe.matmul(tot[:, u], c.ones[:, 0:1], f[:, u], start=True, stop=True).then_inc(s.sums, 1)
                        pe.wait_ge(s.aug_done, 1)
                        for u in range(U):
                            if u:
                                pe.wait_ge(s.q_kept, u)
                                pe.wait_ge(s.k_kept, u)
                            for a in range(2):
                                for h in range(HEADS):
                                    m = pe.transpose(tp[0:A, a, h], aug[:, u, a, h], c.ident)
                            m.then_inc(s.turned, 1)

        big = B.ps("big", [P, 8, 512])
        fb = fox_buffers(B, qT, kT, v, big)
        rb = rwkv_buffers(nc, B, w, big)
        for k in range(TILES + 1):
            names, branches = "", []
            if k >= 1:
                names += RWKV_BACK_SIGNALS
            if k < TILES:
                names += RWKV_FRONT_SIGNALS + FOX_SIGNALS
            with step(nc, names) as (block, s):
                if k < TILES:
                    branches.append(rwkv_front(c, rb, s, proj, k))
                if k >= 1:
                    branches.append(rwkv_back(c, rb, s, mixed, k - 1))
                if k < TILES:
                    branches.append(fox_attend(c, fb, s, proj, mixed, k))

                @block.sync
                def _(sp):
                    together(sp, "sync", branches)

                @block.scalar
                def _(act):
                    together(act, "scalar", branches)

                @block.vector
                def _(dve):
                    together(dve, "vector", branches)

                @block.tensor
                def _(pe):
                    together(pe, "tensor", branches)


def in_turn(banks, uses):
    n = len(banks)
    return {key: (banks[i % n], uses[i - n][1] if i >= n else None) for i, (key, over) in enumerate(uses)}


def fox_buffers(B, qT, kT, v, big):
    b = Constants()
    b.qT, b.kT, b.v, b.big = qT, kT, v, big
    b.z = B.sb("z", [P, GW])
    b.L = B.sb("L", [P, 2, SEQ])
    b.mx = B.sb("mx", [P, HEADS, 4])
    b.top = B.sb("top", [P, HEADS])
    b.den = B.sb("den", [P, HEADS])
    b.pT = B.sb("pT", [P, 2, 4, P])
    b.y = B.sb("y", [P, HEADS, HD])
    return b


def fox_attend(c, b, s, proj, mixed, k):
    W = (k + 1) * P
    L, mx, top, den, pT, z, y, big = b.L, b.mx, b.top, b.den, b.pT, b.z, b.y, b.big
    PIECES = [(x, min(512, W - x)) for x in range(0, W, 512)]
    NP = len(PIECES)
    o = big[:, 7, 0:GW].rearrange("p (h d) -> p h d", h=HEADS)
    N = 12.0
    at_logits = lambda h, p: (0.3 + 2 * h + 1.6 * p / NP) / N
    at_exp = lambda h: (2.1 + 2 * h) / N
    at_turn = lambda h, p: (2.3 + 2 * h + 1.6 * (p + 0.5) / NP) / N
    pitch = 1.6 / NP / N
    uses = []
    for h in range(HEADS + 1):
        for p in range(NP):
            if h < HEADS:
                uses.append((("L", h, p), (s.f_added, h * NP + p + 1)))
            if h:
                uses.append((("T", h - 1, p), (s.f_kept, (h - 1) * NP + p + 1)))
    turns = in_turn([5, 6], uses)

    def take(pe, *key):
        n, before = turns[key]
        if before:
            pe.wait_ge(*before)
        return n

    def sync(sp):
        yield 0.001
        sp.dma_start(z[:], proj[k * P + PAD:(k + 1) * P + PAD, B_Z:B_Z + GW]).then_inc(s.z_in, 16)
        yield 0.98
        sp.wait_ge(s.fy_done, 1)
        sp.dma_start(mixed[k * P:(k + 1) * P, GW:2 * GW], y[:].rearrange("p h d -> p (h d)")).then_inc(s.f_stored, 16)
        sp.wait_ge(s.f_stored, 16)

    def scalar(act):
        yield 5.5 / 80
        act.wait_ge(s.z_in, 16)
        act.activation(z[:], z[:], ACT.Silu).then_inc(s.z_silus, 1)
        for h in range(HEADS):
            if h:
                yield from keep(act, h - 1)
            yield at_exp(h)
            act.wait_ge(s.f_maxed, h + 1)
            act.activation(L[:, h % 2, 0:W], L[:, h % 2, 0:W], ACT.Exp, bias=top[:, h:h + 1],
                           accum_out=den[:, h:h + 1]).then_inc(s.f_exps, 1)
        yield from keep(act, HEADS - 1)

    def keep(act, h):
        for p, (x, wd) in enumerate(PIECES):
            n = h * NP + p
            yield at_turn(h, p) + 0.3 * pitch
            act.wait_ge(s.f_turned, n + 1)
            if n >= 2:
                act.wait_ge(s.f_weighed, n - 1)
            act.activation(pT[:, n % 2, 0:wd // P],
                           big[:, turns["T", h, p][0], 0:wd].rearrange("p (b t) -> p b t", t=P), ACT.Copy)\
               .then_inc(s.f_kept, 1)

    def vector(dve):
        for h in range(HEADS):
            for p, (x, wd) in enumerate(PIECES):
                yield at_logits(h, p) + 0.4 * pitch
                dve.wait_ge(s.logits, h * NP + p + 1)
                if p == 0 and h >= 2:
                    dve.wait_ge(s.f_turned, (h - 1) * NP)
                last = x + wd == W
                m0 = CAUSAL0 + (GROUP + P - wd if last else 0)
                dve.tensor_tensor_reduce(L[:, h % 2, x:x + wd], big[:, turns["L", h, p][0], 0:wd],
                                         c.all[:, m0:m0 + wd], 1.0, 4 * NEG, ALU.add, ALU.max,
                                         mx[:, h, p:p + 1]).then_inc(s.f_added, 1)
            yield at_exp(h)
            dve.drain()
            dve.tensor_reduce(top[:, h:h + 1], mx[:, h, 0:NP], AX.X, ALU.max)
            dve.drain()
            dve.tensor_scalar(top[:, h:h + 1], top[:, h:h + 1], -1.0, None, ALU.mult).then_inc(s.f_maxed, 1)
        yield 11 / N
        dve.wait_ge(s.f_exps, HEADS)
        dve.reciprocal(den[:], den[:])
        dve.wait_ge(s.f_weighed, HEADS * NP)
        dve.wait_ge(s.z_silus, 1)
        dve.drain()
        dve.tensor_tensor(y[:], o, spread(den[:], 2, HD), ALU.mult)
        dve.drain()
        y2 = y[:].rearrange("p h d -> p (h d)")
        dve.tensor_tensor(y2, y2, z[:], ALU.mult).then_inc(s.fy_done, 1)

    def tensor(pe):
        for h in range(HEADS + 1):
            for p in range(NP):
                if h < HEADS:
                    yield at_logits(h, p)
                    x, wd = PIECES[p]
                    n = take(pe, "L", h, p)
                    pe.matmul(big[:, n, 0:wd], b.qT[:, h, k * P:(k + 1) * P], b.kT[:, h, x:x + wd], start=True,
                              stop=True).then_inc(s.logits, 1)
                if h:
                    yield at_turn(h - 1, p)
                    if p == 0:
                        pe.wait_ge(s.f_exps, h)
                    turn(pe, h - 1, p)
                    if p:
                        weigh(pe, h - 1, p - 1)
            if h:
                yield at_turn(h - 1, NP - 1) + 0.35 * pitch
                weigh(pe, h - 1, NP - 1)

    def turn(pe, h, p):
        x, wd = PIECES[p]
        n = take(pe, "T", h, p)
        for t in range(wd // P):
            m = pe.transpose(big[:, n, t * P:(t + 1) * P], L[:, h % 2, x + t * P:x + (t + 1) * P], c.ident)
        m.then_inc(s.f_turned, 1)

    def weigh(pe, h, p):
        x, wd = PIECES[p]
        pe.wait_ge(s.f_kept, h * NP + p + 1)
        for t in range(wd // P):
            m = pe.matmul(o[:, h], pT[:, (h * NP + p) % 2, t], b.v[:, x // P + t, h * HD:(h + 1) * HD],
                          start=(p == 0 and t == 0), stop=(x + (t + 1) * P == W))
        m.then_inc(s.f_weighed, 1)

    return {"sync": sync, "scalar": scalar, "vector": vector, "tensor": tensor}


def mlstm(nc, c, w, proj, mixed):
    V1 = HD + 1
    with ExitStack() as ctx:
        B = Buffers(nc, ctx, "ml")
        cw = B.sb("cw", [P, 4, 2 * GW])
        cb = B.sb("cb", [P, 2 * GW])
        gb = B.sb("gb", [P, 2 * HEADS])
        og = B.sb("og", [P, GW])
        state = B.sb("state", [P, 2, 2 * V1])
        m_prev = B.sb("m_prev", [HEADS, 1])
        x = B.sb("x", [P, 4, 2 * GW])
        vx = B.sb("vx", [P, HEADS, V1])
        vin = B.sb("vin", [P, GW])
        gi = B.sb("gi", [P, 2 * HEADS])
        oz = B.sb("oz", [P, 2, GW])
        qk = B.sb("qk", [P, 2 * GW])
        a_tok = B.sb("a_tok", [P, HEADS])
        nb = B.sb("nb", [P, HEADS])
        a_row = B.sb("a_row", [HEADS, P])
        M = B.sb("M", [HEADS, P])
        nM = B.sb("nM", [HEADS, P])
        rows = B.sb("rows", [HEADS, 3, P])
        tok = B.sb("tok", [P, 3, HEADS])
        cd = B.sb("cd", [P, 2])
        qkT = B.sb("qkT", [P, 4, P])
        E = B.sb("E", [P, HEADS, P])
        kw = B.sb("kw", [P, HEADS, HD])
        num = B.sb("num", [P, HEADS, V1])
        h = B.sb("h", [P, HEADS, HD])
        sq = B.sb("sq", [P, HEADS, HD])
        ss = B.sb("ss", [P, HEADS])
        small = B.ps("small", [P, 512])
        p_nb, p_ar, p_nr = small[:, 0:4], small[0:HEADS, 64:192], small[0:HEADS, 192:320]
        p_tok, p_cd = small[:, 320:332].rearrange("p (a h) -> p a h", a=3), small[:, 340:342]
        p_qk = B.ps("p_qk", [P, 4, P])
        p_M = B.ps("p_M", [P, HEADS, P])
        both = B.ps("both", [P, 2, 512])
        p_s = both[:, :, 0:2 * P].rearrange("p r (j t) -> p j r t", j=2)
        p_int = both[:, :, 2 * P:2 * P + 2 * V1].rearrange("p r (j e) -> p j r e", j=2)
        p_in = B.ps("p_in", [P, HEADS, V1])
        p_up = B.ps("p_up", [P, 2, 2 * V1])
        load(nc, "ml_w", [(cw[:, j], row(w['mlstm_conv_w'][j])) for j in range(4)]
             + [(cb[:], row(w['mlstm_conv_b'])), (gb[:, 0:HEADS], row(w['mlstm_i_b'])),
                (gb[:, HEADS:], row(w['mlstm_f_b'])), (og[:], row(w['mlstm_out_g']))])
        with step(nc, "cleared") as (block, s):

            @block.vector
            def _(dve):
                dve.memset(state[:], 0.0).then_inc(s.cleared, 1)
                dve.memset(m_prev[:], 0.0).then_inc(s.cleared, 1)
                dve.memset(vx[:, :, HD:V1], 1.0).then_inc(s.cleared, 1)
                dve.wait_ge(s.cleared, 3)

        with nc.Fori(0, TILES) as i:
            with step(nc, "x_in v_in g_in oz_in conv_late conved qk_done gates_in logf sums a_done rows_t "
                          "M_done exps_r spread_M toks tok_done cd_ps Ein Eexp turned qkT_done scores "
                          "weighted num_ps kw_done up_ps sqd rs y_done stored tanhs") as (block, s):

                @block.sync
                def _(sp):
                    for j in range(4):
                        sp.dma_start(x[:, j], proj[bass.ds(i * P + (PAD - 3 + j), P), C_QK:C_QK + 2 * GW])\
                          .then_inc(s.x_in, 16)
                    sp.dma_start(gi[:], proj[bass.ds(i * P + PAD, P), C_I:C_I + 2 * HEADS]).then_inc(s.g_in, 16)
                    sp.dma_start(vin[:], proj[bass.ds(i * P + PAD, P), C_V:C_V + GW]).then_inc(s.v_in, 16)
                    sp.dma_start(oz[:].rearrange("p a c -> p (a c)"),
                                 proj[bass.ds(i * P + PAD, P), C_O:C_O + 2 * GW]).then_inc(s.oz_in, 16)
                    sp.wait_ge(s.y_done, 1)
                    sp.dma_start(mixed[bass.ds(i * P, P), 2 * GW:3 * GW], h[:].rearrange("p h d -> p (h d)"))\
                      .then_inc(s.stored, 16)
                    sp.wait_ge(s.stored, 16)

                @block.gpsimd
                def _(pool):
                    pool.wait_ge(s.x_in, 64)
                    pool.tensor_tensor(x[:, 2:4], x[:, 2:4], cw[:, 2:4], ALU.mult).then_inc(s.conv_late, 1)

                @block.scalar
                def _(act):
                    act.wait_ge(s.oz_in, 16)
                    act.activation(oz[:, 1], oz[:, 1], ACT.Silu)
                    act.activation(oz[:, 0], oz[:, 0], ACT.Tanh, scale=0.5).then_inc(s.tanhs, 1)
                    act.wait_ge(s.conved, 1)
                    act.activation(qk[:], qk[:], ACT.Silu).then_inc(s.qk_done, 1)
                    act.wait_ge(s.gates_in, 1)
                    act.activation(gi[:, HEADS:], gi[:, HEADS:], ACT.Exp, scale=-1.0)
                    act.drain()
                    act.activation(gi[:, HEADS:], gi[:, HEADS:], ACT.Ln, bias=c.ones[:, 0:1]).then_inc(s.logf, 1)
                    act.wait_ge(s.turned, 1)
                    act.activation(qkT[:, 0:2], p_qk[:, 0:2], ACT.Copy)
                    act.activation(qkT[:, 2:4], p_qk[:, 2:4], ACT.Copy, scale=HD ** -0.5).then_inc(s.qkT_done, 1)
                    act.wait_ge(s.M_done, 1)
                    act.activation(rows[:, 0], nM[:], ACT.Exp, bias=m_prev[:, 0:1])
                    act.activation(rows[:, 1], rows[:, 1], ACT.Exp)
                    act.activation(rows[:, 2], a_row[:], ACT.Exp, bias=nM[:, P - 1:P]).then_inc(s.exps_r, 1)
                    act.wait_ge(s.Ein, 1)
                    act.activation(E[:], E[:], ACT.Exp).then_inc(s.Eexp, 1)
                    act.wait_ge(s.sqd, 1)
                    rstd(act, c, ss[:], HD).then_inc(s.rs, 1)

                @block.vector
                def _(dve):
                    dve.wait_ge(s.g_in, 16)
                    dve.tensor_tensor(gi[:], gi[:], gb[:], ALU.add).then_inc(s.gates_in, 1)
                    dve.wait_ge(s.x_in, 64)
                    dve.tensor_tensor(x[:, 0:2], x[:, 0:2], cw[:, 0:2], ALU.mult)
                    dve.drain()
                    dve.tensor_tensor(qk[:], x[:, 0], x[:, 1], ALU.add)
                    dve.drain()
                    dve.tensor_tensor(qk[:], qk[:], cb[:], ALU.add)
                    dve.wait_ge(s.conv_late, 1)
                    dve.tensor_tensor(x[:, 2], x[:, 2], x[:, 3], ALU.add)
                    dve.drain()
                    dve.tensor_tensor(qk[:], qk[:], x[:, 2], ALU.add).then_inc(s.conved, 1)
                    dve.wait_ge(s.v_in, 16)
                    dve.tensor_copy(vx[:, :, 0:HD], vin[:].rearrange("p (h d) -> p h d", h=HEADS))
                    dve.wait_ge(s.sums, 1)
                    dve.tensor_copy(nb[:], p_nb)
                    dve.tensor_tensor(a_tok[:], gi[:, 0:HEADS], p_nb, ALU.add)
                    dve.drain().then_inc(s.a_done, 1)
                    dve.wait_ge(s.rows_t, 1)
                    dve.tensor_copy(a_row[:], p_ar)
                    dve.drain()
                    dve.tensor_tensor_scan(M[:], a_row[:], a_row[:], m_prev[:, 0:1], ALU.max, ALU.max)
                    dve.drain()
                    dve.tensor_scalar(nM[:], M[:], -1.0, None, ALU.mult)
                    dve.tensor_tensor(rows[:, 1], p_nr, M[:], ALU.subtract)
                    dve.drain().then_inc(s.M_done, 1)
                    dve.wait_ge(s.spread_M, 1)
                    for k in range(HEADS):
                        dve.tensor_scalar(E[:, k], p_M[:, k], a_tok[:, k:k + 1], 0.0, ALU.add, ALU.min)
                    dve.drain().then_inc(s.Ein, 1)
                    dve.wait_ge(s.toks, 1)
                    dve.tensor_scalar(m_prev[:], M[:, P - 1:P], p_nr[:, P - 1:P], None, ALU.subtract)
                    dve.tensor_copy(tok[:], p_tok)
                    dve.tensor_copy(cd[:], p_cd)
                    dve.drain()
                    dve.wait_ge(s.qk_done, 1)
                    k3 = qk[:, GW:].rearrange("p (h d) -> p h d", h=HEADS)
                    dve.tensor_tensor(kw[:], k3, spread(tok[:, 2], 2, HD), ALU.mult)
                    dve.drain()
                    dve.tensor_scalar(kw[:], kw[:], HD ** -0.5, None, ALU.mult).then_inc(s.kw_done, 1)
                    dve.wait_ge(s.Eexp, 1)
                    dve.tensor_tensor(E[:], E[:], spread(c.upto, 1, HEADS), ALU.mult)
                    dve.wait_ge(s.scores, 1)
                    dve.drain()
                    E4 = E[:].rearrange("p (j r) t -> p j r t", j=2)
                    dve.tensor_tensor(E4, E4, p_s, ALU.mult).then_inc(s.weighted, 1)
                    dve.wait_ge(s.num_ps, 1)
                    for j in range(2):
                        dve.tensor_tensor(num[:, 2 * j:2 * j + 2], p_int[:, j], spread(tok[:, 0, 2 * j:2 * j + 2], 2, V1),
                                          ALU.mult)
                    dve.drain()
                    dve.tensor_tensor(num[:], num[:], p_in[:], ALU.add)
                    dve.drain()
                    d = num[:, :, HD:V1].rearrange("p h o -> p (h o)")
                    dve.scalar_tensor_tensor(out=ss[:], in0=d, scalar=-1.0, in1=d, op0=ALU.mult, op1=ALU.max)
                    dve.drain()
                    dve.tensor_tensor(ss[:], ss[:], tok[:, 1], ALU.max)
                    dve.drain()
                    dve.reciprocal(ss[:], ss[:])
                    dve.wait_ge(s.tanhs, 1)
                    oh = oz[:, 0].rearrange("p (h d) -> p h d", h=HEADS)
                    dve.tensor_scalar(oh, oh, 0.5, 0.5, ALU.mult, ALU.add)
                    dve.drain()
                    dve.tensor_tensor(h[:], num[:, :, 0:HD], spread(ss[:], 2, HD), ALU.mult)
                    dve.drain()
                    dve.tensor_tensor(h[:], h[:], oh, ALU.mult)
                    dve.drain()
                    dve.tensor_tensor(sq[:], h[:], h[:], ALU.mult)
                    dve.drain()
                    dve.tensor_reduce(ss[:], sq[:], AX.X, ALU.add).then_inc(s.sqd, 1)
                    h2 = h[:].rearrange("p h d -> p (h d)")
                    dve.tensor_tensor(h2, h2, og[:], ALU.mult)
                    dve.drain()
                    dve.tensor_tensor(h2, h2, oz[:, 1], ALU.mult)
                    dve.wait_ge(s.up_ps, 1)
                    for j in range(2):
                        dve.scalar_tensor_tensor(out=state[:, j], in0=state[:, j], scalar=cd[:, j:j + 1],
                                                 in1=p_up[:, j], op0=ALU.mult, op1=ALU.add)
                    dve.wait_ge(s.rs, 1)
                    dve.drain()
                    dve.tensor_tensor(h[:], h[:], spread(ss[:], 2, HD), ALU.mult).then_inc(s.y_done, 1)

                @block.tensor
                def _(pe):
                    pe.wait_ge(s.logf, 1)
                    pe.matmul(p_nb, c.upto, gi[:, HEADS:], start=True, stop=True).then_inc(s.sums, 1)
                    pe.wait_ge(s.a_done, 1)
                    pe.transpose(p_ar, a_tok[:], c.ident)
                    pe.transpose(p_nr, nb[:], c.ident).then_inc(s.rows_t, 1)
                    pe.wait_ge(s.qk_done, 1)
                    for j in range(4):
                        m = pe.transpose(p_qk[:, j], qk[:, j * P:(j + 1) * P], c.ident)
                    m.then_inc(s.turned, 1)
                    pe.wait_ge(s.M_done, 1)
                    for k in range(HEADS):
                        m = pe.matmul(p_M[:, k], c.all[0:HEADS, ROW[k]], nM[:], start=True, stop=True)
                    m.then_inc(s.spread_M, 1)
                    pe.wait_ge(s.exps_r, 1)
                    for k in range(3):
                        pe.transpose(p_tok[:, k], rows[:, k], c.ident[0:HEADS, 0:HEADS])
                    for j in range(2):
                        m = pe.matmul(p_cd[:, j:j + 1], c.all[0:HEADS, PAIR[j]], rows[:, 0, P - 1:P], start=True,
                                      stop=True)
                    m.then_inc(s.toks, 1)
                    pe.wait_ge(s.qkT_done, 1)
                    for k in range(HEADS):
                        off, j = HD * (k % 2), k // 2
                        m = pe.matmul(p_s[:, j, k % 2], qkT[off:off + HD, 2 + j], qkT[off:off + HD, j], start=True, stop=True)
                    for k in range(HEADS):
                        off, j = HD * (k % 2), k // 2
                        m = pe.matmul(p_int[:, j, k % 2], qkT[off:off + HD, j],
                                  state[off:off + HD, j, (k % 2) * V1:(k % 2 + 1) * V1], start=True, stop=True)
                    m.then_inc(s.scores, 1)
                    pe.wait_ge(s.weighted, 1)
                    for k in range(HEADS):
                        m = pe.matmul(p_in[:, k], E[:, k], vx[:, k], start=True, stop=True)
                    m.then_inc(s.num_ps, 1)
                    pe.wait_ge(s.kw_done, 1)
                    for j in range(2):
                        m = pe.matmul(p_up[:, j], kw[:, 2 * j:2 * j + 2].rearrange("p h d -> p (h d)"),
                                      vx[:, 2 * j:2 * j + 2].rearrange("p h d -> p (h d)"), start=True, stop=True)
                    m.then_inc(s.up_ps, 1)


RWKV_FRONT_SIGNALS = ("rx_in rp_in shifted lows r_silus low_ps low_kept wa_ps wa_in tanhs la_done cums exps kksq norms "
                      "tilde turned_a turned_b kept_a kept_b grams g_done x_set p1 p1c dx dxc ")
RWKV_BACK_SIGNALS = "s0_done r_ps r_done u_ps u_done ry_ps ry_kept st_ps st_done rsqd rrs ry_done r_stored "


def rwkv_buffers(nc, B, w, big):
    b = Constants()
    b.big = big
    b.mu = B.sb("mu", [P, D_W])
    b.par = B.sb("par", [P, 6, GW])
    b.lo2 = B.sb("lo2", [RANK, 2, GW])
    b.state = B.sb("state", [P, 2, HD])
    b.x = B.sb("x", [P, 2, D_W])
    b.tl = B.sb("tl", [P, 2, 4, GW])
    b.XT4 = B.sb("XT4", [P, 2, 2, 4, P])
    b.G = B.sb("G", [P, 2, 2, HEADS, 2, P])
    b.XT = B.sb("XT", [P, 2, HEADS, P])
    b.em = B.sb("em", [P, 2, 2, 2])
    b.bon = B.sb("bon", [P, 2, HEADS])
    b.pv = B.sb("pv", [P, D_W])
    b.loT = B.sb("loT", [RANK, 2, P])
    b.wa = B.sb("wa", [P, 2, GW])
    b.kk = B.sb("kk", [P, HEADS, HD])
    b.kn = B.sb("kn", [P, GW])
    b.sq = B.sb("rsq", [P, HEADS, HD])
    b.ss = B.sb("rss", [P, HEADS])
    b.ex = B.sb("ex", [P, 3, GW])
    b.X = B.sb("X", [P, HEADS, P])
    b.Pm = B.sb("Pm", [P, HEADS, P])
    b.R = B.sb("R", [P, HEADS, HD])
    b.U = B.sb("U", [P, HEADS, HD])
    b.S0 = B.sb("S0", [P, 2, HD])
    b.y = B.sb("ry", [P, HEADS, HD])
    b.sqb = B.sb("rsqb", [P, HEADS, HD])
    b.ssb = B.sb("rssb", [P, HEADS])
    load(nc, "rw_w", [(b.mu[:], row(w['rwkv_mu'])), (b.lo2[:, 0], w['rwkv_w2']), (b.lo2[:, 1], w['rwkv_a2'])]
         + [(b.par[:, k], row(w[n])) for k, n in enumerate(['rwkv_w0', 'rwkv_a0', 'rwkv_k_k', 'rwkv_k_a'])]
         + [(b.par[:, 4], row(w['rwkv_r_k'].rearrange("h d -> (h d)"))), (b.par[:, 5], row(w['rwkv_ln_g']))])
    with step(nc, "cleared") as (block, s):

        @block.vector
        def _(dve):
            dve.memset(b.state[:], 0.0).then_inc(s.cleared, 1)
            dve.wait_ge(s.cleared, 1)
    return b


def rwkv_front(c, B, s, proj, i):
    R_E = float(np.exp(-0.5))
    o2 = i % 2
    x, tl, XT4, G, XT, em, bon = (t[:, o2] for t in (B.x, B.tl, B.XT4, B.G, B.XT, B.em, B.bon))
    pv, loT, wa, kk, kn, sq, ss, ex, X, Pm = B.pv, B.loT, B.wa, B.kk, B.kn, B.sq, B.ss, B.ex, B.X, B.Pm
    mu, par, lo2 = B.mu, B.par, B.lo2
    b0, b1, b2 = (B.big[:, k] for k in range(3))
    by_head = lambda ap: ap.rearrange("p (h t) -> p h t", h=HEADS)
    masks = c.all[:, 1 * P:3 * P].rearrange("p (a t) -> p a t", a=2)
    level = lambda l, d: (34 + 6 * l + d) / N
    N = 80.0

    def sync(sp):
        yield 0.0
        sp.dma_start(x, proj[i * P + PAD:(i + 1) * P + PAD, D_0:D_0 + D_W]).then_inc(s.rx_in, 16)
        sp.dma_start(pv[:], proj[i * P + PAD - 1:(i + 1) * P + PAD - 1, D_0:D_0 + D_W]).then_inc(s.rp_in, 16)

    def scalar(act):
        yield 5 / N
        act.wait_ge(s.shifted, 1)
        act.activation(x[:, D_WLO:D_WLO + RANK], x[:, D_WLO:D_WLO + RANK], ACT.Tanh).then_inc(s.lows, 1)
        act.activation(x[:, D_Z:D_Z + GW], x[:, D_Z:D_Z + GW], ACT.Silu).then_inc(s.r_silus, 1)
        yield 7 / N
        act.wait_ge(s.low_ps, 1)
        act.activation(loT[:], b1[0:RANK, 0:2 * P].rearrange("p (a t) -> p a t", a=2), ACT.Copy)\
           .then_inc(s.low_kept, 1)
        yield 10 / N
        act.wait_ge(s.kksq, 1)
        act.activation(ss[:], ss[:], ACT.Sqrt).then_inc(s.norms, 1)
        yield 11 / N
        act.wait_ge(s.wa_in, 1)
        act.activation(wa[:], wa[:], ACT.Tanh, scale=0.5).then_inc(s.tanhs, 1)
        yield 15 / N
        act.wait_ge(s.cums, 1)
        cps = b0.rearrange("p (a c) -> p a c", a=2)
        act.activation(ex[:, 0:2], cps, ACT.Exp)
        act.activation(ex[:, 2], cps[:, 0], ACT.Exp, scale=-1.0)
        act.activation(em, b1[:, 0:4].rearrange("p (j e) -> p j e", j=2), ACT.Exp).then_inc(s.exps, 1)
        yield 22 / N
        act.wait_ge(s.turned_a, 1)
        act.activation(XT4[:, 0], b2.rearrange("p (a t) -> p a t", a=4), ACT.Copy).then_inc(s.kept_a, 1)
        yield 23 / N
        act.wait_ge(s.turned_b, 1)
        act.activation(XT4[:, 1], b1.rearrange("p (a t) -> p a t", a=4), ACT.Copy).then_inc(s.kept_b, 1)
        for l in range(1, LEVELS):
            yield level(l, 1.5)
            act.wait_ge(s.p1, l + 1)
            act.activation(Pm[:], by_head(b0), ACT.Copy).then_inc(s.p1c, 1)

    def vector(dve):
        yield 1 / N
        dve.wait_ge(s.rx_in, 16)
        dve.wait_ge(s.rp_in, 16)
        dve.tensor_tensor(pv[:], pv[:], x, ALU.subtract)
        dve.drain()
        yield 2 / N
        dve.tensor_tensor(pv[:], pv[:], mu[:], ALU.mult)
        dve.drain()
        yield 3 / N
        dve.tensor_tensor(x, x, pv[:], ALU.add).then_inc(s.shifted, 1)
        k, v, r = x[:, D_K:D_K + GW], x[:, D_V:D_V + GW], x[:, D_R:D_R + GW]
        dve.drain()
        yield 5 / N
        kk2 = kk[:].rearrange("p h d -> p (h d)")
        dve.tensor_tensor(kk2, k, par[:, 2], ALU.mult)
        dve.drain()
        dve.tensor_tensor(sq[:], kk[:], kk[:], ALU.mult)
        dve.drain()
        dve.tensor_reduce(ss[:], sq[:], AX.X, ALU.add).then_inc(s.kksq, 1)
        yield 9 / N
        dve.wait_ge(s.wa_ps, 1)
        dve.tensor_tensor(wa[:], b2.rearrange("p (a c) -> p a c", a=2), par[:, 0:2], ALU.add).then_inc(s.wa_in, 1)
        yield 13 / N
        dve.wait_ge(s.tanhs, 1)
        dve.tensor_scalar(wa[:, 0], wa[:, 0], -0.5 * R_E, -0.5 * R_E, ALU.mult, ALU.add)
        dve.tensor_scalar(wa[:, 1], wa[:, 1], 0.5, 0.5, ALU.mult, ALU.add)
        dve.drain().then_inc(s.la_done, 1)
        dve.wait_ge(s.norms, 1)
        dve.tensor_scalar(ss[:], ss[:], 1e-12, None, ALU.max)
        dve.drain()
        dve.reciprocal(ss[:], ss[:])
        dve.scalar_tensor_tensor(out=kn[:], in0=wa[:, 1], scalar=-1.0, in1=par[:, 3], op0=ALU.add, op1=ALU.mult)
        dve.drain()
        yield 15 / N
        dve.tensor_tensor(kk[:], kk[:], spread(ss[:], 2, HD), ALU.mult)
        dve.scalar_tensor_tensor(out=kn[:], in0=kn[:], scalar=1.0, in1=k, op0=ALU.add, op1=ALU.mult)
        dve.drain()
        yield 17 / N
        dve.wait_ge(s.exps, 1)
        dve.tensor_tensor(tl[:, 0], r, ex[:, 0], ALU.mult)
        dve.scalar_tensor_tensor(out=tl[:, 1], in0=kk2, scalar=-1.0, in1=ex[:, 1], op0=ALU.mult, op1=ALU.mult)
        dve.tensor_tensor(tl[:, 3], kn[:], ex[:, 2], ALU.mult)
        dve.tensor_tensor(tl[:, 2], kk2, ex[:, 2], ALU.mult)
        dve.drain()
        dve.tensor_tensor(tl[:, 2], tl[:, 2], wa[:, 1], ALU.mult).then_inc(s.tilde, 1)
        yield 20 / N
        dve.tensor_copy(X[:], spread(c.ident, 1, HEADS))
        dve.tensor_copy(XT, spread(c.ident, 1, HEADS))
        dve.drain().then_inc(s.x_set, 1)
        for h in range(HEADS):
            yield (26 + 2 * h) / N
            dve.wait_ge(s.grams, h + 1)
            ps = B.big[:, h % 2].rearrange("p (b a t) -> p b a t", b=2, a=2)
            for b in range(2):
                d = dve.tensor_tensor(G[:, b, h], ps[:, b], masks, ALU.mult)
            d.then_inc(s.g_done, 1)
        dve.drain()
        for l in range(LEVELS):
            yield level(l, 4)
            at = [spread(c.all[:, m[l]].bitcast(U32), 1, HEADS) for m in (LEVEL_T, LEVEL)]
            if l == 0:
                dve.copy_predicated(XT, at[1], G[:, 0, :, 1])
                dve.wait_ge(s.p1, 1)
                dve.copy_predicated(X[:], at[0], by_head(b0))
            else:
                dve.wait_ge(s.dx, l)
                if l < LEVELS - 1:
                    dve.copy_predicated(X[:], at[0], by_head(b1))
                dve.copy_predicated(XT, at[1], by_head(b2))
            dve.drain().then_inc(s.dxc, 1)
            if l == 2:
                yield level(l, 4.5)
                s2 = sq[:].rearrange("p h d -> p (h d)")
                dve.tensor_tensor(s2, r, kn[:], ALU.mult)
                dve.drain()
                dve.tensor_tensor(s2, s2, par[:, 4], ALU.mult)
                dve.drain()
                dve.tensor_reduce(bon, sq[:], AX.X, ALU.add)

    def tensor(pe):
        yield 6 / N
        pe.wait_ge(s.lows, 1)
        pe.transpose(b1[0:RANK, 0:P], x[:, D_WLO:D_WLO + RANK], c.ident)
        pe.transpose(b1[0:RANK, P:2 * P], x[:, D_ALO:D_ALO + RANK], c.ident).then_inc(s.low_ps, 1)
        yield 8 / N
        pe.wait_ge(s.low_kept, 1)
        pe.matmul(b2[:, 0:GW], loT[:, 0], lo2[:, 0], start=True, stop=True)
        pe.matmul(b2[:, GW:2 * GW], loT[:, 1], lo2[:, 1], start=True, stop=True).then_inc(s.wa_ps, 1)
        yield 14 / N
        pe.wait_ge(s.la_done, 1)
        pe.matmul(b0[:, 0:GW], c.all[:, CENTRED], wa[:, 0], start=True, stop=True)
        pe.matmul(b0[:, GW:2 * GW], c.all[:, CENTRED_BEFORE], wa[:, 0], start=True, stop=True)
        for j in range(2):
            lj = wa[:, 0, j * P:(j + 1) * P]
            pe.matmul(b1[:, 2 * j:2 * j + 1], lj, c.upto[:, P // 2 - 1:P // 2], start=True, stop=True)
            m = pe.matmul(b1[:, 2 * j + 1:2 * j + 2], lj, c.after[:, P // 2 - 1:P // 2], start=True, stop=True)
        m.then_inc(s.cums, 1)
        for j in range(2):
            yield (20 + j) / N
            pe.wait_ge(s.tilde, 1)
            for a in range(4):
                m = pe.transpose((b2, b1)[j][:, a * P:(a + 1) * P], tl[:, a, j * P:(j + 1) * P], c.ident)
            m.then_inc((s.turned_a, s.turned_b)[j], 1)
        for h in range(HEADS):
            yield (25 + 2 * h) / N
            off, j = HD * (h % 2), h // 2
            pe.wait_ge(s.kept_a, 1)
            if h:
                pe.wait_ge(s.kept_b, 1)
            if h >= 2:
                pe.wait_ge(s.g_done, h - 1)
            o = slice(off, off + HD)
            for b in range(2):
                m = pe.matmul(B.big[:, h % 2, b * GW:(b + 1) * GW], XT4[o, j, 2 + b],
                              XT4[o, j, 0:2].rearrange("p a t -> p (a t)"), start=True, stop=True)
            m.then_inc(s.grams, 1)
        for l in range(LEVELS):
            yield level(l, 0)
            if l == 0:
                pe.wait_ge(s.g_done, HEADS)
                pe.wait_ge(s.x_set, 1)
            else:
                pe.wait_ge(s.dxc, l)
            for h in range(HEADS):
                m = pe.matmul(b0[:, h * P:(h + 1) * P], G[:, 0, h, 1], X[:, h], start=True, stop=True)
            m.then_inc(s.p1, 1)
            if l:
                yield level(l, 2)
                pe.wait_ge(s.p1c, l)
                for h in range(HEADS):
                    if l < LEVELS - 1:
                        pe.matmul(b1[:, h * P:(h + 1) * P], XT[:, h], Pm[:, h], start=True, stop=True)
                    m = pe.matmul(b2[:, h * P:(h + 1) * P], Pm[:, h], XT[:, h], start=True, stop=True)
                m.then_inc(s.dx, 1)

    return {"sync": sync, "scalar": scalar, "vector": vector, "tensor": tensor}


def rwkv_back(c, B, s, mixed, i):
    o2 = i % 2
    x, tl, XT4, G, XT, em, bon = (t[:, o2] for t in (B.x, B.tl, B.XT4, B.G, B.XT, B.em, B.bon))
    R, U, S0, y, sq, ss, par, state = B.R, B.U, B.S0, B.y, B.sqb, B.ssb, B.par, B.state
    both = B.big[:, 3:5]
    v = x[:, D_V:D_V + GW].rearrange("p (h d) -> p h d", h=HEADS)
    pairs = lambda ap: ap[:, :, 0:2 * HD].rearrange("p r (j d) -> p j r d", d=HD)
    N = 40.0

    def sync(sp):
        yield 0.99
        sp.wait_ge(s.ry_done, 1)
        sp.dma_start(mixed[i * P:(i + 1) * P, 3 * GW:4 * GW], y[:].rearrange("p h d -> p (h d)"))\
          .then_inc(s.r_stored, 16)
        sp.wait_ge(s.r_stored, 16)

    def scalar(act):
        yield 6 / N
        act.wait_ge(s.r_ps, 1)
        act.activation(R[:].rearrange("p (j r) d -> p j r d", j=2), pairs(both), ACT.Copy).then_inc(s.r_done, 1)
        yield 10 / N
        act.wait_ge(s.u_ps, 1)
        act.activation(U[:], both[:, 0, 0:GW].rearrange("p (h d) -> p h d", h=HEADS), ACT.Copy)\
           .then_inc(s.u_done, 1)
        yield 15 / N
        act.wait_ge(s.ry_ps, 1)
        act.activation(y[:].rearrange("p (j r) d -> p j r d", j=2), pairs(both), ACT.Copy).then_inc(s.ry_kept, 1)
        yield 22 / N
        act.wait_ge(s.rsqd, 1)
        rstd(act, c, ss[:], HD).then_inc(s.rrs, 1)

    def vector(dve):
        yield 0.0
        for j in range(2):
            d = dve.tensor_scalar(S0[:, j], state[:, j], em[:, j, 0:1], None, ALU.mult)
        d.then_inc(s.s0_done, 1)
        yield 17 / N
        dve.wait_ge(s.ry_kept, 1)
        dve.tensor_tensor(sq[:], y[:], y[:], ALU.mult)
        dve.drain()
        dve.tensor_reduce(ss[:], sq[:], AX.X, ALU.add).then_inc(s.rsqd, 1)
        y2 = y[:].rearrange("p h d -> p (h d)")
        dve.tensor_tensor(y2, y2, par[:, 5], ALU.mult)
        dve.drain()
        dve.tensor_tensor(sq[:], v, spread(bon, 2, HD), ALU.mult)
        yield 20 / N
        dve.wait_ge(s.st_ps, 1)
        for off in (0, HD):
            o = slice(off, off + HD)
            dve.tensor_tensor(S0[o], S0[o], both[o, 0, 0:2 * P].rearrange("p (j c) -> p j c", j=2)[:, :, o], ALU.add)
        dve.drain()
        for j in range(2):
            dve.tensor_scalar(state[:, j], S0[:, j], em[:, j, 1:2], None, ALU.mult)
        yield 25 / N
        dve.wait_ge(s.rrs, 1)
        dve.drain()
        dve.tensor_tensor(y[:], y[:], spread(ss[:], 2, HD), ALU.mult)
        dve.drain()
        yield 27 / N
        dve.tensor_tensor(y[:], y[:], sq[:], ALU.add)
        dve.drain()
        yield 29 / N
        dve.tensor_tensor(y2, y2, x[:, D_Z:D_Z + GW], ALU.mult).then_inc(s.ry_done, 1)

    def tensor(pe):
        yield 1 / N
        pe.wait_ge(s.s0_done, 1)
        for h in range(HEADS):
            off, j = HD * (h % 2), h // 2
            o, dst = slice(off, off + HD), both[:, h % 2, j * HD:(j + 1) * HD]
            pe.matmul(dst, XT4[o, j, 1], S0[o, j], start=True, stop=False)
            m = pe.matmul(dst, G[:, 1, h, 1], v[:, h], start=False, stop=True)
        m.then_inc(s.r_ps, 1)
        yield 8 / N
        pe.wait_ge(s.r_done, 1)
        for h in range(HEADS):
            m = pe.matmul(both[:, 0, h * HD:(h + 1) * HD], XT[:, h], R[:, h], start=True, stop=True)
        m.then_inc(s.u_ps, 1)
        yield 12 / N
        pe.wait_ge(s.u_done, 1)
        for h in range(HEADS):
            off, j = HD * (h % 2), h // 2
            o, dst = slice(off, off + HD), both[:, h % 2, j * HD:(j + 1) * HD]
            pe.matmul(dst, XT4[o, j, 0], S0[o, j], start=True, stop=False)
            pe.matmul(dst, G[:, 0, h, 0], U[:, h], start=False, stop=False)
            m = pe.matmul(dst, G[:, 1, h, 0], v[:, h], start=False, stop=True)
        m.then_inc(s.ry_ps, 1)
        yield 18 / N
        pe.wait_ge(s.ry_kept, 1)
        for j in range(2):
            dst = both[:, 0, j * P:(j + 1) * P]
            pe.matmul(dst, tl[:, 2, j * P:(j + 1) * P],
                      U[:, 2 * j:2 * j + 2].rearrange("p h d -> p (h d)"), start=True, stop=False)
            m = pe.matmul(dst, tl[:, 3, j * P:(j + 1) * P], x[:, D_V + j * P:D_V + (j + 1) * P],
                          start=False, stop=True)
        m.then_inc(s.st_ps, 1)

    return {"sync": sync, "scalar": scalar, "vector": vector, "tensor": tensor}


ALPHA = 2.0 ** 0.25


def project_out(nc, c, mix, w_out, x_in, x_out, name, turned_out=None, ln=None):
    K = mix.shape[1] // P
    KB = [(k, min(4, K - k)) for k in range(0, K, 4)]
    U = 4
    with ExitStack() as ctx:
        B = Buffers(nc, ctx, name)
        wo = B.sb("wo", [P, K, D_MODEL])
        m = B.sb("m", [P, 2, K * P])
        x = B.sb("x", [P, U, D_MODEL])
        mT = B.sb("mT", [P, 2, K, P])
        tp = B.ps("tp", [P, 2, 4, P])
        acc = B.ps("acc", [P, 2, 2, 512])
        loads = [(wo[:], w_out.rearrange("(k p) n -> p k n", p=P))]
        if ln:
            gb = B.sb("gb", [P, 2, D_MODEL])
            st = B.sb("st", [P, 2, 6])
            ag = B.sb("ag", [P, 2])
            loads += [(gb[:, 0], row(ln[0])), (gb[:, 1], row(ln[1]))]
        else:
            tq = B.ps("tq", [P, 2, 4, P])
        load(nc, f"{name}_w", loads)
        nb = len(KB)
        with nc.Fori(0, TILES // U) as i:
            with step(nc, "m_in0 m_in1 x_in turned kept prod summed vars rs stored x_turned x_kept") as (block, s):
                m_in = (s.m_in0, s.m_in1)

                @block.sync
                def _(sp):
                    sp.dma_start(x[:], tokens(x_in, i * U, U, 0, D_MODEL)).then_inc(s.x_in, 16)
                    for u in range(U):
                        if u >= 2:
                            sp.wait_ge(s.turned, nb * (u - 1))
                        sp.dma_start(m[:, u % 2], mix[bass.ds((i * U + u) * P, P), :]).then_inc(m_in[u % 2], 16)
                    for u in range(U):
                        sp.wait_ge(s.summed, u + 1)
                        sp.dma_start(x_out[bass.ds((i * U + u) * P, P), :], x[:, u]).then_inc(s.stored, 16)
                    sp.wait_ge(s.stored, 16 * U)

                @block.tensor
                def _(pe):
                    def turn(u):
                        pe.wait_ge(m_in[u % 2], 16 * (u // 2 + 1))
                        for b, (k0, kn) in enumerate(KB):
                            n = u * nb + b
                            if n >= 2:
                                pe.wait_ge(s.kept, n - 1)
                            for k in range(kn):
                                t = pe.transpose(tp[:, n % 2, k], m[:, u % 2, (k0 + k) * P:(k0 + k + 1) * P], c.ident)
                            t.then_inc(s.turned, 1)

                    def multiply(u):
                        pe.wait_ge(s.kept, nb * (u + 1))
                        if u >= 2:
                            pe.wait_ge(s.summed, u - 1)
                        for n in range(2):
                            for k in range(K):
                                t = pe.matmul(acc[:, u % 2, n], mT[:, u % 2, k], wo[:, k, n * 512:(n + 1) * 512],
                                              start=(k == 0), stop=(k == K - 1))
                        t.then_inc(s.prod, 1)

                    def turn_x(u):
                        pe.wait_ge(s.summed, u + 1)
                        for b in range(2):
                            n = 2 * u + b
                            if n >= 2:
                                pe.wait_ge(s.x_kept, n - 1)
                            for k in range(4):
                                t = pe.transpose(tq[:, n % 2, k], x[:, u, (4 * b + k) * P:(4 * b + k + 1) * P],
                                                 c.ident)
                            t.then_inc(s.x_turned, 1)

                    turn(0)
                    for u in range(U):
                        if u + 1 < U:
                            turn(u + 1)
                        multiply(u)
                        if not ln and u:
                            turn_x(u - 1)
                    if not ln:
                        turn_x(U - 1)

                @block.scalar
                def _(act):
                    def keep(u):
                        for b, (k0, kn) in enumerate(KB):
                            n = u * nb + b
                            act.wait_ge(s.turned, n + 1)
                            if u >= 2 and b == 0:
                                act.wait_ge(s.prod, u - 1)
                            act.activation(mT[:, u % 2, k0:k0 + kn], tp[:, n % 2, 0:kn], ACT.Copy)\
                               .then_inc(s.kept, 1)

                    keep(0)
                    for u in range(U):
                        if u + 1 < U:
                            keep(u + 1)
                        if ln:
                            act.wait_ge(s.vars, u + 1)
                            act.activation(ag[:, 1:2], ag[:, 1:2], ACT.Ln, bias=c.eps[:, 1:2])
                            act.drain()
                            act.activation(ag[:, 1:2], ag[:, 1:2], ACT.Exp, scale=-0.5).then_inc(s.rs, 1)

                @block.vector
                def _(dve):
                    def keep_x(u):
                        for b in range(2):
                            n = 2 * u + b
                            dve.wait_ge(s.x_turned, n + 1)
                            dve.tensor_copy(turned_out[:, 4 * b:4 * b + 4, bass.ds((i * U + u) * P, P)],
                                            tq[:, n % 2]).then_inc(s.x_kept, 1)

                    dve.wait_ge(s.x_in, 16)
                    for u in range(U):
                        dve.wait_ge(s.prod, u + 1)
                        xu = x[:, u].rearrange("p (n c) -> p n c", n=2)
                        if not ln:
                            dve.tensor_tensor(xu, xu, acc[:, u % 2], ALU.add).then_inc(s.summed, 1)
                            if u:
                                keep_x(u - 1)
                            continue
                        for n in range(2):
                            dve.scalar_tensor_tensor(out=xu[:, n], in0=xu[:, n], scalar=ALPHA, in1=acc[:, u % 2, n],
                                                     op0=ALU.mult, op1=ALU.add)
                        dve.drain()
                        for n in range(2):
                            dve.bn_stats(st[:, n], xu[:, n])
                        dve.drain()
                        dve.bn_aggr(ag[:], st[:].rearrange("p a b -> p (a b)"))
                        dve.drain().then_inc(s.vars, 1)
                        dve.wait_ge(s.rs, u + 1)
                        dve.tensor_scalar(x[:, u], x[:, u], ag[:, 0:1], ag[:, 1:2], ALU.subtract, ALU.mult)
                        dve.drain()
                        dve.tensor_tensor(x[:, u], x[:, u], gb[:, 0], ALU.mult)
                        dve.drain()
                        dve.tensor_tensor(x[:, u], x[:, u], gb[:, 1], ALU.add).then_inc(s.summed, 1)
                    if not ln:
                        keep_x(U - 1)




INDEX_SIGNALS = "iq_in iw_in iq_scaled iq_turned iq_kept dots relus summed "
SELECT_SIGNALS = "threshold_set above_set "
ATTEND_SIGNALS = ("q_in g_in silus q_turned q_kept ql_ps ql_kept biased logits added maxed exps turned kept weighed "
                  "o_kept o_ps y_done y_stored ")
HGRN_SIGNALS = ("hx_in hf_in sigs h_silus f_done logf turned_hq hq_kept turned_hk hk_kept sums b_kept pairs own_set "
                "diffs e_diffs h_exps tilde e_tilde picked e_in e_out ee_done ke_t ktok_done ho_ps up_ps sqd rs hy_done "
                "h_stored ")


def index_buffers(B, ikT, score):
    b = Constants()
    b.ikT, b.score = ikT, score
    b.iq = B.sb("iq", [P, IDX_HEADS, IDX_DIM])
    b.iw = B.sb("iw", [P, 3, IDX_HEADS])
    b.iqT = B.sb("iqT", [IDX_DIM, IDX_HEADS, P])
    b.rel = B.sb("rel", [P, 2, 512])
    return b


def index_scores(c, b, s, proj, big, k):
    W = (k + 1) * P
    iq, iw, iqT, rel, score = b.iq, b.iw, b.iqT, b.rel, b.score[:, k % 2]
    PIECES = [(x, min(512, W - x)) for x in range(0, W, 512)]
    NP = len(PIECES)
    first = 0.06
    place = lambda n: first + (0.96 - first) * n / (IDX_HEADS * NP + 1)

    def sync(sp):
        yield 0.0
        tok = slice(k * P, (k + 1) * P)
        sp.dma_start(iw[:, 0], proj[tok, E_IW:E_IW + IDX_HEADS]).then_inc(s.iw_in, 16)
        sp.dma_start(iq[:].rearrange("p h d -> p (h d)"), proj[tok, E_IQ:E_IQ + IDX_HEADS * IDX_DIM])\
          .then_inc(s.iq_in, 16)

    def vector(dve):
        yield 0.02
        dve.wait_ge(s.iw_in, 16)
        dve.scalar_tensor_tensor(out=iw[:, 1], in0=iw[:, 0], scalar=-1.0, in1=iw[:, 0], op0=ALU.mult, op1=ALU.max)
        dve.tensor_scalar(iw[:, 2], iw[:, 0], 0.0, 2.0, ALU.is_ge, ALU.mult)
        dve.drain()
        dve.tensor_scalar(iw[:, 1], iw[:, 1], float(IDX_HEADS ** -0.5 * IDX_DIM ** -0.5), None, ALU.mult)
        dve.tensor_scalar(iw[:, 2], iw[:, 2], -1.0, None, ALU.add)
        dve.wait_ge(s.iq_in, 16)
        dve.drain()
        dve.tensor_tensor(iq[:], iq[:], spread(iw[:, 1], 2, IDX_DIM), ALU.mult).then_inc(s.iq_scaled, 1)
        n = 0
        for h in range(IDX_HEADS):
            for x, wd in PIECES:
                yield place(n + 1.4)
                dve.wait_ge(s.relus, n + 1)
                sg = iw[:, 2, h:h + 1]
                if h:
                    if NP == 1 or n % NP == 0:
                        dve.drain()
                    d = dve.scalar_tensor_tensor(out=score[:, x:x + wd], in0=rel[:, n % 2, 0:wd], scalar=sg,
                                                 in1=score[:, x:x + wd], op0=ALU.mult, op1=ALU.add)
                else:
                    d = dve.tensor_scalar(score[:, x:x + wd], rel[:, n % 2, 0:wd], sg, 0.0, ALU.mult, ALU.add)
                d.then_inc(s.summed, 1)
                n += 1
        yield 0.98
        dve.drain()
        dve.tensor_tensor(score[:, k * P:W], score[:, k * P:W], c.all[:, CHUNKED], ALU.add)

    def scalar(act):
        yield 0.04
        act.wait_ge(s.iq_turned, 1)
        act.activation(iqT[:].rearrange("p (a h) t -> p a (h t)", a=2), big[0:IDX_DIM, 0:2], ACT.Copy)\
           .then_inc(s.iq_kept, 1)
        n = 0
        for h in range(IDX_HEADS):
            for x, wd in PIECES:
                yield place(n + 0.5)
                act.wait_ge(s.dots, n + 1)
                if n >= 2:
                    act.wait_ge(s.summed, n - 1)
                act.activation(rel[:, n % 2, 0:wd], big[:, n % 2, 0:wd], ACT.Relu).then_inc(s.relus, 1)
                n += 1

    def tensor(pe):
        yield 0.03
        pe.wait_ge(s.iq_scaled, 1)
        for h in range(IDX_HEADS):
            m = pe.transpose(big[0:IDX_DIM, h // 4, (h % 4) * P:(h % 4 + 1) * P], iq[:, h], c.ident)
        m.then_inc(s.iq_turned, 1)
        n = 0
        for h in range(IDX_HEADS):
            for x, wd in PIECES:
                yield place(n)
                if n == 0:
                    pe.wait_ge(s.iq_kept, 1)
                if n >= 2:
                    pe.wait_ge(s.relus, n - 1)
                pe.matmul(big[:, n % 2, 0:wd], iqT[:, h], b.ikT[:, x:x + wd], start=True, stop=True)\
                  .then_inc(s.dots, 1)
                n += 1

    return {"sync": sync, "vector": vector, "scalar": scalar, "tensor": tensor}


def threshold_buffers(B, score, sel):
    b = Constants()
    b.score, b.sel = score, sel
    b.hi = B.sb("hi", [P, SEQ], U16)
    b.lo = B.sb("lo", [P, SEQ], U16)
    b.eq = B.sb("eq", [P, SEQ])
    b.num = B.sb("num", [P, 8])
    return b


def select_keys(c, b, s, k):
    W = (k + 1) * P
    score, sel = b.score[:, k % 2, 0:W], b.sel[:, k % 2, 0:W]
    hi, lo, eq = b.hi[:, 0:W], b.lo[:, 0:W], b.eq[:, 0:W]
    seen = b.eq[:].bitcast(U16)[:, 0:W]
    cell = lambda n: b.num[:, n:n + 1]
    cand, count, hit, need, top, bits, sign, n_hi = (cell(n) for n in range(8))
    u = sel.bitcast(U32)
    halves = sel.bitcast(U16).rearrange("p (n a) -> p n a", a=2)
    KEEP = float(TOPK)

    def vector(dve):
        if W <= TOPK:
            yield 0.0
            dve.memset(sel, 0.0)
            dve.drain()
            dve.tensor_copy(b.sel[:, k % 2, k * P:W], c.all[:, CHUNKED])
            return

        def halve(x, wanted, place):
            dve.memset(cand, 32768.0)
            for bit in range(15, -1, -1):
                yield place + 0.43 * (15 - bit) / 16
                dve.drain()
                dve.tensor_scalar(seen, x, cand, 0.0, ALU.is_ge, ALU.add, accum_out=count)
                dve.drain()
                dve.tensor_scalar(hit, count, wanted, float(1 << bit), ALU.is_ge, ALU.mult)
                dve.drain()
                dve.scalar_tensor_tensor(out=cand, in0=hit, scalar=-float(1 << bit >> 1) if bit else -1.0, in1=cand,
                                         op0=ALU.add, op1=ALU.add)
            dve.drain()

        yield 0.0
        dve.tensor_scalar(u.bitcast(I32), score.bitcast(I32), 31, -2 ** 31, ALU.arith_shift_right, ALU.bitwise_or)
        dve.drain()
        dve.tensor_tensor(u, u, score.bitcast(U32), ALU.bitwise_xor)
        dve.drain()
        dve.tensor_copy(hi, halves[:, :, 1])
        yield from halve(hi, KEEP, 0.03)
        dve.tensor_copy(top, cand)
        dve.tensor_scalar(seen, hi, cand, 0.0, ALU.is_gt, ALU.add, accum_out=n_hi)
        dve.scalar_tensor_tensor(out=lo, in0=hi, scalar=cand, in1=halves[:, :, 0], op0=ALU.is_equal, op1=ALU.mult)
        dve.drain()
        dve.tensor_scalar(need, n_hi, -1.0, KEEP, ALU.mult, ALU.add)
        dve.drain()
        yield from halve(lo, need, 0.47)
        dve.tensor_scalar(seen, lo, cand, 0.0, ALU.is_gt, ALU.add, accum_out=count)
        dve.tensor_copy(bits.bitcast(U16)[:, 1:2], top)
        dve.tensor_copy(bits.bitcast(U16)[:, 0:1], cand)
        dve.drain()
        dve.tensor_scalar(sign.bitcast(I32), bits.bitcast(I32), 31, -1, ALU.arith_shift_right, ALU.bitwise_xor)
        dve.drain()
        dve.tensor_scalar(sign.bitcast(I32), sign.bitcast(I32), -2 ** 31, None, ALU.bitwise_or)
        dve.drain()
        dve.tensor_tensor(bits.bitcast(U32), bits.bitcast(U32), sign.bitcast(U32), ALU.bitwise_xor)
        dve.tensor_tensor(need, need, count, ALU.subtract)
        dve.drain().then_inc(s.threshold_set, 1)
        yield 0.92
        dve.tensor_scalar(eq, score, bits, None, ALU.is_equal)
        dve.drain()
        yield 0.94
        dve.wait_ge(s.above_set, 1)
        dve.tensor_tensor_scan(score, eq, eq, 0.0, ALU.add, ALU.max)
        dve.drain()
        yield 0.96
        dve.scalar_tensor_tensor(out=eq, in0=score, scalar=need, in1=eq, op0=ALU.is_le, op1=ALU.mult)
        dve.drain()
        yield 0.98
        dve.scalar_tensor_tensor(out=sel, in0=eq, scalar=-NEG, in1=sel, op0=ALU.mult, op1=ALU.add)
        dve.drain()
        dve.tensor_tensor(b.sel[:, k % 2, k * P:W], b.sel[:, k % 2, k * P:W], c.all[:, CHUNKED], ALU.add)

    def gpsimd(pool):
        if W <= TOPK:
            return
        yield 0.92
        pool.wait_ge(s.threshold_set, 1)
        pool.tensor_scalar(sel, score, bits, None, ALU.is_gt)
        pool.drain()
        pool.tensor_scalar(sel, sel, -1.0, -NEG, ALU.add, ALU.mult)
        pool.drain().then_inc(s.above_set, 1)

    return {"vector": vector, "gpsimd": gpsimd} if W > TOPK else {"vector": vector}


def attend_buffers(B, cT, ct, uk, uv, bias, sel):
    b = Constants()
    b.cT, b.ct, b.uk, b.uv, b.bias, b.sel = cT, ct, uk, uv, bias, sel
    b.q = B.sb("q", [P, 4 * P])
    b.gate = B.sb("gate", [P, 4, P])
    b.qT = B.sb("qT", [P, 4, P])
    b.ql = B.sb("ql", [P, 4, P])
    b.L = B.sb("L", [P, 2, SEQ])
    b.mx = B.sb("mx", [P, 4, 4])
    b.top = B.sb("top", [P, 4])
    b.den = B.sb("den", [P, 4])
    b.pT = B.sb("pT", [P, 2, 4, P])
    return b


def attend(c, b, s, proj, mix, big, k):
    H, R = 4, P
    W = (k + 1) * P
    q, gate, qT, ql, mx, top, den, pT, bias = b.q, b.gate, b.qT, b.ql, b.mx, b.top, b.den, b.pT, b.bias
    oT, y = b.qT, b.q
    PIECES = [(x, min(512, W - x)) for x in range(0, W, 512)]
    NP = len(PIECES)
    tok = slice(k * P, (k + 1) * P)
    N = 13.6
    at_logits = lambda h, p: (2 + 2 * h + 1.6 * p / NP) / N
    at_exp = lambda h: (3.8 + 2 * h) / N
    at_turn = lambda h, p: (4 + 2 * h + 1.6 * (p + 0.5) / NP) / N
    pitch = 1.6 / NP / N
    uses = [("q", (s.q_kept, 1)), ("ql", (s.ql_kept, 1))]
    for h in range(H + 1):
        for p in range(NP):
            if h < H:
                uses.append((("L", h, p), (s.added, h * NP + p + 1)))
            if h:
                uses.append((("T", h - 1, p), (s.kept, (h - 1) * NP + p + 1)))
    uses += [("o", (s.y_done, 1))]
    turns = in_turn([2, 3, 4], uses)

    def bank(*key):
        return turns[key if len(key) > 1 else key[0]][0]

    def take(pe, *key):
        n, before = turns[key if len(key) > 1 else key[0]]
        if before:
            pe.wait_ge(*before)
        return n

    def sync(sp):
        yield 0.001
        sp.dma_start(q[:], proj[tok, E_Q:E_Q + H * R]).then_inc(s.q_in, 16)
        sp.dma_start(gate[:].rearrange("p h d -> p (h d)"), proj[tok, E_G:E_G + H * P]).then_inc(s.g_in, 16)
        yield 1.0
        sp.wait_ge(s.y_done, 1)
        sp.dma_start(mix[tok, 0:512], y[:]).then_inc(s.y_stored, 16)
        sp.wait_ge(s.y_stored, 16)

    def gpsimd(pool):
        for h in range(H):
            yield 0.0 if h < 2 else (1.65 + 2 * h) / N
            if h >= 2:
                pool.wait_ge(s.turned, (h - 1) * NP)
            pool.tensor_tensor(b.L[:, h % 2, 0:W], b.sel[:, k % 2, 0:W],
                               bias[:, h, (TILES - 1 - k) * P:(TILES - 1 - k) * P + W], ALU.add).then_inc(s.biased, 1)

    def scalar(act):
        yield 0.0
        act.wait_ge(s.g_in, 16)
        act.activation(gate[:], gate[:], ACT.Silu).then_inc(s.silus, 1)
        yield 0.5 / N
        act.wait_ge(s.q_turned, 1)
        act.activation(qT[:], big[:, bank("q")].rearrange("p (h t) -> p h t", h=H), ACT.Copy)\
           .then_inc(s.q_kept, 1)
        act.wait_ge(s.ql_ps, 1)
        act.activation(ql[:], big[:, bank("ql")].rearrange("p (h t) -> p h t", h=H), ACT.Copy,
                       scale=P ** -0.5).then_inc(s.ql_kept, 1)
        for h in range(H):
            if h:
                yield from keep(act, h - 1)
            yield at_exp(h)
            act.wait_ge(s.maxed, h + 1)
            act.activation(b.L[:, h % 2, 0:W], b.L[:, h % 2, 0:W], ACT.Exp, bias=top[:, h:h + 1],
                           accum_out=den[:, h:h + 1]).then_inc(s.exps, 1)
        yield from keep(act, H - 1)
        yield 12.0 / N
        act.wait_ge(s.weighed, H * NP)
        act.activation(oT[:], big[:, 5].rearrange("p (h t) -> p h t", h=H), ACT.Copy).then_inc(s.o_kept, 1)

    def keep(act, h):
        for p, (x, wd) in enumerate(PIECES):
            n = h * NP + p
            yield at_turn(h, p) + 0.4 * pitch
            act.wait_ge(s.turned, n + 1)
            if n >= 2:
                act.wait_ge(s.weighed, n - 1)
            act.activation(pT[:, n % 2, 0:wd // P],
                           big[:, bank("T", h, p), 0:wd].rearrange("p (b t) -> p b t", t=P), ACT.Copy)\
               .then_inc(s.kept, 1)

    def vector(dve):
        for h in range(H):
            for p, (x, wd) in enumerate(PIECES):
                yield at_logits(h, p) + 0.9 * pitch
                if p == 0:
                    dve.wait_ge(s.biased, h + 1)
                dve.wait_ge(s.logits, h * NP + p + 1)
                L = b.L[:, h % 2, x:x + wd]
                dve.tensor_tensor_reduce(L, big[:, bank("L", h, p), 0:wd], L, 1.0, 4 * NEG, ALU.add, ALU.max,
                                         mx[:, h, p:p + 1]).then_inc(s.added, 1)
            yield at_exp(h)
            dve.drain()
            dve.tensor_reduce(top[:, h:h + 1], mx[:, h, 0:NP], AX.X, ALU.max)
            dve.drain()
            dve.tensor_scalar(top[:, h:h + 1], top[:, h:h + 1], -1.0, None, ALU.mult).then_inc(s.maxed, 1)
        yield 12.0 / N
        dve.wait_ge(s.exps, H)
        dve.reciprocal(den[:], den[:])
        dve.wait_ge(s.silus, 1)
        dve.drain()
        dve.tensor_tensor(gate[:], gate[:], spread(den[:], 2, P), ALU.mult)
        dve.drain()
        yield 12.8 / N
        dve.wait_ge(s.o_ps, 1)
        dve.tensor_tensor(y[:].rearrange("p (h t) -> p h t", h=H),
                          big[:, bank("o")].rearrange("p (h t) -> p h t", h=H), gate[:], ALU.mult)\
           .then_inc(s.y_done, 1)

    def tensor(pe):
        yield 0.5 / N
        pe.wait_ge(s.q_in, 16)
        n = take(pe, "q")
        for h in range(H):
            m = pe.transpose(big[:, n, h * P:(h + 1) * P], q[:, h * R:(h + 1) * R], c.ident)
        m.then_inc(s.q_turned, 1)
        pe.wait_ge(s.q_kept, 1)
        n = take(pe, "ql")
        for h in range(H):
            m = pe.matmul(big[:, n, h * P:(h + 1) * P], b.uk[:, h], qT[:, h], start=True, stop=True)
        m.then_inc(s.ql_ps, 1)
        for h in range(H + 1):
            for p in range(NP):
                if h < H:
                    yield at_logits(h, p)
                    if h == p == 0:
                        pe.wait_ge(s.ql_kept, 1)
                    logits(pe, h, p)
                if h:
                    yield at_turn(h - 1, p)
                    if p == 0:
                        pe.wait_ge(s.exps, h)
                    turn(pe, h - 1, p)
                    if p:
                        weigh(pe, h - 1, p - 1)
            if h:
                yield at_turn(h - 1, NP - 1) + 0.45 * pitch
                weigh(pe, h - 1, NP - 1)
        yield 12.0 / N
        pe.wait_ge(s.o_kept, 1)
        n = take(pe, "o")
        for h in range(H):
            m = pe.matmul(big[:, n, h * P:(h + 1) * P], oT[:, h], b.uv[:, h], start=True, stop=True)
        m.then_inc(s.o_ps, 1)

    def logits(pe, h, p):
        x, wd = PIECES[p]
        n = take(pe, "L", h, p)
        pe.matmul(big[:, n, 0:wd], ql[:, h], b.cT[:, x:x + wd], start=True, stop=True).then_inc(s.logits, 1)

    def turn(pe, h, p):
        x, wd = PIECES[p]
        n = take(pe, "T", h, p)
        for t in range(wd // P):
            m = pe.transpose(big[:, n, t * P:(t + 1) * P], b.L[:, h % 2, x + t * P:x + (t + 1) * P], c.ident)
        m.then_inc(s.turned, 1)

    def weigh(pe, h, p):
        x, wd = PIECES[p]
        pe.wait_ge(s.kept, h * NP + p + 1)
        for t in range(wd // P):
            m = pe.matmul(big[:, 5, h * P:(h + 1) * P], b.ct[:, x // P + t], pT[:, (h * NP + p) % 2, t],
                          start=(p == 0 and t == 0), stop=(x + (t + 1) * P == W))
        m.then_inc(s.weighed, 1)

    return {"sync": sync, "gpsimd": gpsimd, "vector": vector, "scalar": scalar, "tensor": tensor}


def hgrn_buffers(B, big):
    H = BH
    b = Constants()
    b.lb = B.sb("lb", [P, 2, H * BD])
    b.g = B.sb("hg", [P, H * BD])
    b.state = B.sb("state", [P, H, BD])
    b.x = B.sb("x", [P, 4, H * BD])
    b.k = B.sb("k", [P, H * BD])
    b.kT = B.sb("kT", [P, H, P])
    b.hqT = B.sb("hqT", [P, H, P])
    b.bT = B.sb("bT", [P, H, P])
    b.E = B.sb("E", [P, 2, H, P])
    b.A = B.sb("A", [P, H, P])
    b.qe = B.sb("qe", [P, H, P])
    b.ke = B.sb("ke", [P, H, P])
    b.ktok = B.sb("ktok", [P, H, P])
    b.dec = B.sb("dec", [P, H])
    b.y = B.sb("y", [P, H, BD])
    b.ss = B.sb("ssq", [P, H])
    b.big = big
    return b


def hgrn_setup(nc, w, b):
    lb, g, E, state = b.lb, b.g, b.E, b.state
    load(nc, "hg_w", [(lb[:, 0], row(w['lb_logits_2'][0])), (lb[:, 1], row(w['lb_logits_2'][1])),
                      (g[:], row(w['hgrn_norm_g_2']))])
    with step(nc, "expd diffd cleared lbd") as (block, s):

        @block.vector
        def _(dve):
            dve.memset(state[:], 0.0).then_inc(s.cleared, 1)
            dve.tensor_tensor(E[:, 0].rearrange("p h t -> p (h t)"), lb[:, 0], lb[:, 1], ALU.max)
            dve.drain()
            for n in range(2):
                dve.tensor_tensor(lb[:, n], lb[:, n], E[:, 0].rearrange("p h t -> p (h t)"), ALU.subtract)
            dve.drain().then_inc(s.diffd, 1)
            dve.wait_ge(s.expd, 1)
            dve.tensor_tensor(lb[:, 1], lb[:, 0], lb[:, 1], ALU.add)
            dve.drain()
            dve.reciprocal(lb[:, 1], lb[:, 1])
            dve.drain()
            dve.tensor_tensor(lb[:, 0], lb[:, 0], lb[:, 1], ALU.mult)
            dve.drain()
            dve.tensor_scalar(lb[:, 1], lb[:, 0], -1.0, 1.0, ALU.mult, ALU.add).then_inc(s.lbd, 1)

        @block.scalar
        def _(act):
            act.wait_ge(s.diffd, 1)
            act.activation(lb[:], lb[:], ACT.Exp).then_inc(s.expd, 1)


def hgrn_chunk(c, b, s, proj, mix, i):
    H = BH
    lb, g, state, x, k, qT, kT, bT, E, A = b.lb, b.g, b.state, b.x, b.k, b.hqT, b.kT, b.bT, b.E, b.A
    qe, ke, ktok, dec, y, ss, big = b.qe, b.ke, b.ktok, b.dec, b.y, b.ss, b.big
    four = lambda n: big[:, n].rearrange("p (h t) -> p h t", h=H)
    tok = slice(i * P, (i + 1) * P)

    N = 29.0

    def halves(ap, l):
        v = ap.rearrange("p h (n a b) -> p h n a b", a=2, b=1 << l)
        return v[:, :, :, 0], v[:, :, :, 1]

    def joint(l):
        half = 1 << l
        v = bT[:].rearrange("p h (n a b) -> p h n a b", a=2, b=half)[:, :, :, 0, half - 1]
        return spread(v, 3, half)

    def sync(sp):
        yield 0.002
        sp.dma_start(x[:, 1], proj[tok, H_F:H_F + H * BD]).then_inc(s.hf_in, 16)
        sp.dma_start(x[:, 0], proj[tok, H_Q:H_Q + H * BD]).then_inc(s.hx_in, 16)
        sp.dma_start(x[:, 2:4].rearrange("p a c -> p (a c)"), proj[tok, H_I:H_I + 2 * H * BD]).then_inc(s.hx_in, 16)
        yield 1.0
        sp.wait_ge(s.hy_done, 1)
        sp.dma_start(mix[tok, 512:1024], y[:].rearrange("p h d -> p (h d)")).then_inc(s.h_stored, 16)
        sp.wait_ge(s.h_stored, 16)

    def scalar(act):
        yield 1 / N
        act.wait_ge(s.hf_in, 16)
        act.activation(x[:, 1], x[:, 1], ACT.Sigmoid).then_inc(s.sigs, 1)
        act.wait_ge(s.hx_in, 32)
        act.activation(x[:, 0], x[:, 0], ACT.Silu)
        act.activation(x[:, 3], x[:, 3], ACT.Silu).then_inc(s.h_silus, 1)
        yield 3 / N
        act.wait_ge(s.f_done, 1)
        act.activation(x[:, 1], x[:, 1], ACT.Ln).then_inc(s.logf, 1)
        act.wait_ge(s.turned_hq, 1)
        act.activation(qT[:], four(6), ACT.Copy).then_inc(s.hq_kept, 1)
        act.wait_ge(s.turned_hk, 1)
        act.activation(kT[:], four(7), ACT.Copy).then_inc(s.hk_kept, 1)
        yield 4 / N
        act.wait_ge(s.sums, 1)
        act.activation(bT[:], four(6), ACT.Copy).then_inc(s.b_kept, 1)
        for l in range(LEVELS):
            yield (6.5 + 2 * l) / N
            act.wait_ge(s.diffs, l + 1)
            act.wait_ge(s.e_diffs, l + 1)
            act.activation(E[:, l % 2], E[:, l % 2], ACT.Exp).then_inc(s.h_exps, 1)
            if l == 0:
                yield 7.2 / N
                act.wait_ge(s.e_in, 1)
                act.activation(ke[:], ke[:], ACT.Exp)
                act.drain()
                act.activation(qe[:], bT[:], ACT.Exp)
                act.activation(dec[:], bT[:, :, P - 1], ACT.Exp).then_inc(s.e_out, 1)
        yield 23.5 / N
        act.wait_ge(s.ke_t, 1)
        act.activation(ktok[:], four(7), ACT.Copy).then_inc(s.ktok_done, 1)
        yield 24.5 / N
        act.wait_ge(s.ho_ps, 1)
        act.activation(y[:], four(6), ACT.Copy)
        act.drain()
        for h in range(H):
            act.activation(E[:, 0, h], y[:, h], ACT.Square, accum_out=ss[:, h:h + 1])
        act.drain().then_inc(s.sqd, 1)
        rstd(act, c, ss[:], BD).then_inc(s.rs, 1)

    def gpsimd(pool):

        def diffs(l):
            e0, b0 = halves(E[:, l % 2], l)[0], halves(bT[:], l)[0]
            if l >= 2:
                pool.wait_ge(s.pairs, l)
            pool.tensor_tensor(e0, joint(l), b0, ALU.subtract).then_inc(s.e_diffs, 1)

        def tilde(l):
            e0 = halves(E[:, l % 2], l)[0]
            pool.wait_ge(s.h_exps, l + 1)
            pool.tensor_tensor(e0, e0, halves(kT[:], l)[0], ALU.mult).then_inc(s.e_tilde, 1)

        yield 6 / N
        pool.wait_ge(s.b_kept, 1)
        diffs(0)
        pool.tensor_tensor(ke[:], spread(bT[:, :, P - 1], 2, P), bT[:], ALU.subtract).then_inc(s.e_in, 1)
        for l in range(LEVELS):
            if l + 1 < LEVELS:
                yield (7 + 2 * l) / N
                diffs(l + 1)
            yield (7.5 + 2 * l) / N
            tilde(l)
        yield 20 / N
        pool.wait_ge(s.e_out, 1)
        pool.tensor_tensor(ke[:], ke[:], kT[:], ALU.mult)
        pool.tensor_tensor(qe[:], qe[:], qT[:], ALU.mult)
        pool.drain().then_inc(s.ee_done, 1)
        yield 25 / N
        y2 = y[:].rearrange("p h d -> p (h d)")
        pool.wait_ge(s.sqd, 1)
        pool.tensor_tensor(y2, y2, g[:], ALU.mult)
        pool.drain()
        pool.tensor_tensor(y2, y2, x[:, 3], ALU.mult)
        pool.wait_ge(s.rs, 1)
        pool.drain()
        pool.tensor_tensor(y[:], y[:], spread(ss[:], 2, BD), ALU.mult).then_inc(s.hy_done, 1)

    def vector(dve):
        yield 2 / N
        dve.wait_ge(s.sigs, 1)
        f = x[:, 1]
        dve.tensor_tensor(f, f, lb[:, 1], ALU.mult)
        dve.drain()
        dve.tensor_tensor(f, f, lb[:, 0], ALU.add)
        dve.drain()
        dve.tensor_scalar(k[:], f, -1.0, 1.0, ALU.mult, ALU.add)
        dve.drain().then_inc(s.f_done, 1)

        def diffs(l):
            e1, b1 = halves(E[:, l % 2], l)[1], halves(bT[:], l)[1]
            if l >= 2:
                dve.wait_ge(s.pairs, l)
            dve.tensor_tensor(e1, b1, joint(l), ALU.subtract).then_inc(s.diffs, 1)

        def tilde(l):
            e1 = halves(E[:, l % 2], l)[1]
            dve.wait_ge(s.h_exps, l + 1)
            dve.tensor_tensor(e1, e1, halves(qT[:], l)[1], ALU.mult).then_inc(s.tilde, 1)

        def pick(l):
            dve.wait_ge(s.pairs, l + 2)
            dve.drain()
            dve.copy_predicated(A[:], spread(c.all[:, LEVEL[l]].bitcast(U32), 1, H), four(6 + l % 2))\
               .then_inc(s.picked, 1)

        yield 6 / N
        dve.wait_ge(s.b_kept, 1)
        diffs(0)
        dve.wait_ge(s.pairs, 1)
        dve.tensor_tensor(A[:], four(7), spread(c.ident, 1, H), ALU.mult).then_inc(s.own_set, 1)
        for l in range(LEVELS):
            if l + 1 < LEVELS:
                yield (7 + 2 * l) / N
                diffs(l + 1)
            yield (7.5 + 2 * l) / N
            tilde(l)
            if l:
                yield (8.5 + 2 * l) / N
                pick(l - 1)
        yield 22.5 / N
        pick(LEVELS - 1)
        yield 25.5 / N
        dve.wait_ge(s.up_ps, 1)
        for h in range(H):
            dve.scalar_tensor_tensor(out=state[:, h], in0=state[:, h], scalar=dec[:, h:h + 1],
                                     in1=big[:, 7, h * BD:(h + 1) * BD], op0=ALU.mult, op1=ALU.add)

    def tensor(pe):
        yield 1.5 / N
        pe.wait_ge(s.h_silus, 1)
        for h in range(H):
            m = pe.transpose(big[:, 6, h * P:(h + 1) * P], x[:, 0, h * BD:(h + 1) * BD], c.ident)
        m.then_inc(s.turned_hq, 1)
        yield 2.5 / N
        pe.wait_ge(s.f_done, 1)
        for h in range(H):
            m = pe.transpose(big[:, 7, h * P:(h + 1) * P], k[:, h * BD:(h + 1) * BD], c.ident)
        m.then_inc(s.turned_hk, 1)
        yield 3.5 / N
        pe.wait_ge(s.logf, 1)
        pe.wait_ge(s.hq_kept, 1)
        for h in range(H):
            m = pe.matmul(big[:, 6, h * P:(h + 1) * P], x[:, 1, h * BD:(h + 1) * BD], c.upto, start=True, stop=True)
        m.then_inc(s.sums, 1)
        yield 5 / N
        pe.wait_ge(s.hk_kept, 1)
        for h in range(H):
            m = pe.matmul(big[:, 7, h * P:(h + 1) * P], kT[:, h], qT[:, h], start=True, stop=True)
        m.then_inc(s.pairs, 1)
        for l in range(LEVELS):
            yield (8 + 2 * l) / N
            pe.wait_ge(s.tilde, l + 1)
            pe.wait_ge(s.e_tilde, l + 1)
            if l == 0:
                pe.wait_ge(s.b_kept, 1)
            elif l == 1:
                pe.wait_ge(s.own_set, 1)
            else:
                pe.wait_ge(s.picked, l - 1)
            for h in range(H):
                m = pe.matmul(big[:, 6 + l % 2, h * P:(h + 1) * P], E[:, l % 2, h], E[:, l % 2, h],
                              start=True, stop=True)
            m.then_inc(s.pairs, 1)
        yield 23 / N
        pe.wait_ge(s.ee_done, 1)
        pe.wait_ge(s.picked, LEVELS - 1)
        for h in range(H):
            m = pe.transpose(big[:, 7, h * P:(h + 1) * P], ke[:, h], c.ident)
        m.then_inc(s.ke_t, 1)
        yield 24 / N
        pe.wait_ge(s.picked, LEVELS)
        for h in range(H):
            v = x[:, 2, h * BD:(h + 1) * BD]
            pe.matmul(big[:, 6, h * BD:(h + 1) * BD], qe[:, h], state[:, h], start=True, stop=False)
            m = pe.matmul(big[:, 6, h * BD:(h + 1) * BD], A[:, h], v, start=False, stop=True)
        m.then_inc(s.ho_ps, 1)
        yield 25 / N
        pe.wait_ge(s.ktok_done, 1)
        for h in range(H):
            m = pe.matmul(big[:, 7, h * BD:(h + 1) * BD], ktok[:, h], x[:, 2, h * BD:(h + 1) * BD],
                          start=True, stop=True)
        m.then_inc(s.up_ps, 1)

    return {"sync": sync, "gpsimd": gpsimd, "vector": vector, "scalar": scalar, "tensor": tensor}


def second_mixers(nc, c, w, proj, mix, table, onehot):
    H, R, KEEP = 4, 128, float(TOPK)
    with ExitStack() as ctx:
        B = Buffers(nc, ctx, "ds")
        cT = B.sb("cT", [P, SEQ])
        ct = B.sb("ct", [P, TILES, R])
        ikT = B.sb("ikT", [IDX_DIM, SEQ])
        uk = B.sb("uk", [P, H, R])
        uv = B.sb("uv", [P, H, P])
        bias = B.sb("bias", [P, H, SKEW])
        big = B.ps("big", [P, 8, 512])
        with ExitStack() as early:
            E = Buffers(nc, early, "dp")
            g = E.sb("g", [P, R])
            ik = E.sb("ik", [P, TILES, IDX_DIM])
            sq = E.sb("sq", [P, TILES, R])
            ss = E.sb("ss", [P, TILES])
            rb = E.sb("rb", [BUCKETS, H])
            oh = E.sb("oh", [BUCKETS, TAB])
            tb = E.sb("tb", [H, TAB])
            load(nc, "ds_w", [(uk[:], w['w_uk_2'].rearrange("h d r -> d h r")),
                              (uv[:], w['w_uv_2'].rearrange("h r v -> r h v")), (g[:], row(w['kv_norm_g_2'])),
                              (ik[:], proj[:, E_IK:E_IK + IDX_DIM].rearrange("(t p) c -> p t c", p=P)),
                              (ct[:], proj[:, E_C:E_C + R].rearrange("(t p) c -> p t c", p=P)),
                              (rb[:], w['rel_bias_2']), (oh[:], onehot)])
            with step(nc, "squares rs normed turned kept biases bias_kept table_out bias_in ik_t ik_kept") as (block, s):

                @block.vector
                def _(dve):
                    dve.tensor_tensor(sq[:], ct[:], ct[:], ALU.mult)
                    dve.drain()
                    dve.tensor_reduce(ss[:], sq[:], AX.X, ALU.add).then_inc(s.squares, 1)
                    dve.tensor_tensor(ct[:], ct[:], spread(g[:], 1, TILES), ALU.mult)
                    dve.wait_ge(s.rs, 1)
                    dve.drain()
                    dve.tensor_tensor(ct[:], ct[:], spread(ss[:], 2, R), ALU.mult).then_inc(s.normed, 1)
                    dve.wait_ge(s.biases, 1)
                    dve.tensor_copy(tb[:].rearrange("h (a b) -> h a b", a=5), big[0:H, 0:5]).then_inc(s.bias_kept, 1)
                    dve.wait_ge(s.turned, 1)
                    dve.tensor_copy(cT[:].rearrange("p (a b) -> p a b", a=4), big[:, 0:4]).then_inc(s.kept, 1)
                    dve.wait_ge(s.ik_t, 1)
                    dve.tensor_copy(ikT[:].rearrange("p (a b) -> p a b", a=4), big[0:IDX_DIM, 4:8])\
                       .then_inc(s.ik_kept, 1)

                @block.scalar
                def _(act):
                    act.wait_ge(s.squares, 1)
                    rstd(act, c, ss[:], R).then_inc(s.rs, 1)

                @block.tensor
                def _(pe):
                    for k in range(5):
                        m = pe.matmul(big[0:H, k], rb[:], oh[:, k * 512:(k + 1) * 512], start=True, stop=True)
                    m.then_inc(s.biases, 1)
                    pe.wait_ge(s.bias_kept, 1)
                    pe.wait_ge(s.normed, 1)
                    for t in range(TILES):
                        m = pe.transpose(big[:, t // 4, (t % 4) * P:(t % 4 + 1) * P], ct[:, t], c.ident)
                    m.then_inc(s.turned, 1)
                    for t in range(TILES):
                        m = pe.transpose(big[0:IDX_DIM, 4 + t // 4, (t % 4) * P:(t % 4 + 1) * P], ik[:, t], c.ident)
                    m.then_inc(s.ik_t, 1)

                @block.sync
                def _(sp):
                    sp.wait_ge(s.bias_kept, 1)
                    sp.dma_start(table, tb[:]).then_inc(s.table_out, 16)
                    sp.wait_ge(s.table_out, 16)
                    sp.dma_start(bias[:], bass.AP(tensor=table.tensor, offset=0,
                                                  ap=[[1, P], [TAB, H], [1, SKEW]])).then_inc(s.bias_in, 16)
                    sp.wait_ge(s.bias_in, 16)

        FL = SKEW // 8
        with step(nc, "flipped copied") as (block, s):

            @block.tensor
            def _(pe):
                for n in range(8 * H):
                    if n >= 8:
                        pe.wait_ge(s.copied, n - 7)
                    pe.matmul(big[:, n % 8, 0:FL], c.all[:, FLIP], bias[:, n // 8, n % 8 * FL:(n % 8 + 1) * FL],
                              start=True, stop=True).then_inc(s.flipped, 1)

            @block.vector
            def _(dve):
                for n in range(8 * H):
                    dve.wait_ge(s.flipped, n + 1)
                    dve.tensor_copy(bias[:, n // 8, n % 8 * FL:(n % 8 + 1) * FL], big[:, n % 8, 0:FL])\
                       .then_inc(s.copied, 1)

        score = B.sb("score", [P, 2, SEQ])
        sel = B.sb("sel", [P, 2, SEQ])
        ib = index_buffers(B, ikT, score)
        tb = threshold_buffers(B, score, sel)
        ab = attend_buffers(B, cT, ct, uk, uv, bias, sel)
        hb = hgrn_buffers(B, big)
        hgrn_setup(nc, w, hb)
        for k in range(TILES + 2):
            names, branches = "", []
            if k < TILES:
                names += INDEX_SIGNALS + HGRN_SIGNALS
            if 1 <= k <= TILES:
                names += SELECT_SIGNALS
            if k >= 2:
                names += ATTEND_SIGNALS
            with step(nc, names) as (block, s):
                if k < TILES:
                    branches.append(index_scores(c, ib, s, proj, big, k))
                if 1 <= k <= TILES:
                    branches.append(select_keys(c, tb, s, k - 1))
                if k >= 2:
                    branches.append(attend(c, ab, s, proj, mix, big, k - 2))
                if k < TILES:
                    branches.append(hgrn_chunk(c, hb, s, proj, mix, k))

                @block.sync
                def _(sp):
                    together(sp, "sync", branches)

                @block.gpsimd
                def _(pool):
                    together(pool, "gpsimd", branches)

                @block.scalar
                def _(act):
                    together(act, "scalar", branches)

                @block.vector
                def _(dve):
                    together(dve, "vector", branches)

                @block.tensor
                def _(pe):
                    together(pe, "tensor", branches)


def program(nc, t, consts, onehot, out):
    w = {n: (v[0] if v.shape[0] == 1 else v) for n, v in t.items()}
    out = out[0]

    def scratch(name, shape):
        return nc.dram_tensor(name, shape, F32, kind="Internal").ap()

    proj1, mixed1 = scratch("proj1", [SEQ + PAD, COLS1]), scratch("mixed1", [SEQ, MIX1])
    x2 = scratch("x2", [SEQ, D_MODEL])
    proj2, mixed2 = scratch("proj2", [SEQ, COLS2]), scratch("mixed2", [SEQ, D_MODEL])
    table = scratch("table", [HEADS, TAB])
    with ExitStack() as ctx:
        c = load_constants(nc, ctx, consts)
        with ExitStack() as own:
            B = Buffers(nc, own, "first")
            hT = B.sb("hT", [P, KD, SEQ])
            zero_rows(nc, hT, proj1)
            norm_transpose(nc, c, w['x'], w['norm_g'], hT, "n1")
            gemm(nc, c, hT, w['w_in'], proj1, COLS1, "g1", PAD)
        sgu(nc, c, w, proj1, mixed1)
        memory_attention(nc, c, w, proj1, mixed1)
        mlstm(nc, c, w, proj1, mixed1)
        fox_and_rwkv(nc, c, w, proj1, mixed1)
        with ExitStack() as own:
            B = Buffers(nc, own, "second")
            hT = B.sb("hT", [P, KD, SEQ])
            project_out(nc, c, mixed1, w['w_out'], w['x'], x2, "po", turned_out=hT)
            gemm(nc, c, hT, w['w_in_2'], proj2, COLS2, "g2", 0)
        second_mixers(nc, c, w, proj2, mixed2, table, onehot)
        project_out(nc, c, mixed2, w['w_o_2'], x2, out, "pf", ln=(w['ln_g_2'], w['ln_b_2']))


INPUTS = """x mem norm_g w_in w_out sgu_norm_g sgu_w sgu_b fox_q_g fox_k_g fox_f_b mlstm_conv_w mlstm_conv_b
mlstm_i_b mlstm_f_b mlstm_out_g rwkv_mu rwkv_w0 rwkv_w2 rwkv_a0 rwkv_a2 rwkv_k_k rwkv_k_a rwkv_r_k rwkv_ln_g
mem_norm_g mem_w_kv mem_q_g mem_k_g w_in_2 w_uk_2 w_uv_2 kv_norm_g_2 rel_bias_2 lb_logits_2 hgrn_norm_g_2 w_o_2
ln_g_2 ln_b_2""".split()


def kernel(**inputs):
    import concourse.bacc as bacc
    from concourse.bass_utils import run_bass_kernel_spmd

    nc = bacc.Bacc("TRN2", target_bir_lowering=False, num_devices=1)
    arrays, views = {}, {}
    for n in INPUTS:
        a = np.ascontiguousarray(inputs[n])
        arrays[f"in_{n}"] = a
        views[n] = nc.dram_tensor(f"in_{n}", a.shape, F32, kind="ExternalInput").ap()
    made = {"consts": shape_constants(), "onehot": bucket_table()}
    for n, a in made.items():
        arrays[n] = a
        views[n] = nc.dram_tensor(n, a.shape, F32, kind="ExternalInput").ap()
    out = nc.dram_tensor("out", [1, SEQ, D_MODEL], F32, kind="ExternalOutput").ap()
    program(nc, {n: views[n] for n in INPUTS}, views["consts"], views["onehot"], out)
    r = run_bass_kernel_spmd(nc, [arrays], core_ids=[0])
    return r.results[0]["out"]
```

```python
from contextlib import ExitStack, contextmanager

import numpy as np

import concourse.bass as bass
from concourse import mybir

F32 = mybir.dt.float32
F32R = mybir.dt.float32r
U32 = mybir.dt.uint32
I32 = mybir.dt.int32
U16 = mybir.dt.uint16
ALU = mybir.AluOpType
ACT = mybir.ActivationFunctionType
AX = mybir.AxisListType

P = 128
SEQ = 2048
TILES = SEQ // P
D_MODEL = 1024
KD = D_MODEL // P
HEADS = 4
HD = 64
GW = HEADS * HD
N_MEM = 256
RANK = 16
MIX1 = 5 * GW
EPS = 1e-6
LN_EPS = 1e-5
NEG = -1e30

A_U, A_V, A_Z = 0, 256, 512
B_Q, B_K, B_V, B_F, B_Z = 768, 1024, 1280, 1536, 1540
C_QK, C_V, C_I, C_F, C_O, C_Z = 1796, 2308, 2564, 2568, 2572, 2828
D_0 = 3084
D_R, D_WLO, D_K, D_V, D_ALO, D_Z = 0, 256, 272, 528, 784, 800
D_W = 1056
M_Q, M_Z = 4140, 4396
COLS1 = 4652
E_Q, E_C, E_IQ, E_IK, E_IW, E_G = 0, 512, 640, 1152, 1216, 1224
H_Q, H_F, H_I, H_G = 1736, 2248, 2760, 3272
COLS2 = 3784
IDX_HEADS = 8
IDX_DIM = 64
TOPK = 256
BH = 4
BD = 128
PAD = 4
GROUP = 512
LEVELS = 7
BUCKETS = 32
TAB = 2560
SKEW = SEQ


def shape_constants():
    p = np.arange(P)[:, None]
    f = np.arange(P)[None, :]
    cols = [p == f, p <= f, p < f, p > f]
    for l in range(LEVELS):
        half = 1 << l
        cols.append((p // (2 * half) == f // (2 * half)) & (p // half % 2 == 0) & (f // half % 2 == 1))
    cols.append(np.ones((P, P)))
    cols += [(p == h) & (f >= 0) for h in range(HEADS)]
    cols += [p == 2 * j + f // HD for j in range(2)]
    cols += [(p <= f) * 1.0 - (p < P // 2), (p < f) * 1.0 - (p < P // 2)]
    cols += [cols[4 + l].T for l in range(LEVELS)]
    cols += [p + f == P - 1]
    cols += [np.zeros((P, GROUP)), (f > p) * NEG, (f > p // 64 * 64 + 63) * NEG]
    return np.concatenate([c.astype(np.float32) for c in cols], axis=1)


IDENT, UPTO, BEFORE, AFTER = (slice(P * k, P * k + P) for k in range(4))
LEVEL = [slice(P * (4 + l), P * (5 + l)) for l in range(LEVELS)]
ONES = slice(P * 11, P * 12)
ROW = [slice(P * (12 + h), P * (13 + h)) for h in range(HEADS)]
PAIR = [slice(P * (16 + j), P * (17 + j)) for j in range(2)]
CENTRED, CENTRED_BEFORE = (slice(P * k, P * k + P) for k in (18, 19))
LEVEL_T = [slice(P * (20 + l), P * (21 + l)) for l in range(LEVELS)]
FLIP = slice(P * 27, P * 28)
CAUSAL0 = P * 28
CHUNKED = slice(CAUSAL0 + GROUP + P, CAUSAL0 + GROUP + 2 * P)
CONST_COLS = CAUSAL0 + GROUP + 2 * P


def bucket_table():
    rel = np.arange(TAB) - (SEQ - 1)
    nb, max_dist = BUCKETS // 2, 256
    exact = nb // 2
    n = np.abs(rel)
    nf = np.maximum(n, 1).astype(np.float32)
    large = exact + (np.log(nf / np.float32(exact)) / np.float32(np.log(max_dist / exact))
                     * np.float32(nb - exact)).astype(np.int32)
    bucket = np.where(rel > 0, nb, 0) + np.where(n < exact, n, np.minimum(large, nb - 1))
    return (np.arange(BUCKETS)[:, None] == bucket[None, :]).astype(np.float32)


@contextmanager
def step(nc, names):
    with ExitStack() as ctx:
        sems = {n: ctx.enter_context(nc.semaphore(n)) for n in names.split()}
        with nc.Block() as block:
            yield block, type("Signals", (), sems)
        for sem in sems.values():
            nc.sync.sem_clear(sem)
        nc.all_engine_barrier()


class Buffers:

    def __init__(self, nc, ctx, phase):
        self._nc, self._ctx, self._phase = nc, ctx, phase

    def sb(self, name, shape, dt=F32):
        t = self._ctx.enter_context(self._nc.sbuf_tensor(f"{self._phase}_{name}", shape, dt))
        return t

    def ps(self, name, shape):
        t = self._ctx.enter_context(self._nc.psum_tensor(f"{self._phase}_{name}", shape, F32))
        return t


def together(engine, name, branches):
    at = []
    for n, branch in enumerate(branches):
        if name in branch:
            steps = branch[name](engine)
            place = next(steps, None)
            if place is not None:
                at.append([place, n, steps])
    while at:
        first = min(at, key=lambda b: (b[0], b[1]))
        place = next(first[2], None)
        assert place is None or place >= first[0], (name, first, place)
        if place is None:
            at.remove(first)
        else:
            first[0] = place




def spread(ap, axis, n):
    shape = list(ap.shape)
    v = ap.unsqueeze(axis)
    shape.insert(axis, n)
    return v.broadcast_to(shape)


def row(ap, n=P):
    return ap.partition_broadcast(n)


def load(nc, name, pairs):
    with step(nc, "arrived") as (block, s):
        arrived = s.arrived

        @block.sync
        def _(sp):
            for dst, src in pairs:
                sp.dma_start(dst, src, allow_slow_non_contiguous=True).then_inc(arrived, 16)
            sp.wait_ge(arrived, 16 * len(pairs))


class Split:

    def __init__(self, B, name, shape):
        self.hi = B.sb(f"{name}_hi", shape, F32R)
        self.lo = B.sb(f"{name}_lo", shape, F32R)


def gemm(nc, c, hT, w, out, cols, name, pad):
    w_v = w.rearrange("(k p) n -> p k n", p=P)
    groups = [(n, min(512, cols - n)) for n in range(0, cols, 512)]
    with ExitStack() as ctx:
        B = Buffers(nc, ctx, name)
        raw = B.sb("w", [P, KD, 512])
        wt = Split(B, "ws", [P, KD, 512])
        stage = B.sb("stage", [P, 4, 512])
        acc = B.ps("acc", [P, 4, 512])
        with step(nc, "w_in w_hi w_lo w_free product act_copied dve_copied stored0 stored1 stored2 stored3") \
                as (block, s):
            stored = (s.stored0, s.stored1, s.stored2, s.stored3)
            copied = (s.act_copied, s.dve_copied)

            @block.sync
            def _(sp):
                def weights(g):
                    n0, width = groups[g]
                    for k in range(KD):
                        if g:
                            sp.wait_ge(s.w_lo, KD * (g - 1) + k + 1)
                        sp.dma_start(raw[:, k, 0:width], w_v[:, k, n0:n0 + width]).then_inc(s.w_in, 16)

                weights(0)
                for g, (n0, width) in enumerate(groups):
                    for t in range(TILES):
                        m = g * TILES + t
                        sp.wait_ge(copied[m % 2], m // 2 + 1)
                        sp.dma_start(out[pad + t * P:pad + (t + 1) * P, n0:n0 + width], stage[:, m % 4, 0:width])\
                          .then_inc(stored[m % 4], 16)
                        if t == 1 and g + 1 < len(groups):
                            weights(g + 1)
                for slot in range(4):
                    sp.wait_ge(stored[slot], 16 * TILES * len(groups) // 4)

            @block.tensor
            def _(pe):
                for g, (n0, width) in enumerate(groups):
                    for t in range(TILES):
                        m = g * TILES + t
                        if m >= 4:
                            pe.wait_ge(copied[m % 2], (m - 4) // 2 + 1)
                        tile, sums = slice(t * P, (t + 1) * P), acc[:, m % 4, 0:width]
                        for k in range(KD):
                            if t == 0:
                                pe.wait_ge(s.w_lo, KD * g + k + 1)
                            pe.matmul(sums, hT.hi[:, k, tile], wt.hi[:, k, 0:width], start=(k == 0), stop=False)
                            pe.matmul(sums, hT.hi[:, k, tile], wt.lo[:, k, 0:width], start=False, stop=False)
                            mm = pe.matmul(sums, hT.lo[:, k, tile], wt.hi[:, k, 0:width], start=False,
                                           stop=(k == KD - 1))
                            if t == TILES - 1 and k < KD - 1:
                                mm.then_inc(s.w_free, 1)
                        mm.then_inc(s.product, 1)

            def copy_out(eng, copy, m, width):
                eng.wait_ge(s.product, m + 1)
                if m >= 4:
                    eng.wait_ge(stored[m % 4], 16 * (m // 4))
                copy(stage[:, m % 4, 0:width], acc[:, m % 4, 0:width]).then_inc(copied[m % 2], 1)

            @block.scalar
            def _(act):
                for g, (n0, width) in enumerate(groups):
                    act.wait_ge(s.w_in, 16 * KD * (g + 1))
                    for k in range(KD):
                        if g and k < KD - 1:
                            act.wait_ge(s.w_free, (KD - 1) * (g - 1) + k + 1)
                        elif g:
                            act.wait_ge(s.product, TILES * g)
                        act.activation(wt.hi[:, k, 0:width], raw[:, k, 0:width], ACT.Copy).then_inc(s.w_hi, 1)
                    for t in range(0, TILES, 2):
                        copy_out(act, lambda o, i: act.activation(o, i, ACT.Copy), g * TILES + t, width)

            @block.vector
            def _(dve):
                for g, (n0, width) in enumerate(groups):
                    for k in range(KD):
                        dve.wait_ge(s.w_hi, KD * g + k + 1)
                        dve.tensor_tensor(wt.lo[:, k, 0:width], raw[:, k, 0:width],
                                          wt.hi[:, k, 0:width].bitcast(F32), ALU.subtract).then_inc(s.w_lo, 1)
                    if g:
                        copy_out(dve, dve.tensor_copy, g * TILES - 1, groups[g - 1][1])
                    for t in range(1, TILES - 1, 2):
                        copy_out(dve, dve.tensor_copy, g * TILES + t, width)
                copy_out(dve, dve.tensor_copy, TILES * len(groups) - 1, groups[-1][1])


def norm_transpose(nc, c, x, gain, hT, name, tiles=TILES):
    U = min(4, tiles)
    sets = tiles // U
    split = isinstance(hT, Split)
    with ExitStack() as ctx:
        B = Buffers(nc, ctx, name)
        xt = B.sb("xt", [P, 2, U, D_MODEL])
        sq = B.sb("sq", [P, D_MODEL])
        ss = B.sb("ss", [P, 2, U])
        g = B.sb("g", [P, KD])
        full = B.sb("full", [P, 2, KD // 2, P])
        tp = B.ps("tp", [P, 4, KD // 2, P])

        def place(t, v):
            return t[:, 4 * (v % 2):4 * (v % 2) + 4, v // 2 * P:(v // 2 + 1) * P]

        with step(nc, "g_in x_in0 x_in1 rs normed turned copied rounded rest") as (block, s):
            x_in = (s.x_in0, s.x_in1)

            @block.sync
            def _(sp):
                for b in range(sets):
                    if b >= 2:
                        sp.wait_ge(s.turned, 2 * U * (b - 1))
                    for u in range(U):
                        t = b * U + u
                        sp.dma_start(xt[:, b % 2, u], x[t * P:(t + 1) * P, :]).then_inc(x_in[b % 2], 16)
                    if b == 0:
                        sp.dma_start(g[:], gain.rearrange("(k p) -> p k", p=P), allow_slow_non_contiguous=True)\
                          .then_inc(s.g_in, 16)

            @block.scalar
            def _(act):
                def norms(b):
                    act.wait_ge(x_in[b % 2], 16 * U * (b // 2 + 1))
                    for u in range(U):
                        act.activation(sq[:], xt[:, b % 2, u], ACT.Square, accum_out=ss[:, b % 2, u:u + 1])
                        act.drain()
                    act.activation(ss[:, b % 2], ss[:, b % 2], ACT.Ln, scale=1.0 / D_MODEL, bias=c.eps[:, 0:1])
                    act.drain()
                    act.activation(ss[:, b % 2], ss[:, b % 2], ACT.Exp, scale=-0.5).then_inc(s.rs, 1)

                norms(0)
                for b in range(sets):
                    if b + 1 < sets:
                        if b >= 1:
                            act.wait_ge(s.normed, U * b)
                        norms(b + 1)
                    for v in range(2 * U * b, 2 * U * (b + 1) if split else 0):
                        act.wait_ge(s.copied, v + 1)
                        act.activation(place(hT.hi, v), full[:, v % 2], ACT.Copy).then_inc(s.rounded, 1)

            @block.vector
            def _(dve):
                dve.wait_ge(s.g_in, 16)
                for b in range(sets):
                    dve.wait_ge(s.rs, b + 1)
                    for u in range(U):
                        dve.tensor_scalar(xt[:, b % 2, u], xt[:, b % 2, u], ss[:, b % 2, u:u + 1], None, ALU.mult)\
                           .then_inc(s.normed, 1)
                    for v in range(2 * U * b, 2 * U * (b + 1)):
                        dve.wait_ge(s.turned, v + 1)
                        if split and v >= 2:
                            dve.wait_ge(s.rest, v - 1)
                        half = v % 2
                        dve.tensor_tensor(full[:, half] if split else place(hT, v), tp[:, v % 4],
                                          spread(g[:, 4 * half:4 * half + 4], 2, P), ALU.mult).then_inc(s.copied, 1)

            @block.gpsimd
            def _(pool):
                for v in range(2 * tiles if split else 0):
                    pool.wait_ge(s.rounded, v + 1)
                    pool.tensor_tensor(place(hT.lo, v), full[:, v % 2], place(hT.hi, v).bitcast(F32),
                                       ALU.subtract).then_inc(s.rest, 1)

            @block.tensor
            def _(pe):
                for v in range(2 * tiles):
                    t, half = v // 2, v % 2
                    pe.wait_ge(s.normed, t + 1)
                    if v >= 4:
                        pe.wait_ge(s.copied, v - 3)
                    for k in range(4):
                        kk = 4 * half + k
                        m = pe.transpose(tp[:, v % 4, k], xt[:, t // U % 2, t % U, kk * P:(kk + 1) * P], c.ident)
                    m.then_inc(s.turned, 1)


class Named:
    pass


def load_constants(nc, ctx, consts):
    c = Named()
    t = ctx.enter_context(nc.sbuf_tensor("consts_sb", [P, CONST_COLS], F32))
    e = ctx.enter_context(nc.sbuf_tensor("eps_sb", [P, 2], F32))
    c.all, c.eps = t, e
    c.ident, c.upto, c.before, c.after, c.ones = (t[:, k] for k in (IDENT, UPTO, BEFORE, AFTER, ONES))
    with step(nc, "const_in eps_set") as (block, s):

        @block.sync
        def _(sp):
            sp.dma_start(t[:], consts).then_inc(s.const_in, 16)
            sp.wait_ge(s.const_in, 16)

        @block.vector
        def _(dve):
            dve.memset(e[:, 0:1], EPS).then_inc(s.eps_set, 1)
            dve.memset(e[:, 1:2], LN_EPS).then_inc(s.eps_set, 1)
            dve.wait_ge(s.eps_set, 2)
    return c


def tokens(ap, i, n, c0, c1, pad=0):
    return ap[bass.ds(i * P + pad, n * P), c0:c1].rearrange("(u p) c -> p u c", p=P)


def rstd(act, c, ss, width):
    act.drain()
    act.activation(ss, ss, ACT.Ln, scale=1.0 / width, bias=c.eps[:, 0:1])
    act.drain()
    return act.activation(ss, ss, ACT.Exp, scale=-0.5)


SGU_SIGNALS = "gx_ahead gelus gsquares grs gnormed gmixes gy_done gsilus gstored "
SGU_TILES = 4


def sgu_buffers(nc, c, B, w):
    b = Named()
    U = SGU_TILES
    b.wt = B.sb("gwt", [P, HEADS, P])
    b.wT = B.sb("gwT", [P, HEADS, P])
    b.b = B.sb("gb", [P, HEADS])
    b.g = B.sb("gg", [P, GW])
    b.x = B.sb("gx", [P, 2, U, 3 * GW])
    b.sq = B.sb("gsq", [P, U, GW])
    b.ss = B.sb("gss", [P, U * HEADS])
    b.tp = B.ps("gtp", [P, HEADS, P])
    b.mx = B.ps("gmx", [P, HEADS, U * HD])
    load(nc, "sgu_w", [(b.wt[:], w['sgu_w'].rearrange("g t s -> t g s")),
                       (b.b[:], w['sgu_b'].rearrange("g t -> t g")), (b.g[:], row(w['sgu_norm_g']))])
    with step(nc, "turned masked") as (block, s):

        @block.tensor
        def _(pe):
            for h in range(HEADS):
                t = pe.transpose(b.tp[:, h], b.wt[:, h], c.ident)
            t.then_inc(s.turned, 1)

        @block.vector
        def _(dve):
            dve.wait_ge(s.turned, 1)
            dve.tensor_tensor(b.wT[:], b.tp[:], spread(c.upto, 1, HEADS), ALU.mult).then_inc(s.masked, 1)
    return b


def sgu_loads(b, sp, arrived, proj, i):
    sp.dma_start(b.x[:, i % 2], tokens(proj, i * SGU_TILES, SGU_TILES, A_U, A_U + 3 * GW, PAD)).then_inc(arrived, 16)
    return 16


def sgu(c, B, s, proj, mixed, i):
    U = SGU_TILES
    x, wT, b, g, sq, ss, mx = B.x[:, i % 2], B.wT, B.b, B.g, B.sq, B.ss, B.mx
    u, v, z = (x[:, :, k * GW:(k + 1) * GW] for k in range(3))
    vh = v.rearrange("p u (h d) -> p u h d", h=HEADS)

    def sync(sp):
        if (i + 1) * U < TILES:
            yield 0.0
            n = sgu_loads(B, sp, s.gx_ahead, proj, i + 1)
            yield 0.99
            sp.wait_ge(s.gx_ahead, n)
        yield 1.0
        sp.wait_ge(s.gy_done, 1)
        sp.dma_start(tokens(mixed, i * U, U, 0, GW), u).then_inc(s.gstored, 16)
        sp.wait_ge(s.gstored, 16)

    def scalar(act):
        yield 0.0
        act.activation(x[:, :, 0:2 * GW], x[:, :, 0:2 * GW], ACT.Gelu_apprx_tanh).then_inc(s.gelus, 1)
        act.activation(z, z, ACT.Silu).then_inc(s.gsilus, 1)
        yield 0.3
        act.wait_ge(s.gsquares, 1)
        rstd(act, c, ss[:], HD).then_inc(s.grs, 1)

    def vector(dve):
        yield 0.2
        dve.wait_ge(s.gelus, 1)
        dve.tensor_tensor(sq[:], v, v, ALU.mult)
        dve.drain()
        dve.tensor_reduce(ss[:], sq[:].rearrange("p u (h d) -> p (u h) d", h=HEADS), AX.X, ALU.add)\
           .then_inc(s.gsquares, 1)
        dve.tensor_tensor(v, v, spread(g[:], 1, U), ALU.mult)
        yield 0.45
        dve.wait_ge(s.grs, 1)
        dve.drain()
        dve.tensor_tensor(vh, vh, spread(ss[:].rearrange("p (u h) -> p u h", u=U), 3, HD), ALU.mult)\
           .then_inc(s.gnormed, 1)
        yield 0.8
        dve.wait_ge(s.gmixes, 1)
        for h in range(HEADS):
            cols = slice(h * HD, (h + 1) * HD)
            dve.scalar_tensor_tensor(out=u[:, :, cols], in0=mx[:, h].rearrange("p (u d) -> p u d", u=U),
                                     scalar=b[:, h:h + 1], in1=u[:, :, cols], op0=ALU.add, op1=ALU.mult)
        dve.wait_ge(s.gsilus, 1)
        dve.drain()
        dve.tensor_tensor(u, u, z, ALU.mult).then_inc(s.gy_done, 1)

    def tensor(pe):
        yield 0.6
        pe.wait_ge(s.gnormed, 1)
        for h in range(HEADS):
            m = pe.matmul(mx[:, h].rearrange("p (u d) -> p u d", u=U), wT[:, h],
                          v.rearrange("p u (h d) -> p h u d", h=HEADS)[:, h], start=True, stop=True)
        m.then_inc(s.gmixes, 1)

    return {"sync": sync, "scalar": scalar, "vector": vector, "tensor": tensor}


def memory_buffers(nc, c, B, w):
    MT = N_MEM // P
    kT = B.sb("kT", [HD, HEADS, N_MEM])
    vm = B.sb("vm", [P, MT, GW])
    gq = B.sb("gq", [P, HD])
    gk = B.sb("gk", [P, HD])
    load(nc, "mem_g", [(gq[:], row(w['mem_q_g'])), (gk[:], row(w['mem_k_g']))])
    with ExitStack() as early:
        E = Buffers(nc, early, "memkv")
        hT = E.sb("hT", [P, KD, N_MEM])
        norm_transpose(nc, c, w['mem'], w['mem_norm_g'], hT, "nm", tiles=MT)
        wk = E.sb("wk", [P, KD, 2 * GW])
        k = E.sb("k", [P, MT, HEADS, HD])
        sq = E.sb("sq", [P, MT, HEADS, HD])
        ss = E.sb("ss", [P, MT, HEADS])
        acc = E.ps("acc", [P, MT, 2 * GW])
        tp = E.ps("tp", [P, HEADS, N_MEM])
        with step(nc, "w_in prods split squares rs normed turned kept") as (block, s):

            @block.sync
            def _(sp):
                sp.dma_start(wk[:], w['mem_w_kv'].rearrange("(k p) n -> p k n", p=P)).then_inc(s.w_in, 16)

            @block.tensor
            def _(pe):
                pe.wait_ge(s.w_in, 16)
                for t in range(MT):
                    for j in range(KD):
                        m = pe.matmul(acc[:, t], hT[:, j, t * P:(t + 1) * P], wk[:, j], start=(j == 0),
                                      stop=(j == KD - 1))
                m.then_inc(s.prods, 1)
                pe.wait_ge(s.normed, 1)
                for t in range(MT):
                    for h in range(HEADS):
                        m = pe.transpose(tp[0:HD, h, t * P:(t + 1) * P], k[:, t, h], c.ident)
                m.then_inc(s.turned, 1)

            @block.scalar
            def _(act):
                act.wait_ge(s.squares, 1)
                rstd(act, c, ss[:], HD).then_inc(s.rs, 1)

            @block.vector
            def _(dve):
                dve.wait_ge(s.prods, 1)
                dve.tensor_copy(k[:], acc[:, :, 0:GW].rearrange("p t (h d) -> p t h d", h=HEADS))
                dve.tensor_copy(vm[:], acc[:, :, GW:2 * GW])
                dve.drain()
                dve.tensor_tensor(sq[:], k[:], k[:], ALU.mult)
                dve.drain()
                dve.tensor_reduce(ss[:], sq[:], AX.X, ALU.add).then_inc(s.squares, 1)
                dve.wait_ge(s.rs, 1)
                dve.tensor_tensor(k[:], k[:], spread(ss[:], 3, HD), ALU.mult)
                dve.drain()
                kk = k[:].rearrange("p t h d -> p (t h) d")
                dve.tensor_tensor(kk, kk, spread(gk[:], 1, MT * HEADS), ALU.mult).then_inc(s.normed, 1)
                dve.wait_ge(s.turned, 1)
                dve.tensor_copy(kT[:], tp[0:HD]).then_inc(s.kept, 1)

    b = Named()
    b.kT, b.vm, b.gq = kT, vm, gq
    b.qz = B.sb("qz", [P, 2, 2 * GW])
    b.sq = B.sb("sqq", [P, GW])
    b.ss = B.sb("ss", [P, HEADS])
    b.qT = B.sb("qT", [HD, HEADS, P])
    b.pr = B.sb("pr", [P, HEADS, N_MEM])
    b.mx = B.sb("mx", [P, HEADS])
    b.den = B.sb("den", [P, HEADS])
    b.pT = B.sb("pT", [P, HEADS, MT, P])
    return b


def zero_rows(nc, proj):
    with ExitStack() as own:
        zeros = Buffers(nc, own, "zr").sb("zeros", [PAD, COLS1])
        with step(nc, "zeroed stored") as (block, s):

            @block.vector
            def _(dve):
                dve.memset(zeros[:], 0.0).then_inc(s.zeroed, 1)

            @block.sync
            def _(sp):
                sp.wait_ge(s.zeroed, 1)
                sp.dma_start(proj[0:PAD, :], zeros[:]).then_inc(s.stored, 16)
                sp.wait_ge(s.stored, 16)


FOX_SIGNALS = "z_ahead z_silus logits f_added f_maxed f_exps f_turned f_kept f_weighed fy_done "


def fox_rwkv_and_gating(nc, c, w, proj, mixed):
    A = HD + 1
    with ExitStack() as ctx:
        B = Buffers(nc, ctx, "fox")
        qT = B.sb("qT", [A, HEADS, SEQ])
        kT = B.sb("kT", [A, HEADS, SEQ])
        v = B.sb("v", [P, TILES, GW])
        gq = B.sb("gq", [P, 2, HD])
        fb = B.sb("fb", [P, HEADS])
        carry = B.sb("carry", [1, HEADS])
        load(nc, "fox_g", [(gq[:, 0], row(w['fox_q_g'])), (gq[:, 1], row(w['fox_k_g'])), (fb[:], row(w['fox_f_b'])),
                           (v[:], proj[PAD:, B_V:B_V + GW].rearrange("(t p) c -> p t c", p=P))])
        with step(nc, "scaled cleared") as (block, s):

            @block.vector
            def _(dve):
                dve.tensor_scalar(gq[:, 0], gq[:, 0], HD ** -0.5, None, ALU.mult).then_inc(s.scaled, 1)
                dve.memset(carry[:], 0.0).then_inc(s.cleared, 1)

        with ExitStack() as early:
            E = Buffers(nc, early, "foxq")
            pb = fox_prepare_buffers(E, qT, kT, gq, fb, carry)
            ub = sgu_buffers(nc, c, E, w)
            with step(nc, "arrived") as (block, s):

                @block.sync
                def _(sp):
                    n = fox_prepare_loads(pb, sp, s.arrived, proj, 0) + sgu_loads(ub, sp, s.arrived, proj, 0)
                    sp.wait_ge(s.arrived, n)

            for i in range(TILES // SGU_TILES):
                with step(nc, PREPARE_SIGNALS + SGU_SIGNALS) as (block, s):
                    branches = [fox_prepare(c, pb, s, proj, i), sgu(c, ub, s, proj, mixed, i)]

                    @block.sync
                    def _(sp):
                        together(sp, "sync", branches)

                    @block.scalar
                    def _(act):
                        together(act, "scalar", branches)

                    @block.vector
                    def _(dve):
                        together(dve, "vector", branches)

                    @block.tensor
                    def _(pe):
                        together(pe, "tensor", branches)

        big = B.ps("big", [P, 8, 512])
        fb = fox_buffers(B, qT, kT, v, big)
        rb = rwkv_buffers(nc, B, w, big)
        with step(nc, "arrived") as (block, s):

            @block.sync
            def _(sp):
                sp.dma_start(fb.z[:, 0], proj[PAD:P + PAD, B_Z:B_Z + GW]).then_inc(s.arrived, 16)
                n = rwkv_loads(rb, sp, s.arrived, proj, 0)
                sp.wait_ge(s.arrived, 16 + n)

        for k in range(TILES + 2):
            names, branches = "stored ", []
            if 1 <= k <= TILES:
                names += RWKV_BACK_SIGNALS
            if k < TILES:
                names += RWKV_FRONT_SIGNALS + FOX_SIGNALS
            with step(nc, names) as (block, s):
                if k < TILES:
                    branches.append(rwkv_front(c, rb, s, proj, k))
                if 1 <= k <= TILES:
                    branches.append(rwkv_back(c, rb, s, k - 1))
                if k < TILES:
                    branches.append(fox_attend(c, fb, s, proj, k))

                @block.sync
                def _(sp):
                    stores = 0
                    if 1 <= k <= TILES:
                        sp.dma_start(mixed[(k - 1) * P:k * P, GW:2 * GW],
                                     fb.y[:, (k - 1) % 2].rearrange("p h d -> p (h d)")).then_inc(s.stored, 16)
                        stores += 1
                    if k >= 2:
                        sp.dma_start(mixed[(k - 2) * P:(k - 1) * P, 3 * GW:4 * GW],
                                     rb.y[:, k % 2].rearrange("p h d -> p (h d)")).then_inc(s.stored, 16)
                        stores += 1
                    together(sp, "sync", branches)
                    if stores:
                        sp.wait_ge(s.stored, 16 * stores)

                @block.scalar
                def _(act):
                    together(act, "scalar", branches)

                @block.vector
                def _(dve):
                    together(dve, "vector", branches)

                @block.tensor
                def _(pe):
                    together(pe, "tensor", branches)


def in_turn(banks, uses):
    n = len(banks)
    return {key: (banks[i % n], uses[i - n][1] if i >= n else None) for i, (key, over) in enumerate(uses)}


def fox_buffers(B, qT, kT, v, big):
    b = Named()
    b.qT, b.kT, b.v, b.big = qT, kT, v, big
    b.z = B.sb("z", [P, 2, GW])
    b.L = B.sb("L", [P, 2, SEQ])
    b.mx = B.sb("mx", [P, HEADS, 4])
    b.top = B.sb("top", [P, HEADS])
    b.den = B.sb("den", [P, HEADS])
    b.pT = B.sb("pT", [P, 2, 4, P])
    b.y = B.sb("y", [P, 2, HEADS, HD])
    return b


def fox_attend(c, b, s, proj, k):
    W = (k + 1) * P
    L, mx, top, den, pT, z, y, big = b.L, b.mx, b.top, b.den, b.pT, b.z[:, k % 2], b.y[:, k % 2], b.big
    PIECES = [(x, min(512, W - x)) for x in range(0, W, 512)]
    NP = len(PIECES)
    o = big[:, 7, 0:GW].rearrange("p (h d) -> p h d", h=HEADS)
    N = 12.0
    at_logits = lambda h, p: (0.3 + 2 * h + 1.6 * p / NP) / N
    at_exp = lambda h: (2.1 + 2 * h) / N
    at_turn = lambda h, p: (2.3 + 2 * h + 1.6 * (p + 0.5) / NP) / N
    pitch = 1.6 / NP / N
    uses = []
    for h in range(HEADS + 1):
        for p in range(NP):
            if h < HEADS:
                uses.append((("L", h, p), (s.f_added, h * NP + p + 1)))
            if h:
                uses.append((("T", h - 1, p), (s.f_kept, (h - 1) * NP + p + 1)))
    turns = in_turn([5, 6], uses)

    def take(pe, *key):
        n, before = turns[key]
        if before:
            pe.wait_ge(*before)
        return n

    def sync(sp):
        if k + 1 < TILES:
            yield 0.02
            sp.dma_start(b.z[:, (k + 1) % 2], proj[(k + 1) * P + PAD:(k + 2) * P + PAD, B_Z:B_Z + GW])\
              .then_inc(s.z_ahead, 16)
            yield 0.9
            sp.wait_ge(s.z_ahead, 16)

    def scalar(act):
        yield 5.5 / 80
        act.activation(z, z, ACT.Silu).then_inc(s.z_silus, 1)
        for h in range(HEADS):
            if h:
                yield from keep(act, h - 1)
            yield at_exp(h)
            act.wait_ge(s.f_maxed, h + 1)
            act.activation(L[:, h % 2, 0:W], L[:, h % 2, 0:W], ACT.Exp, bias=top[:, h:h + 1],
                           accum_out=den[:, h:h + 1]).then_inc(s.f_exps, 1)
        yield from keep(act, HEADS - 1)

    def keep(act, h):
        for p, (x, wd) in enumerate(PIECES):
            n = h * NP + p
            yield at_turn(h, p) + 0.3 * pitch
            act.wait_ge(s.f_turned, n + 1)
            if n >= 2:
                act.wait_ge(s.f_weighed, n - 1)
            act.activation(pT[:, n % 2, 0:wd // P],
                           big[:, turns["T", h, p][0], 0:wd].rearrange("p (b t) -> p b t", t=P), ACT.Copy)\
               .then_inc(s.f_kept, 1)

    def vector(dve):
        for h in range(HEADS):
            for p, (x, wd) in enumerate(PIECES):
                yield at_logits(h, p) + 0.4 * pitch
                dve.wait_ge(s.logits, h * NP + p + 1)
                if p == 0 and h >= 2:
                    dve.wait_ge(s.f_turned, (h - 1) * NP)
                last = x + wd == W
                m0 = CAUSAL0 + (GROUP + P - wd if last else 0)
                dve.tensor_tensor_reduce(L[:, h % 2, x:x + wd], big[:, turns["L", h, p][0], 0:wd],
                                         c.all[:, m0:m0 + wd], 1.0, 4 * NEG, ALU.add, ALU.max,
                                         mx[:, h, p:p + 1]).then_inc(s.f_added, 1)
            yield at_exp(h)
            dve.drain()
            dve.tensor_reduce(top[:, h:h + 1], mx[:, h, 0:NP], AX.X, ALU.max)
            dve.drain()
            dve.tensor_scalar(top[:, h:h + 1], top[:, h:h + 1], -1.0, None, ALU.mult).then_inc(s.f_maxed, 1)
        yield 11 / N
        dve.wait_ge(s.f_exps, HEADS)
        dve.reciprocal(den[:], den[:])
        dve.wait_ge(s.f_weighed, HEADS * NP)
        dve.wait_ge(s.z_silus, 1)
        dve.drain()
        dve.tensor_tensor(y, o, spread(den[:], 2, HD), ALU.mult)
        dve.drain()
        y2 = y.rearrange("p h d -> p (h d)")
        dve.tensor_tensor(y2, y2, z, ALU.mult).then_inc(s.fy_done, 1)

    def tensor(pe):
        for h in range(HEADS + 1):
            for p in range(NP):
                if h < HEADS:
                    yield at_logits(h, p)
                    x, wd = PIECES[p]
                    n = take(pe, "L", h, p)
                    pe.matmul(big[:, n, 0:wd], b.qT[:, h, k * P:(k + 1) * P], b.kT[:, h, x:x + wd], start=True,
                              stop=True).then_inc(s.logits, 1)
                if h:
                    yield at_turn(h - 1, p)
                    if p == 0:
                        pe.wait_ge(s.f_exps, h)
                    turn(pe, h - 1, p)
                    if p:
                        weigh(pe, h - 1, p - 1)
            if h:
                yield at_turn(h - 1, NP - 1) + 0.35 * pitch
                weigh(pe, h - 1, NP - 1)

    def turn(pe, h, p):
        x, wd = PIECES[p]
        n = take(pe, "T", h, p)
        for t in range(wd // P):
            m = pe.transpose(big[:, n, t * P:(t + 1) * P], L[:, h % 2, x + t * P:x + (t + 1) * P], c.ident)
        m.then_inc(s.f_turned, 1)

    def weigh(pe, h, p):
        x, wd = PIECES[p]
        pe.wait_ge(s.f_kept, h * NP + p + 1)
        for t in range(wd // P):
            m = pe.matmul(o[:, h], pT[:, (h * NP + p) % 2, t], b.v[:, x // P + t, h * HD:(h + 1) * HD],
                          start=(p == 0 and t == 0), stop=(x + (t + 1) * P == W))
        m.then_inc(s.f_weighed, 1)

    return {"sync": sync, "scalar": scalar, "vector": vector, "tensor": tensor}


PREPARE_SIGNALS = "p_ahead squares rs logf sums carried aug_done turned q_kept k_kept biased "


def fox_prepare_buffers(E, qT, kT, gq, fb, carry):
    U = SGU_TILES
    b = Named()
    b.qT, b.kT, b.gq, b.fb, b.carry = qT, kT, gq, fb, carry
    b.x = E.sb("x", [P, 2, U, 2, HEADS, HD])
    b.f = E.sb("f", [P, 2, U, HEADS])
    b.aug = E.sb("aug", [P, U, 2, HEADS, HD + 1])
    b.sq = E.sb("sq", [P, U, 2 * GW])
    b.ss = E.sb("ss", [P, U, 2, HEADS])
    b.cum = E.ps("cum", [P, U, HEADS])
    b.tot = E.ps("tot", [1, U, HEADS])
    b.tp = E.ps("tp", [P, 2, HEADS, P])
    return b


def fox_prepare_loads(b, sp, arrived, proj, i):
    U = SGU_TILES
    sp.dma_start(b.x[:, i % 2].rearrange("p u a h d -> p u (a h d)"), tokens(proj, i * U, U, B_Q, B_Q + 2 * GW, PAD))\
      .then_inc(arrived, 16)
    sp.dma_start(b.f[:, i % 2], tokens(proj, i * U, U, B_F, B_F + HEADS, PAD)).then_inc(arrived, 16)
    return 32


def fox_prepare(c, b, s, proj, i):
    U, A = SGU_TILES, HD + 1
    x, f = b.x[:, i % 2], b.f[:, i % 2]
    aug, sq, ss, cum, tot, tp, carry, qT, kT, gq, fb = (b.aug, b.sq, b.ss, b.cum, b.tot, b.tp, b.carry, b.qT, b.kT,
                                                        b.gq, b.fb)

    def sync(sp):
        if (i + 1) * U < TILES:
            yield 0.0
            n = fox_prepare_loads(b, sp, s.p_ahead, proj, i + 1)
            yield 0.98
            sp.wait_ge(s.p_ahead, n)

    def scalar(act):
        yield 0.05
        act.wait_ge(s.biased, 1)
        act.activation(f, f, ACT.Exp, scale=-1.0)
        act.drain()
        act.activation(f, f, ACT.Ln, bias=c.ones[:, 0:1]).then_inc(s.logf, 1)
        act.wait_ge(s.squares, 1)
        rstd(act, c, ss[:], HD).then_inc(s.rs, 1)
        for u in range(U):
            yield 0.5 + 0.1 * u
            act.wait_ge(s.turned, u + 1)
            act.activation(qT[:, :, (i * U + u) * P:(i * U + u + 1) * P], tp[0:A, 0], ACT.Copy).then_inc(s.q_kept, 1)

    def vector(dve):
        yield 0.0
        dve.tensor_tensor(f, f, spread(fb[:], 1, U), ALU.add).then_inc(s.biased, 1)
        x2 = x.rearrange("p u a h d -> p u (a h d)")
        dve.tensor_tensor(sq[:], x2, x2, ALU.mult)
        dve.memset(aug[:, :, 0, :, HD:A], 1.0)
        dve.drain()
        dve.tensor_reduce(ss[:].rearrange("p u a h -> p (u a h)"), sq[:].rearrange("p u (x d) -> p (u x) d", d=HD),
                          AX.X, ALU.add).then_inc(s.squares, 1)
        yield 0.1
        for u in range(U):
            for a in range(2):
                dve.tensor_tensor(x[:, u, a], x[:, u, a], spread(gq[:, a], 1, HEADS), ALU.mult)
        yield 0.2
        for u in range(U):
            dve.wait_ge(s.sums, u + 1)
            dve.tensor_copy(aug[:, u, 1, :, HD:A].rearrange("p h o -> p (h o)"), cum[:, u])
            dve.tensor_tensor(carry[:], carry[:], tot[:, u], ALU.add)
            dve.drain().then_inc(s.carried, 1)
        yield 0.4
        dve.wait_ge(s.rs, 1)
        dve.drain()
        for u in range(U):
            for a in range(2):
                dve.tensor_tensor(aug[:, u, a, :, 0:HD], x[:, u, a], spread(ss[:, u, a], 2, HD), ALU.mult)
            dve.drain().then_inc(s.aug_done, 1)
        for u in range(U):
            yield 0.5 + 0.1 * u
            dve.wait_ge(s.turned, u + 1)
            dve.tensor_copy(kT[:, :, (i * U + u) * P:(i * U + u + 1) * P], tp[0:A, 1]).then_inc(s.k_kept, 1)

    def tensor(pe):
        yield 0.1
        pe.wait_ge(s.logf, 1)
        for u in range(U):
            yield 0.2
            if u:
                pe.wait_ge(s.carried, u)
            pe.matmul(cum[:, u], c.upto, f[:, u], start=True, stop=False)
            pe.matmul(cum[:, u], c.ones[0:1], carry[:], start=False, stop=True)
            pe.matmul(tot[:, u], c.ones[:, 0:1], f[:, u], start=True, stop=True).then_inc(s.sums, 1)
        for u in range(U):
            yield 0.45 + 0.1 * u
            pe.wait_ge(s.aug_done, u + 1)
            if u:
                pe.wait_ge(s.q_kept, u)
                pe.wait_ge(s.k_kept, u)
            for a in range(2):
                for h in range(HEADS):
                    m = pe.transpose(tp[0:A, a, h], aug[:, u, a, h], c.ident)
            m.then_inc(s.turned, 1)

    return {"sync": sync, "scalar": scalar, "vector": vector, "tensor": tensor}


MLSTM_FRONT_SIGNALS = ("m_ahead moz_in conv_late conved gates_in mlogf msums a_done rows_t rows_kept qk_done "
                       "mturned qkT_done mscores s_kept tanhs ")
MLSTM_BACK_SIGNALS = ("int_ps int_kept M_done spread_M exps_r Ein Eexp toks tok_kept kw_done mup_ps weighted in_ps msqd "
                      "mrs my_done ")


def mlstm_buffers(nc, B, w, big):
    V1 = HD + 1
    b = Named()
    b.big = big
    b.cw = B.sb("cw", [P, 4, 2 * GW])
    b.cb = B.sb("cb", [P, 2 * GW])
    b.gb = B.sb("gb", [P, 2 * HEADS])
    b.og = B.sb("og", [P, GW])
    b.state = B.sb("state", [P, 2, 2 * V1])
    b.m_prev = B.sb("m_prev", [HEADS, 1])
    b.qk = B.sb("qk", [P, 2, 2 * GW])
    b.qkT = B.sb("qkT", [P, 2, 4, P])
    b.sT = B.sb("sT", [P, 2, 2, 2, P])
    b.a_tok = B.sb("a_tok", [P, 2, HEADS])
    b.a_row = B.sb("a_row", [HEADS, 2, P])
    b.nr = B.sb("nr", [HEADS, 2, P])
    b.vx = B.sb("vx", [P, 2, HEADS, V1])
    b.oz = B.sb("oz", [P, 2, 2, GW])
    b.x = B.sb("x", [P, 2, 4, 2 * GW])
    b.vin = B.sb("vin", [P, 2, GW])
    b.gi = B.sb("gi", [P, 2, 2 * HEADS])
    b.nb = B.sb("nb", [P, HEADS])
    b.M = B.sb("M", [HEADS, P])
    b.nM = B.sb("nM", [HEADS, P])
    b.rows = B.sb("rows", [HEADS, 3, P])
    b.tok = B.sb("tok", [P, 3, HEADS])
    b.cd = B.sb("cd", [P, 2])
    b.E = B.sb("E", [P, HEADS, P])
    b.kw = B.sb("kw", [P, HEADS, HD])
    b.inter = B.sb("inter", [P, 2, 2, V1])
    b.num = B.sb("num", [P, HEADS, V1])
    b.h = B.sb("h", [P, 2, HEADS, HD])
    b.sq = B.sb("msq", [P, HEADS, HD])
    b.ss = B.sb("mss", [P, HEADS])
    load(nc, "ml_w", [(b.cw[:, j], row(w['mlstm_conv_w'][j])) for j in range(4)]
         + [(b.cb[:], row(w['mlstm_conv_b'])), (b.gb[:, 0:HEADS], row(w['mlstm_i_b'])),
            (b.gb[:, HEADS:], row(w['mlstm_f_b'])), (b.og[:], row(w['mlstm_out_g']))])
    with step(nc, "cleared") as (block, s):

        @block.vector
        def _(dve):
            dve.memset(b.state[:], 0.0).then_inc(s.cleared, 1)
            dve.memset(b.m_prev[:], 0.0).then_inc(s.cleared, 1)
            dve.memset(b.vx[:, :, :, HD:V1], 1.0).then_inc(s.cleared, 1)
            dve.wait_ge(s.cleared, 3)
    return b


def mlstm_loads(b, sp, arrived, proj, t0, parity):
    x, gi, vin = (t[:, parity] for t in (b.x, b.gi, b.vin))
    sp.dma_start(gi, proj[bass.ds(t0 + PAD, P), C_I:C_I + 2 * HEADS]).then_inc(arrived, 16)
    for j in range(4):
        sp.dma_start(x[:, j], proj[bass.ds(t0 + (PAD - 3 + j), P), C_QK:C_QK + 2 * GW]).then_inc(arrived, 16)
    sp.dma_start(vin, proj[bass.ds(t0 + PAD, P), C_V:C_V + GW]).then_inc(arrived, 16)
    return 16 * 6


def mlstm_front(c, b, s, proj, t0, parity, more):
    nb, cw = b.nb, b.cw
    qk, qkT, sT, a_tok, vx, oz, x, gi, vin = (t[:, parity] for t in (b.qk, b.qkT, b.sT, b.a_tok, b.vx, b.oz, b.x,
                                                                    b.gi, b.vin))
    a_row, nr = b.a_row[:, parity], b.nr[:, parity]
    f0, f1 = b.big[:, 0], b.big[:, 1]
    p_nb, p_rows = f0[:, 0:4], f0[0:HEADS, 64:320]
    p_s = b.big[:, 0:2, 0:2 * P].rearrange("p r (j t) -> p j r t", j=2)
    N = 30.0

    def sync(sp):
        yield 0.0
        sp.dma_start(oz.rearrange("p a c -> p (a c)"), proj[bass.ds(t0 + PAD, P), C_O:C_O + 2 * GW])\
          .then_inc(s.moz_in, 16)
        if more:
            n = mlstm_loads(b, sp, s.m_ahead, proj, t0 + P, 1 - parity)
            yield 0.9
            sp.wait_ge(s.m_ahead, n)

    def gpsimd(pool):
        yield 1 / N
        pool.tensor_tensor(x[:, 2:4], x[:, 2:4], cw[:, 2:4], ALU.mult).then_inc(s.conv_late, 1)
        yield 2 / N
        pool.tensor_copy(vx[:, :, 0:HD], vin.rearrange("p (h d) -> p h d", h=HEADS))

    def scalar(act):
        yield 1 / N
        act.wait_ge(s.gates_in, 1)
        act.activation(gi[:, HEADS:], gi[:, HEADS:], ACT.Exp, scale=-1.0)
        act.drain()
        act.activation(gi[:, HEADS:], gi[:, HEADS:], ACT.Ln, bias=c.ones[:, 0:1]).then_inc(s.mlogf, 1)
        yield 13 / N
        act.wait_ge(s.moz_in, 16)
        act.activation(oz[:, 1], oz[:, 1], ACT.Silu)
        act.activation(oz[:, 0], oz[:, 0], ACT.Tanh, scale=0.5).then_inc(s.tanhs, 1)
        act.wait_ge(s.conved, 1)
        act.activation(qk, qk, ACT.Silu).then_inc(s.qk_done, 1)
        yield 17 / N
        p_qk = f1.rearrange("p (a t) -> p a t", a=4)
        act.wait_ge(s.mturned, 1)
        act.activation(qkT[:, 0:2], p_qk[:, 0:2], ACT.Copy)
        act.activation(qkT[:, 2:4], p_qk[:, 2:4], ACT.Copy, scale=HD ** -0.5).then_inc(s.qkT_done, 1)
        yield 21 / N
        act.wait_ge(s.mscores, 1)
        act.activation(sT, p_s, ACT.Copy).then_inc(s.s_kept, 1)

    def vector(dve):
        yield 0.0
        dve.tensor_tensor(gi, gi, b.gb[:], ALU.add).then_inc(s.gates_in, 1)
        yield 3 / N
        dve.tensor_tensor(x[:, 0:2], x[:, 0:2], cw[:, 0:2], ALU.mult)
        dve.drain()
        dve.tensor_tensor(qk, x[:, 0], x[:, 1], ALU.add)
        dve.drain()
        dve.tensor_tensor(qk, qk, b.cb[:], ALU.add)
        yield 7 / N
        dve.wait_ge(s.msums, 1)
        dve.tensor_copy(nb[:], p_nb)
        dve.tensor_tensor(a_tok, gi[:, 0:HEADS], p_nb, ALU.add)
        dve.drain().then_inc(s.a_done, 1)
        yield 10 / N
        dve.wait_ge(s.conv_late, 1)
        dve.tensor_tensor(x[:, 2], x[:, 2], x[:, 3], ALU.add)
        dve.drain()
        dve.tensor_tensor(qk, qk, x[:, 2], ALU.add).then_inc(s.conved, 1)
        yield 12 / N
        dve.wait_ge(s.rows_t, 1)
        dve.tensor_copy(a_row, p_rows[:, 0:P])
        dve.tensor_copy(nr, p_rows[:, P:2 * P]).then_inc(s.rows_kept, 1)
        yield 18 / N
        dve.wait_ge(s.tanhs, 1)
        dve.tensor_scalar(oz[:, 0], oz[:, 0], 0.5, 0.5, ALU.mult, ALU.add)

    def tensor(pe):
        yield 3 / N
        pe.wait_ge(s.mlogf, 1)
        pe.matmul(p_nb, c.upto, gi[:, HEADS:], start=True, stop=True).then_inc(s.msums, 1)
        yield 9 / N
        pe.wait_ge(s.a_done, 1)
        pe.transpose(p_rows[:, 0:P], a_tok, c.ident)
        pe.transpose(p_rows[:, P:2 * P], nb[:], c.ident).then_inc(s.rows_t, 1)
        yield 15 / N
        pe.wait_ge(s.qk_done, 1)
        for j in range(4):
            m = pe.transpose(f1[:, j * P:(j + 1) * P], qk[:, j * P:(j + 1) * P], c.ident)
        m.then_inc(s.mturned, 1)
        yield 19 / N
        pe.wait_ge(s.qkT_done, 1)
        pe.wait_ge(s.rows_kept, 1)
        for k in range(HEADS):
            off, j = HD * (k % 2), k // 2
            m = pe.matmul(p_s[:, j, k % 2], qkT[off:off + HD, 2 + j], qkT[off:off + HD, j], start=True, stop=True)
        m.then_inc(s.mscores, 1)

    return {"sync": sync, "gpsimd": gpsimd, "scalar": scalar, "vector": vector, "tensor": tensor}


def mlstm_back(c, b, s, parity):
    V1 = HD + 1
    M, nM, rows, tok, cd, E, kw, inter, num, sq, ss = (b.M, b.nM, b.rows, b.tok, b.cd, b.E, b.kw, b.inter, b.num,
                                                       b.sq, b.ss)
    h = b.h[:, parity]
    m_prev, state = b.m_prev, b.state
    qk, qkT, sT, a_tok, vx, oz = (t[:, parity] for t in (b.qk, b.qkT, b.sT, b.a_tok, b.vx, b.oz))
    a_row, nr = b.a_row[:, parity], b.nr[:, parity]
    g0, g1 = b.big[:, 2], b.big[:, 3]
    p_int = b.big[:, 2:4, 0:2 * V1].rearrange("p r (j e) -> p j r e", j=2)
    p_M = g0.rearrange("p (h t) -> p h t", h=HEADS)
    p_tok, p_cd = g1[:, 0:12].rearrange("p (a h) -> p a h", a=3), g1[:, 16:18]
    p_in = g0[:, 0:HEADS * V1].rearrange("p (h e) -> p h e", h=HEADS)
    p_up = g1[:, 0:4 * V1].rearrange("p (j e) -> p j e", j=2)
    N = 30.0

    def scalar(act):
        yield 1.5 / N
        act.wait_ge(s.int_ps, 1)
        act.activation(inter[:], p_int, ACT.Copy).then_inc(s.int_kept, 1)
        yield 4 / N
        act.wait_ge(s.M_done, 1)
        act.activation(rows[:, 0], nM[:], ACT.Exp, bias=m_prev[:, 0:1])
        act.activation(rows[:, 1], rows[:, 1], ACT.Exp)
        act.activation(rows[:, 2], a_row, ACT.Exp, bias=nM[:, P - 1:P]).then_inc(s.exps_r, 1)
        yield 7 / N
        act.wait_ge(s.Ein, 1)
        act.activation(E[:], E[:], ACT.Exp).then_inc(s.Eexp, 1)
        yield 24 / N
        act.wait_ge(s.msqd, 1)
        rstd(act, c, ss[:], HD).then_inc(s.mrs, 1)

    def vector(dve):
        yield 0.0
        dve.tensor_tensor_scan(M[:], a_row, a_row, m_prev[:, 0:1], ALU.max, ALU.max)
        dve.drain()
        dve.tensor_scalar(nM[:], M[:], -1.0, None, ALU.mult)
        dve.tensor_tensor(rows[:, 1], nr, M[:], ALU.subtract)
        dve.drain().then_inc(s.M_done, 1)
        yield 5.5 / N
        dve.wait_ge(s.spread_M, 1)
        for k in range(HEADS):
            dve.tensor_scalar(E[:, k], p_M[:, k], a_tok[:, k:k + 1], 0.0, ALU.add, ALU.min)
        dve.drain().then_inc(s.Ein, 1)
        yield 8 / N
        dve.wait_ge(s.toks, 1)
        dve.tensor_scalar(m_prev[:], M[:, P - 1:P], nr[:, P - 1:P], None, ALU.subtract)
        dve.tensor_copy(tok[:], p_tok)
        dve.tensor_copy(cd[:], p_cd)
        dve.drain().then_inc(s.tok_kept, 1)
        dve.tensor_tensor(kw[:], qk[:, GW:].rearrange("p (h d) -> p h d", h=HEADS), spread(tok[:, 2], 2, HD), ALU.mult)
        dve.drain()
        dve.tensor_scalar(kw[:], kw[:], HD ** -0.5, None, ALU.mult).then_inc(s.kw_done, 1)
        yield 9 / N
        dve.wait_ge(s.int_kept, 1)
        for j in range(2):
            dve.tensor_tensor(num[:, 2 * j:2 * j + 2], inter[:, j], spread(tok[:, 0, 2 * j:2 * j + 2], 2, V1), ALU.mult)
        yield 11 / N
        dve.wait_ge(s.Eexp, 1)
        dve.tensor_tensor(E[:], E[:], spread(c.upto, 1, HEADS), ALU.mult)
        dve.drain()
        E4 = E[:].rearrange("p (j r) t -> p j r t", j=2)
        dve.tensor_tensor(E4, E4, sT, ALU.mult).then_inc(s.weighted, 1)
        yield 16 / N
        dve.wait_ge(s.in_ps, 1)
        dve.tensor_tensor(num[:], num[:], p_in, ALU.add)
        dve.drain()
        d = num[:, :, HD:V1].rearrange("p h o -> p (h o)")
        dve.scalar_tensor_tensor(out=ss[:], in0=d, scalar=-1.0, in1=d, op0=ALU.mult, op1=ALU.max)
        dve.drain()
        dve.tensor_tensor(ss[:], ss[:], tok[:, 1], ALU.max)
        dve.drain()
        dve.reciprocal(ss[:], ss[:])
        dve.drain()
        yield 19 / N
        dve.tensor_tensor(h, num[:, :, 0:HD], spread(ss[:], 2, HD), ALU.mult)
        dve.drain()
        dve.tensor_tensor(h, h, oz[:, 0].rearrange("p (h d) -> p h d", h=HEADS), ALU.mult)
        dve.drain()
        yield 22 / N
        dve.tensor_tensor(sq[:], h, h, ALU.mult)
        dve.drain()
        dve.tensor_reduce(ss[:], sq[:], AX.X, ALU.add).then_inc(s.msqd, 1)
        yield 24 / N
        h2 = h.rearrange("p h d -> p (h d)")
        dve.tensor_tensor(h2, h2, b.og[:], ALU.mult)
        dve.drain()
        dve.tensor_tensor(h2, h2, oz[:, 1], ALU.mult)
        dve.wait_ge(s.mup_ps, 1)
        for j in range(2):
            dve.scalar_tensor_tensor(out=state[:, j], in0=state[:, j], scalar=cd[:, j:j + 1], in1=p_up[:, j],
                                     op0=ALU.mult, op1=ALU.add)
        yield 28 / N
        dve.wait_ge(s.mrs, 1)
        dve.drain()
        dve.tensor_tensor(h, h, spread(ss[:], 2, HD), ALU.mult).then_inc(s.my_done, 1)

    def tensor(pe):
        yield 0.0
        for k in range(HEADS):
            off, j = HD * (k % 2), k // 2
            m = pe.matmul(p_int[:, j, k % 2], qkT[off:off + HD, j],
                          state[off:off + HD, j, (k % 2) * V1:(k % 2 + 1) * V1], start=True, stop=True)
        m.then_inc(s.int_ps, 1)
        yield 3 / N
        pe.wait_ge(s.int_kept, 1)
        pe.wait_ge(s.M_done, 1)
        for k in range(HEADS):
            m = pe.matmul(p_M[:, k], c.all[0:HEADS, ROW[k]], nM[:], start=True, stop=True)
        m.then_inc(s.spread_M, 1)
        yield 6 / N
        pe.wait_ge(s.exps_r, 1)
        for k in range(3):
            pe.transpose(p_tok[:, k], rows[:, k], c.ident[0:HEADS, 0:HEADS])
        for j in range(2):
            m = pe.matmul(p_cd[:, j:j + 1], c.all[0:HEADS, PAIR[j]], rows[:, 0, P - 1:P], start=True, stop=True)
        m.then_inc(s.toks, 1)
        yield 12 / N
        pe.wait_ge(s.kw_done, 1)
        pe.wait_ge(s.tok_kept, 1)
        for j in range(2):
            m = pe.matmul(p_up[:, j], kw[:, 2 * j:2 * j + 2].rearrange("p h d -> p (h d)"),
                          vx[:, 2 * j:2 * j + 2].rearrange("p h d -> p (h d)"), start=True, stop=True)
        m.then_inc(s.mup_ps, 1)
        yield 14 / N
        pe.wait_ge(s.Ein, 1)
        pe.wait_ge(s.weighted, 1)
        for k in range(HEADS):
            m = pe.matmul(p_in[:, k], E[:, k], vx[:, k], start=True, stop=True)
        m.then_inc(s.in_ps, 1)

    return {"scalar": scalar, "vector": vector, "tensor": tensor}


MEMORY_SIGNALS = ("q_ahead qsquares qrs qnormed qx_turned qx_kept qscored qmaxed qexps qturned qkept qweighed qsilus qy_done ")


def memory_chunk(c, b, s, proj, t0, parity, more):
    MT = N_MEM // P
    sq, ss, qT, pr, mx, den, pT, kT, vm, gq, big = (b.sq, b.ss, b.qT, b.pr, b.mx, b.den, b.pT, b.kT, b.vm, b.gq,
                                                    b.big)
    qz = b.qz[:, parity]
    tq = big[0:HD, 4].rearrange("p (h t) -> p h t", h=HEADS)
    sc = big[:, 5:7].rearrange("p b (h t) -> p (b h) t", h=2)
    tp = big[:, 4:6].rearrange("p b (h m t) -> p (b h) m t", h=2, m=MT)
    o = big[:, 7, 0:GW].rearrange("p (h d) -> p h d", h=HEADS)
    q, z = qz[:, 0:GW], qz[:, GW:]
    q64 = q.rearrange("p (h d) -> p h d", h=HEADS)
    N = 30.0

    def sync(sp):
        yield 0.3
        if more:
            sp.dma_start(b.qz[:, 1 - parity], proj[bass.ds(t0 + P + PAD, P), M_Q:M_Q + 2 * GW]).then_inc(s.q_ahead, 16)
            yield 0.9
            sp.wait_ge(s.q_ahead, 16)

    def scalar(act):
        yield 2.5 / N
        act.wait_ge(s.qsquares, 1)
        rstd(act, c, ss[:], HD).then_inc(s.qrs, 1)
        yield 8 / N
        act.wait_ge(s.qx_turned, 1)
        act.activation(qT[:], tq, ACT.Copy).then_inc(s.qx_kept, 1)
        yield 12 / N
        act.wait_ge(s.qmaxed, 1)
        for h in range(HEADS):
            act.activation(pr[:, h], sc[:, h], ACT.Exp, bias=mx[:, h:h + 1], accum_out=den[:, h:h + 1])\
               .then_inc(s.qexps, 1)
        yield 13 / N
        act.activation(z, z, ACT.Silu).then_inc(s.qsilus, 1)
        yield 18 / N
        act.wait_ge(s.qturned, 1)
        act.activation(pT[:], tp, ACT.Copy).then_inc(s.qkept, 1)

    def vector(dve):
        yield 0.5 / N
        dve.tensor_tensor(sq[:], q, q, ALU.mult)
        dve.drain()
        dve.tensor_reduce(ss[:], sq[:].rearrange("p (h d) -> p h d", h=HEADS), AX.X, ALU.add).then_inc(s.qsquares, 1)
        yield 6 / N
        dve.wait_ge(s.qrs, 1)
        dve.tensor_tensor(q64, q64, spread(ss[:], 2, HD), ALU.mult)
        dve.drain()
        dve.scalar_tensor_tensor(out=q64, in0=q64, scalar=HD ** -0.5, in1=spread(gq[:], 1, HEADS), op0=ALU.mult,
                                 op1=ALU.mult).then_inc(s.qnormed, 1)
        yield 11 / N
        dve.wait_ge(s.qscored, 1)
        dve.tensor_reduce(mx[:], sc, AX.X, ALU.max)
        dve.drain()
        dve.tensor_scalar(mx[:], mx[:], -1.0, None, ALU.mult).then_inc(s.qmaxed, 1)
        yield 23 / N
        dve.wait_ge(s.qexps, HEADS)
        dve.reciprocal(den[:], den[:])
        dve.wait_ge(s.qweighed, 1)
        dve.drain()
        dve.tensor_tensor(q64, o, spread(den[:], 2, HD), ALU.mult)
        dve.wait_ge(s.qsilus, 1)
        dve.drain()
        dve.tensor_tensor(q, q, z, ALU.mult).then_inc(s.qy_done, 1)

    def tensor(pe):
        yield 7 / N
        pe.wait_ge(s.qnormed, 1)
        for h in range(HEADS):
            m = pe.transpose(tq[:, h], q64[:, h], c.ident)
        m.then_inc(s.qx_turned, 1)
        yield 10 / N
        pe.wait_ge(s.qx_kept, 1)
        for h in range(HEADS):
            m = pe.matmul(sc[:, h], qT[:, h], kT[:, h], start=True, stop=True)
        m.then_inc(s.qscored, 1)
        yield 16 / N
        pe.wait_ge(s.qexps, HEADS)
        for h in range(HEADS):
            for t in range(MT):
                m = pe.transpose(tp[:, h, t], pr[:, h, t * P:(t + 1) * P], c.ident)
        m.then_inc(s.qturned, 1)
        yield 20 / N
        pe.wait_ge(s.qkept, 1)
        for h in range(HEADS):
            for t in range(MT):
                m = pe.matmul(o[:, h], pT[:, h, t], vm[:, t, h * HD:(h + 1) * HD], start=(t == 0), stop=(t == MT - 1))
        m.then_inc(s.qweighed, 1)

    return {"sync": sync, "scalar": scalar, "vector": vector, "tensor": tensor}


def memory_and_mlstm(nc, c, w, proj, mixed):
    with ExitStack() as ctx:
        B = Buffers(nc, ctx, "mm")
        qb = memory_buffers(nc, c, B, w)
        big = B.ps("big", [P, 8, 512])
        qb.big = big
        mb = mlstm_buffers(nc, B, w, big)

        def store(sp, s, t0, parity):
            sp.dma_start(mixed[bass.ds(t0, P), 2 * GW:3 * GW], mb.h[:, parity].rearrange("p h d -> p (h d)"))\
              .then_inc(s.stored, 16)
            sp.dma_start(mixed[bass.ds(t0, P), 4 * GW:5 * GW], qb.qz[:, parity, 0:GW]).then_inc(s.stored, 16)
            sp.wait_ge(s.stored, 32)

        def stage(t0, parity, front, back, more=True, before=True):
            names = (MLSTM_BACK_SIGNALS + MEMORY_SIGNALS if back else "") + (MLSTM_FRONT_SIGNALS if front else "")
            with step(nc, names + "stored") as (block, s):
                branches = []
                if back:
                    branches.append(mlstm_back(c, mb, s, parity))
                if front:
                    branches.append(mlstm_front(c, mb, s, proj, t0 + P, 1 - parity, more))
                if back:
                    branches.append(memory_chunk(c, qb, s, proj, t0, parity, front))

                @block.sync
                def _(sp):
                    if before:
                        store(sp, s, t0 - P, 1 - parity)
                    together(sp, "sync", branches)

                @block.gpsimd
                def _(pool):
                    together(pool, "gpsimd", branches)

                @block.scalar
                def _(act):
                    together(act, "scalar", branches)

                @block.vector
                def _(dve):
                    together(dve, "vector", branches)

                @block.tensor
                def _(pe):
                    together(pe, "tensor", branches)

        with step(nc, "arrived") as (block, s):

            @block.sync
            def _(sp):
                sp.dma_start(qb.qz[:, 0], proj[PAD:P + PAD, M_Q:M_Q + 2 * GW]).then_inc(s.arrived, 16)
                n = mlstm_loads(mb, sp, s.arrived, proj, 0, 0)
                sp.wait_ge(s.arrived, 16 + n)

        stage(-P, 1, True, False, before=False)
        stage(0, 0, True, True, before=False)
        with nc.Fori(0, TILES // 2 - 2) as j:
            stage(j * (2 * P) + P, 1, True, True)
            stage(j * (2 * P) + 2 * P, 0, True, True)
        stage(SEQ - 3 * P, 1, True, True)
        stage(SEQ - 2 * P, 0, True, True, more=False)
        stage(SEQ - P, 1, False, True)
        with step(nc, "stored") as (block, s):

            @block.sync
            def _(sp):
                store(sp, s, SEQ - P, 1)


RWKV_FRONT_SIGNALS = ("r_ahead shifted lows r_silus low_ps low_kept wa_ps wa_in tanhs la_done cums exps kksq norms "
                      "tilde turned_a turned_b kept_a kept_b grams g_done x_set p1 p1c x_ps xt_ps x_kept xt_kept ")
RWKV_BACK_SIGNALS = "s0_done r_ps r_done u_ps u_done ry_ps ry_kept st_ps st_done rsqd rrs ry_done "


def rwkv_buffers(nc, B, w, big):
    b = Named()
    b.big = big
    b.mu = B.sb("mu", [P, D_W])
    b.par = B.sb("par", [P, 6, GW])
    b.lo2 = B.sb("lo2", [RANK, 2, GW])
    b.state = B.sb("state", [P, 2, HD])
    b.x = B.sb("x", [P, 3, D_W])
    b.tl = B.sb("tl", [P, 2, 4, GW])
    b.XT4 = B.sb("XT4", [P, 2, 2, 4, P])
    b.G = B.sb("G", [P, 2, 2, HEADS, 2, P])
    b.XT = B.sb("XT", [P, 2, HEADS, P])
    b.em = B.sb("em", [P, 2, 2, 2])
    b.bon = B.sb("bon", [P, 2, HEADS])
    b.pv = B.sb("pv", [P, 2, D_W])
    b.loT = B.sb("loT", [RANK, 2, P])
    b.wa = B.sb("wa", [P, 2, GW])
    b.kk = B.sb("kk", [P, HEADS, HD])
    b.kn = B.sb("kn", [P, GW])
    b.sq = B.sb("rsq", [P, HEADS, HD])
    b.ss = B.sb("rss", [P, HEADS])
    b.ex = B.sb("ex", [P, 3, GW])
    b.X = B.sb("X", [P, HEADS, P])
    b.Pm = b.ex[:, 0:2].rearrange("p a (h t) -> p (a h) t", h=2)
    b.R = B.sb("R", [P, HEADS, HD])
    b.U = B.sb("U", [P, HEADS, HD])
    b.S0 = B.sb("S0", [P, 2, HD])
    b.y = B.sb("ry", [P, 2, HEADS, HD])
    b.sqb = b.R
    b.ssb = B.sb("rssb", [P, HEADS])
    load(nc, "rw_w", [(b.mu[:], row(w['rwkv_mu'])), (b.lo2[:, 0], w['rwkv_w2']), (b.lo2[:, 1], w['rwkv_a2'])]
         + [(b.par[:, k], row(w[n])) for k, n in enumerate(['rwkv_w0', 'rwkv_a0', 'rwkv_k_k', 'rwkv_k_a'])]
         + [(b.par[:, 4], row(w['rwkv_r_k'].rearrange("h d -> (h d)"))), (b.par[:, 5], row(w['rwkv_ln_g']))])
    with step(nc, "cleared") as (block, s):

        @block.vector
        def _(dve):
            dve.memset(b.state[:], 0.0).then_inc(s.cleared, 1)
            dve.wait_ge(s.cleared, 1)
    return b


def rwkv_loads(b, sp, arrived, proj, i):
    sp.dma_start(b.x[:, i % 3], proj[i * P + PAD:(i + 1) * P + PAD, D_0:D_0 + D_W]).then_inc(arrived, 16)
    sp.dma_start(b.pv[:, i % 2], proj[i * P + PAD - 1:(i + 1) * P + PAD - 1, D_0:D_0 + D_W]).then_inc(arrived, 16)
    return 32


def rwkv_front(c, B, s, proj, i):
    R_E = float(np.exp(-0.5))
    o2 = i % 2
    x = B.x[:, i % 3]
    tl, XT4, G, XT, em, bon = (t[:, o2] for t in (B.tl, B.XT4, B.G, B.XT, B.em, B.bon))
    pv = B.pv[:, o2]
    loT, wa, kk, kn, sq, ss, ex, X, Pm = B.loT, B.wa, B.kk, B.kn, B.sq, B.ss, B.ex, B.X, B.Pm
    mu, par, lo2 = B.mu, B.par, B.lo2
    b0, b1, b2 = (B.big[:, k] for k in range(3))
    by_head = lambda ap: ap.rearrange("p (h t) -> p h t", h=HEADS)
    masks = c.all[:, 1 * P:3 * P].rearrange("p (a t) -> p a t", a=2)
    level = lambda l, d: (34 + 5.5 * l + d) / N
    N = 76.0

    def sync(sp):
        if i + 1 < TILES:
            yield 0.01
            n = rwkv_loads(B, sp, s.r_ahead, proj, i + 1)
            yield 0.9
            sp.wait_ge(s.r_ahead, n)

    def scalar(act):
        yield 4 / N
        act.wait_ge(s.shifted, 1)
        act.activation(x[:, D_WLO:D_WLO + RANK], x[:, D_WLO:D_WLO + RANK], ACT.Tanh).then_inc(s.lows, 1)
        act.activation(x[:, D_Z:D_Z + GW], x[:, D_Z:D_Z + GW], ACT.Silu).then_inc(s.r_silus, 1)
        yield 7 / N
        act.wait_ge(s.low_ps, 1)
        act.activation(loT[:], b1[0:RANK, 0:2 * P].rearrange("p (a t) -> p a t", a=2), ACT.Copy)\
           .then_inc(s.low_kept, 1)
        yield 10 / N
        act.wait_ge(s.kksq, 1)
        act.activation(ss[:], ss[:], ACT.Sqrt).then_inc(s.norms, 1)
        yield 11 / N
        act.wait_ge(s.wa_in, 1)
        act.activation(wa[:], wa[:], ACT.Tanh, scale=0.5).then_inc(s.tanhs, 1)
        yield 15 / N
        act.wait_ge(s.cums, 1)
        cps = b0.rearrange("p (a c) -> p a c", a=2)
        act.activation(ex[:, 0:2], cps, ACT.Exp)
        act.activation(ex[:, 2], cps[:, 0], ACT.Exp, scale=-1.0)
        act.activation(em, b1[:, 0:4].rearrange("p (j e) -> p j e", j=2), ACT.Exp).then_inc(s.exps, 1)
        yield 22 / N
        act.wait_ge(s.turned_a, 1)
        act.activation(XT4[:, 0], b2.rearrange("p (a t) -> p a t", a=4), ACT.Copy).then_inc(s.kept_a, 1)
        yield 23 / N
        act.wait_ge(s.turned_b, 1)
        act.activation(XT4[:, 1], b1.rearrange("p (a t) -> p a t", a=4), ACT.Copy).then_inc(s.kept_b, 1)
        for l in range(1, LEVELS):
            yield level(l, 1.5)
            act.wait_ge(s.p1, l + 1)
            act.activation(Pm, by_head(b0), ACT.Copy).then_inc(s.p1c, 1)

    def vector(dve):
        yield 0.0
        dve.tensor_tensor(pv, pv, x, ALU.subtract)
        dve.drain()
        yield 2 / N
        dve.tensor_tensor(pv, pv, mu[:], ALU.mult)
        dve.drain()
        yield 3 / N
        dve.tensor_tensor(x, x, pv, ALU.add).then_inc(s.shifted, 1)
        k, v, r = x[:, D_K:D_K + GW], x[:, D_V:D_V + GW], x[:, D_R:D_R + GW]
        dve.drain()
        yield 5 / N
        kk2 = kk[:].rearrange("p h d -> p (h d)")
        dve.tensor_tensor(kk2, k, par[:, 2], ALU.mult)
        dve.drain()
        dve.tensor_tensor(sq[:], kk[:], kk[:], ALU.mult)
        dve.drain()
        dve.tensor_reduce(ss[:], sq[:], AX.X, ALU.add).then_inc(s.kksq, 1)
        yield 9 / N
        dve.wait_ge(s.wa_ps, 1)
        dve.tensor_tensor(wa[:], b2.rearrange("p (a c) -> p a c", a=2), par[:, 0:2], ALU.add).then_inc(s.wa_in, 1)
        yield 13 / N
        dve.wait_ge(s.tanhs, 1)
        dve.tensor_scalar(wa[:, 0], wa[:, 0], -0.5 * R_E, -0.5 * R_E, ALU.mult, ALU.add)
        dve.tensor_scalar(wa[:, 1], wa[:, 1], 0.5, 0.5, ALU.mult, ALU.add)
        dve.drain().then_inc(s.la_done, 1)
        dve.wait_ge(s.norms, 1)
        dve.tensor_scalar(ss[:], ss[:], 1e-12, None, ALU.max)
        dve.drain()
        dve.reciprocal(ss[:], ss[:])
        dve.scalar_tensor_tensor(out=kn[:], in0=wa[:, 1], scalar=-1.0, in1=par[:, 3], op0=ALU.add, op1=ALU.mult)
        dve.drain()
        yield 15 / N
        dve.tensor_tensor(kk[:], kk[:], spread(ss[:], 2, HD), ALU.mult)
        dve.scalar_tensor_tensor(out=kn[:], in0=kn[:], scalar=1.0, in1=k, op0=ALU.add, op1=ALU.mult)
        dve.drain()
        yield 17 / N
        dve.wait_ge(s.exps, 1)
        dve.tensor_tensor(tl[:, 0], r, ex[:, 0], ALU.mult)
        dve.scalar_tensor_tensor(out=tl[:, 1], in0=kk2, scalar=-1.0, in1=ex[:, 1], op0=ALU.mult, op1=ALU.mult)
        dve.tensor_tensor(tl[:, 3], kn[:], ex[:, 2], ALU.mult)
        dve.tensor_tensor(tl[:, 2], kk2, ex[:, 2], ALU.mult)
        dve.drain()
        dve.tensor_tensor(tl[:, 2], tl[:, 2], wa[:, 1], ALU.mult).then_inc(s.tilde, 1)
        yield 20 / N
        dve.tensor_copy(X[:], spread(c.ident, 1, HEADS))
        dve.tensor_copy(XT, spread(c.ident, 1, HEADS))
        dve.drain().then_inc(s.x_set, 1)
        for h in range(HEADS):
            yield (26 + 2 * h) / N
            dve.wait_ge(s.grams, h + 1)
            ps = B.big[:, h % 2].rearrange("p (b a t) -> p b a t", b=2, a=2)
            for b in range(2):
                d = dve.tensor_tensor(G[:, b, h], ps[:, b], masks, ALU.mult)
            d.then_inc(s.g_done, 1)
        dve.drain()
        at = [[spread(c.all[:, m].bitcast(U32), 1, HEADS) for m in ms] for ms in (LEVEL_T, LEVEL)]
        for l in range(LEVELS):
            if l == 0:
                yield level(0, 0)
                dve.copy_predicated(XT, at[1][0], G[:, 0, :, 1])
                dve.drain().then_inc(s.xt_kept, 1)
                dve.wait_ge(s.p1, 1)
                dve.copy_predicated(X[:], at[0][0], by_head(b0))
                dve.drain().then_inc(s.x_kept, 1)
                continue
            if l < LEVELS - 1:
                yield level(l, 3)
                dve.wait_ge(s.x_ps, l)
                dve.copy_predicated(X[:], at[0][l], by_head(b1))
                dve.drain().then_inc(s.x_kept, 1)
            yield level(l, 4)
            dve.wait_ge(s.xt_ps, l)
            dve.copy_predicated(XT, at[1][l], by_head(b2))
            dve.drain().then_inc(s.xt_kept, 1)
            if l == 2:
                s2 = sq[:].rearrange("p h d -> p (h d)")
                dve.tensor_tensor(s2, r, kn[:], ALU.mult)
                dve.drain()
                yield level(l, 4.5)
                dve.tensor_tensor(s2, s2, par[:, 4], ALU.mult)
                dve.drain()
                yield level(l, 5)
                dve.tensor_reduce(bon, sq[:], AX.X, ALU.add)

    def tensor(pe):
        yield 6 / N
        pe.wait_ge(s.lows, 1)
        pe.transpose(b1[0:RANK, 0:P], x[:, D_WLO:D_WLO + RANK], c.ident)
        pe.transpose(b1[0:RANK, P:2 * P], x[:, D_ALO:D_ALO + RANK], c.ident).then_inc(s.low_ps, 1)
        yield 8 / N
        pe.wait_ge(s.low_kept, 1)
        pe.matmul(b2[:, 0:GW], loT[:, 0], lo2[:, 0], start=True, stop=True)
        pe.matmul(b2[:, GW:2 * GW], loT[:, 1], lo2[:, 1], start=True, stop=True).then_inc(s.wa_ps, 1)
        yield 14 / N
        pe.wait_ge(s.la_done, 1)
        pe.matmul(b0[:, 0:GW], c.all[:, CENTRED], wa[:, 0], start=True, stop=True)
        pe.matmul(b0[:, GW:2 * GW], c.all[:, CENTRED_BEFORE], wa[:, 0], start=True, stop=True)
        for j in range(2):
            lj = wa[:, 0, j * P:(j + 1) * P]
            pe.matmul(b1[:, 2 * j:2 * j + 1], lj, c.upto[:, P // 2 - 1:P // 2], start=True, stop=True)
            m = pe.matmul(b1[:, 2 * j + 1:2 * j + 2], lj, c.after[:, P // 2 - 1:P // 2], start=True, stop=True)
        m.then_inc(s.cums, 1)
        for j in range(2):
            yield (20 + j) / N
            pe.wait_ge(s.tilde, 1)
            for a in range(4):
                m = pe.transpose((b2, b1)[j][:, a * P:(a + 1) * P], tl[:, a, j * P:(j + 1) * P], c.ident)
            m.then_inc((s.turned_a, s.turned_b)[j], 1)
        for h in range(HEADS):
            yield (25 + 2 * h) / N
            off, j = HD * (h % 2), h // 2
            pe.wait_ge(s.kept_a, 1)
            if h:
                pe.wait_ge(s.kept_b, 1)
            if h >= 2:
                pe.wait_ge(s.g_done, h - 1)
            o = slice(off, off + HD)
            for b in range(2):
                m = pe.matmul(B.big[:, h % 2, b * GW:(b + 1) * GW], XT4[o, j, 2 + b],
                              XT4[o, j, 0:2].rearrange("p a t -> p (a t)"), start=True, stop=True)
            m.then_inc(s.grams, 1)
        for l in range(LEVELS):
            yield level(l, -0.6 if l else 0)
            if l == 0:
                pe.wait_ge(s.g_done, HEADS)
                pe.wait_ge(s.x_set, 1)
            else:
                pe.wait_ge(s.x_kept, l)
            for h in range(HEADS):
                m = pe.matmul(b0[:, h * P:(h + 1) * P], G[:, 0, h, 1], X[:, h], start=True, stop=True)
            m.then_inc(s.p1, 1)
            if l:
                yield level(l, 2)
                pe.wait_ge(s.p1c, l)
                pe.wait_ge(s.xt_kept, l)
                if l < LEVELS - 1:
                    for h in range(HEADS):
                        m = pe.matmul(b1[:, h * P:(h + 1) * P], XT[:, h], Pm[:, h], start=True, stop=True)
                    m.then_inc(s.x_ps, 1)
                for h in range(HEADS):
                    m = pe.matmul(b2[:, h * P:(h + 1) * P], Pm[:, h], XT[:, h], start=True, stop=True)
                m.then_inc(s.xt_ps, 1)

    return {"sync": sync, "scalar": scalar, "vector": vector, "tensor": tensor}


def rwkv_back(c, B, s, i):
    o2 = i % 2
    x = B.x[:, i % 3]
    tl, XT4, G, XT, em, bon = (t[:, o2] for t in (B.tl, B.XT4, B.G, B.XT, B.em, B.bon))
    R, U, S0, y, sq, ss, par, state = B.R, B.U, B.S0, B.y[:, o2], B.sqb, B.ssb, B.par, B.state
    both = B.big[:, 3:5]
    v = x[:, D_V:D_V + GW].rearrange("p (h d) -> p h d", h=HEADS)
    pairs = lambda ap: ap[:, :, 0:2 * HD].rearrange("p r (j d) -> p j r d", d=HD)
    N = 40.0

    def scalar(act):
        yield 6 / N
        act.wait_ge(s.r_ps, 1)
        act.activation(R[:].rearrange("p (j r) d -> p j r d", j=2), pairs(both), ACT.Copy).then_inc(s.r_done, 1)
        yield 10 / N
        act.wait_ge(s.u_ps, 1)
        act.activation(U[:], both[:, 0, 0:GW].rearrange("p (h d) -> p h d", h=HEADS), ACT.Copy)\
           .then_inc(s.u_done, 1)
        yield 15 / N
        act.wait_ge(s.ry_ps, 1)
        act.activation(y.rearrange("p (j r) d -> p j r d", j=2), pairs(both), ACT.Copy).then_inc(s.ry_kept, 1)
        yield 22 / N
        act.wait_ge(s.rsqd, 1)
        rstd(act, c, ss[:], HD).then_inc(s.rrs, 1)

    def vector(dve):
        yield 0.0
        for j in range(2):
            d = dve.tensor_scalar(S0[:, j], state[:, j], em[:, j, 0:1], None, ALU.mult)
        d.then_inc(s.s0_done, 1)
        yield 17 / N
        dve.wait_ge(s.ry_kept, 1)
        dve.tensor_tensor(sq[:], y, y, ALU.mult)
        dve.drain()
        dve.tensor_reduce(ss[:], sq[:], AX.X, ALU.add).then_inc(s.rsqd, 1)
        y2 = y.rearrange("p h d -> p (h d)")
        dve.tensor_tensor(y2, y2, par[:, 5], ALU.mult)
        dve.drain()
        dve.tensor_tensor(sq[:], v, spread(bon, 2, HD), ALU.mult)
        yield 20 / N
        dve.wait_ge(s.st_ps, 1)
        for off in (0, HD):
            o = slice(off, off + HD)
            dve.tensor_tensor(S0[o], S0[o], both[o, 0, 0:2 * P].rearrange("p (j c) -> p j c", j=2)[:, :, o], ALU.add)
        dve.drain()
        for j in range(2):
            dve.tensor_scalar(state[:, j], S0[:, j], em[:, j, 1:2], None, ALU.mult)
        yield 25 / N
        dve.wait_ge(s.rrs, 1)
        dve.drain()
        dve.tensor_tensor(y, y, spread(ss[:], 2, HD), ALU.mult)
        dve.drain()
        yield 27 / N
        dve.tensor_tensor(y, y, sq[:], ALU.add)
        dve.drain()
        yield 29 / N
        dve.tensor_tensor(y2, y2, x[:, D_Z:D_Z + GW], ALU.mult).then_inc(s.ry_done, 1)

    def tensor(pe):
        yield 1 / N
        pe.wait_ge(s.s0_done, 1)
        for h in range(HEADS):
            off, j = HD * (h % 2), h // 2
            o, dst = slice(off, off + HD), both[:, h % 2, j * HD:(j + 1) * HD]
            pe.matmul(dst, XT4[o, j, 1], S0[o, j], start=True, stop=False)
            m = pe.matmul(dst, G[:, 1, h, 1], v[:, h], start=False, stop=True)
        m.then_inc(s.r_ps, 1)
        yield 8 / N
        pe.wait_ge(s.r_done, 1)
        for h in range(HEADS):
            m = pe.matmul(both[:, 0, h * HD:(h + 1) * HD], XT[:, h], R[:, h], start=True, stop=True)
        m.then_inc(s.u_ps, 1)
        yield 12 / N
        pe.wait_ge(s.u_done, 1)
        for h in range(HEADS):
            off, j = HD * (h % 2), h // 2
            o, dst = slice(off, off + HD), both[:, h % 2, j * HD:(j + 1) * HD]
            pe.matmul(dst, XT4[o, j, 0], S0[o, j], start=True, stop=False)
            pe.matmul(dst, G[:, 0, h, 0], U[:, h], start=False, stop=False)
            m = pe.matmul(dst, G[:, 1, h, 0], v[:, h], start=False, stop=True)
        m.then_inc(s.ry_ps, 1)
        yield 18 / N
        pe.wait_ge(s.ry_kept, 1)
        for j in range(2):
            dst = both[:, 0, j * P:(j + 1) * P]
            pe.matmul(dst, tl[:, 2, j * P:(j + 1) * P],
                      U[:, 2 * j:2 * j + 2].rearrange("p h d -> p (h d)"), start=True, stop=False)
            m = pe.matmul(dst, tl[:, 3, j * P:(j + 1) * P], x[:, D_V + j * P:D_V + (j + 1) * P],
                          start=False, stop=True)
        m.then_inc(s.st_ps, 1)

    return {"scalar": scalar, "vector": vector, "tensor": tensor}


ALPHA = 2.0 ** 0.25


def project_out(nc, c, mix, w_out, x_old, x_out, name, turned_out=None, ln=None):
    K = mix.shape[1] // P
    KB = [(k, min(4, K - k)) for k in range(0, K, 4)]
    nb = len(KB)
    with ExitStack() as ctx:
        B = Buffers(nc, ctx, name)
        wo = B.sb("wo", [P, K, D_MODEL])
        m = B.sb("m", [P, K * P])
        x = B.sb("x", [P, 3, D_MODEL])
        mT = B.sb("mT", [P, K, P])
        tp = B.ps("tp", [P, nb, 4, P])
        acc = B.ps("acc", [P, 2, 2, 512])
        loads = []
        if ln:
            gb = B.sb("gb", [P, 2, D_MODEL])
            st = B.sb("st", [P, 2, 6])
            ag = B.sb("ag", [P, 2])
            loads += [(gb[:, 0], row(ln[0])), (gb[:, 1], row(ln[1]))]
        else:
            tq = B.ps("tq", [P, 4, P])
        with step(nc, "w_in0 w_in1 w_in2 par_in m_in x_in0 x_in1 x_in2 turned kept passed prod added summed vars rs "
                      "stored0 stored1 stored2 x_turned x_hi x_lo") as (block, s):
            x_in, stored = (s.x_in0, s.x_in1, s.x_in2), (s.stored0, s.stored1, s.stored2)
            w_in = (s.w_in0, s.w_in1, s.w_in2)
            w_v = w_out.rearrange("(k p) n -> p k n", p=P)

            @block.sync
            def _(sp):
                def store(u):
                    sp.wait_ge(s.summed, u + 1)
                    sp.dma_start(x_out[u * P:(u + 1) * P, :], x[:, u % 3]).then_inc(stored[u % 3], 16)

                for u in range(TILES):
                    if u:
                        sp.wait_ge(s.turned, nb * u)
                    sp.dma_start(m[:], mix[u * P:(u + 1) * P, :]).then_inc(s.m_in, 16)
                    if u == 0:
                        for k in range(K):
                            sp.dma_start(wo[:, k], w_v[:, k]).then_inc(w_in[k // 4], 16)
                    if u >= 3:
                        store(u - 3)
                        sp.wait_ge(stored[u % 3], 16 * (u // 3))
                        if not ln:
                            sp.wait_ge(s.x_turned, 2 * (u - 2))
                    sp.dma_start(x[:, u % 3], x_old[u * P:(u + 1) * P, :]).then_inc(x_in[u % 3], 16)
                    if u == 1:
                        for dst, src in loads:
                            sp.dma_start(dst, src).then_inc(s.par_in, 16)
                for u in range(TILES - 3, TILES):
                    store(u)
                for slot in range(3):
                    sp.wait_ge(stored[slot], 16 * len(range(slot, TILES, 3)))

            @block.tensor
            def _(pe):
                def turn(u):
                    pe.wait_ge(s.m_in, 16 * (u + 1))
                    for b, (k0, kn) in enumerate(KB):
                        if u:
                            pe.wait_ge(s.kept, nb * (u - 1) + b + 1)
                        for k in range(kn):
                            t = pe.transpose(tp[:, b, k], m[:, (k0 + k) * P:(k0 + k + 1) * P], c.ident)
                        t.then_inc(s.turned, 1)

                def multiply(u, b):
                    k0, kn = KB[b]
                    pe.wait_ge(s.kept, nb * u + b + 1)
                    if u == 0:
                        pe.wait_ge(w_in[b], 16 * kn)
                    if u >= 2 and b == 0:
                        pe.wait_ge(s.added, u - 1)
                    for k in range(k0, k0 + kn):
                        for n in range(2):
                            t = pe.matmul(acc[:, u % 2, n], mT[:, k], wo[:, k, n * 512:(n + 1) * 512],
                                          start=(k == 0), stop=(k == K - 1))
                    t.then_inc(s.passed if b < nb - 1 else s.prod, 1)

                def turn_x(u, half):
                    pe.wait_ge(s.summed, u + 1)
                    if 2 * u + half:
                        pe.wait_ge(s.x_lo, 2 * u + half)
                    for k in range(4):
                        t = pe.transpose(tq[:, k], x[:, u % 3, (4 * half + k) * P:(4 * half + k + 1) * P], c.ident)
                    t.then_inc(s.x_turned, 1)

                turn(0)
                for u in range(TILES):
                    if u + 1 < TILES:
                        turn(u + 1)
                    for b in range(nb):
                        multiply(u, b)
                        if not ln and u and b < 2:
                            turn_x(u - 1, b)
                if not ln:
                    turn_x(TILES - 1, 0)
                    turn_x(TILES - 1, 1)

            @block.scalar
            def _(act):
                def keep(u, b):
                    act.wait_ge(s.turned, nb * u + b + 1)
                    if u and b < nb - 1:
                        act.wait_ge(s.passed, (nb - 1) * (u - 1) + b + 1)
                    elif u:
                        act.wait_ge(s.prod, u)
                    k0, kn = KB[b]
                    act.activation(mT[:, k0:k0 + kn], tp[:, b, 0:kn], ACT.Copy).then_inc(s.kept, 1)

                def round_x(u, half):
                    act.wait_ge(s.x_turned, 2 * u + half + 1)
                    act.activation(turned_out.hi[:, 4 * half:4 * half + 4, u * P:(u + 1) * P], tq[:], ACT.Copy)\
                       .then_inc(s.x_hi, 1)

                for b in range(nb):
                    keep(0, b)
                for u in range(TILES):
                    for b in range(nb):
                        if u + 1 < TILES:
                            keep(u + 1, b)
                        if not ln and u and b < 2:
                            round_x(u - 1, b)
                    if ln:
                        act.wait_ge(s.vars, u + 1)
                        act.activation(ag[:, 1:2], ag[:, 1:2], ACT.Ln, bias=c.eps[:, 1:2])
                        act.drain()
                        act.activation(ag[:, 1:2], ag[:, 1:2], ACT.Exp, scale=-0.5).then_inc(s.rs, 1)
                if not ln:
                    round_x(TILES - 1, 0)
                    round_x(TILES - 1, 1)

            @block.vector
            def _(dve):
                def rest_x(u):
                    for half in range(2):
                        place = (slice(None), slice(4 * half, 4 * half + 4), slice(u * P, (u + 1) * P))
                        dve.wait_ge(s.x_hi, 2 * u + half + 1)
                        dve.tensor_tensor(turned_out.lo[place], tq[:], turned_out.hi[place].bitcast(F32),
                                          ALU.subtract).then_inc(s.x_lo, 1)

                for u in range(TILES):
                    if not ln and u:
                        rest_x(u - 1)
                    dve.wait_ge(x_in[u % 3], 16 * (u // 3 + 1))
                    dve.wait_ge(s.prod, u + 1)
                    xt = x[:, u % 3]
                    xu = xt.rearrange("p (n c) -> p n c", n=2)
                    if not ln:
                        dve.tensor_tensor(xu, xu, acc[:, u % 2], ALU.add)
                        dve.drain().then_inc(s.added, 1)
                        dve.drain().then_inc(s.summed, 1)
                        continue
                    for n in range(2):
                        dve.scalar_tensor_tensor(out=xu[:, n], in0=xu[:, n], scalar=ALPHA, in1=acc[:, u % 2, n],
                                                 op0=ALU.mult, op1=ALU.add)
                    dve.drain().then_inc(s.added, 1)
                    for n in range(2):
                        dve.bn_stats(st[:, n], xu[:, n])
                    dve.drain()
                    dve.bn_aggr(ag[:], st[:].rearrange("p a b -> p (a b)"))
                    dve.drain().then_inc(s.vars, 1)
                    dve.wait_ge(s.rs, u + 1)
                    dve.tensor_scalar(xt, xt, ag[:, 0:1], ag[:, 1:2], ALU.subtract, ALU.mult)
                    dve.drain()
                    if u == 0:
                        dve.wait_ge(s.par_in, 32)
                    dve.tensor_tensor(xt, xt, gb[:, 0], ALU.mult)
                    dve.drain()
                    dve.tensor_tensor(xt, xt, gb[:, 1], ALU.add).then_inc(s.summed, 1)
                if not ln:
                    rest_x(TILES - 1)


INDEX_SIGNALS = "iq_ahead iq_scaled iq_turned iq_kept dots relus summed "
ATTEND_SIGNALS = ("q_ahead g_in silus q_turned q_kept ql_ps ql_kept biased logits added maxed exps turned kept weighed "
                  "o_kept o_ps y_done ")
HGRN_SIGNALS = ("hx_in hf_ahead sigs h_silus f_done logf turned_hq hq_kept turned_hk hk_kept sums b_kept pairs own_set "
                "diffs h_exps tilde picked e_in e_out ee_done ke_t ktok_done ho_ps up_ps sqd rs hy_done ")


BIAS_SIGNALS = "bias_in flipped flip_kept "


def bias_load(bias, s, table):

    def sync(sp):
        yield 0.003
        sp.dma_start(bias[:], bass.AP(tensor=table.tensor, offset=0, ap=[[1, P], [TAB, HEADS], [1, SKEW]]))\
          .then_inc(s.bias_in, 16)
        yield 1.0
        sp.wait_ge(s.bias_in, 16)

    return {"sync": sync}


def bias_flip(c, bias, s, big):
    FL = SKEW // 4
    n_all = 4 * HEADS
    part = lambda n: bias[:, n // 4, n % 4 * FL:(n % 4 + 1) * FL]

    def tensor(pe):
        for n in range(n_all):
            yield n / n_all
            if n >= 4:
                pe.wait_ge(s.flip_kept, n - 3)
            pe.matmul(big[:, 2 + n % 4, 0:FL], c.all[:, FLIP], part(n), start=True, stop=True).then_inc(s.flipped, 1)

    def vector(dve):
        for n in range(n_all):
            yield (n + 1) / n_all
            dve.wait_ge(s.flipped, n + 1)
            dve.tensor_copy(part(n), big[:, 2 + n % 4, 0:FL]).then_inc(s.flip_kept, 1)

    return {"tensor": tensor, "vector": vector}


def index_buffers(B, ikT, score):
    b = Named()
    b.ikT, b.score = ikT, score
    b.iq = B.sb("iq", [P, 2, IDX_HEADS, IDX_DIM])
    b.iw = B.sb("iw", [P, 2, 3, IDX_HEADS])
    b.iqT = B.sb("iqT", [IDX_DIM, IDX_HEADS, P])
    b.rel = B.sb("rel", [P, 2, 512])
    return b


def index_loads(b, sp, arrived, proj, k):
    tok = slice(k * P, (k + 1) * P)
    sp.dma_start(b.iw[:, k % 2, 0], proj[tok, E_IW:E_IW + IDX_HEADS]).then_inc(arrived, 16)
    sp.dma_start(b.iq[:, k % 2].rearrange("p h d -> p (h d)"), proj[tok, E_IQ:E_IQ + IDX_HEADS * IDX_DIM])\
      .then_inc(arrived, 16)
    return 32


def index_scores(c, b, s, proj, big, k):
    W = (k + 1) * P
    iq, iw, iqT, rel, score = b.iq[:, k % 2], b.iw[:, k % 2], b.iqT, b.rel, b.score[:, k % 2]
    PIECES = [(x, min(512, W - x)) for x in range(0, W, 512)]
    NP = len(PIECES)
    first = 0.06
    place = lambda n: first + (0.96 - first) * n / (IDX_HEADS * NP + 1)

    def sync(sp):
        if k:
            yield 0.001
            n = index_loads(b, sp, s.iq_ahead, proj, k - 1)
            yield 1.0
            sp.wait_ge(s.iq_ahead, n)

    def vector(dve):
        yield 0.0
        dve.scalar_tensor_tensor(out=iw[:, 1], in0=iw[:, 0], scalar=-1.0, in1=iw[:, 0], op0=ALU.mult, op1=ALU.max)
        dve.tensor_scalar(iw[:, 2], iw[:, 0], 0.0, 2.0, ALU.is_ge, ALU.mult)
        dve.drain()
        dve.tensor_scalar(iw[:, 1], iw[:, 1], float(IDX_HEADS ** -0.5 * IDX_DIM ** -0.5), None, ALU.mult)
        dve.tensor_scalar(iw[:, 2], iw[:, 2], -1.0, None, ALU.add)
        dve.drain()
        dve.tensor_tensor(iq, iq, spread(iw[:, 1], 2, IDX_DIM), ALU.mult).then_inc(s.iq_scaled, 1)
        n = 0
        for h in range(IDX_HEADS):
            for x, wd in PIECES:
                yield place(n + 1.4)
                dve.wait_ge(s.relus, n + 1)
                sg = iw[:, 2, h:h + 1]
                if h:
                    if NP == 1 or n % NP == 0:
                        dve.drain()
                    d = dve.scalar_tensor_tensor(out=score[:, x:x + wd], in0=rel[:, n % 2, 0:wd], scalar=sg,
                                                 in1=score[:, x:x + wd], op0=ALU.mult, op1=ALU.add)
                else:
                    d = dve.tensor_scalar(score[:, x:x + wd], rel[:, n % 2, 0:wd], sg, 0.0, ALU.mult, ALU.add)
                d.then_inc(s.summed, 1)
                n += 1
        yield 0.98
        dve.drain()
        dve.tensor_tensor(score[:, k * P:W], score[:, k * P:W], c.all[:, CHUNKED], ALU.add)

    def scalar(act):
        yield 0.04
        act.wait_ge(s.iq_turned, 1)
        act.activation(iqT[:].rearrange("p (a h) t -> p a (h t)", a=2), big[0:IDX_DIM, 0:2], ACT.Copy)\
           .then_inc(s.iq_kept, 1)
        n = 0
        for h in range(IDX_HEADS):
            for x, wd in PIECES:
                yield place(n + 0.5)
                act.wait_ge(s.dots, n + 1)
                if n >= 2:
                    act.wait_ge(s.summed, n - 1)
                act.activation(rel[:, n % 2, 0:wd], big[:, n % 2, 0:wd], ACT.Relu).then_inc(s.relus, 1)
                n += 1

    def tensor(pe):
        yield 0.03
        pe.wait_ge(s.iq_scaled, 1)
        for h in range(IDX_HEADS):
            m = pe.transpose(big[0:IDX_DIM, h // 4, (h % 4) * P:(h % 4 + 1) * P], iq[:, h], c.ident)
        m.then_inc(s.iq_turned, 1)
        n = 0
        for h in range(IDX_HEADS):
            for x, wd in PIECES:
                yield place(n)
                if n == 0:
                    pe.wait_ge(s.iq_kept, 1)
                if n >= 2:
                    pe.wait_ge(s.relus, n - 1)
                pe.matmul(big[:, n % 2, 0:wd], iqT[:, h], b.ikT[:, x:x + wd], start=True, stop=True)\
                  .then_inc(s.dots, 1)
                n += 1

    return {"sync": sync, "vector": vector, "scalar": scalar, "tensor": tensor}


def threshold_buffers(B, score, sel):
    b = Named()
    b.score, b.sel = score, sel
    b.hi = B.sb("hi", [P, SEQ], U16)
    b.lo = B.sb("lo", [P, SEQ], U16)
    b.eq = B.sb("eq", [P, SEQ])
    b.num = B.sb("num", [P, 8])
    return b


def select_keys(c, b, s, k):
    W = (k + 1) * P
    score, sel = b.score[:, k % 2, 0:W], b.sel[:, k % 2, 0:W]
    hi, lo, eq = b.hi[:, 0:W], b.lo[:, 0:W], b.eq[:, 0:W]
    seen = b.eq[:].bitcast(U16)[:, 0:W]
    cell = lambda n: b.num[:, n:n + 1]
    cand, count, hit, need, top, bits, sign, n_hi = (cell(n) for n in range(8))
    u = sel.bitcast(U32)
    halves = sel.bitcast(U16).rearrange("p (n a) -> p n a", a=2)
    KEEP = float(TOPK)

    def vector(dve):
        if W <= TOPK:
            yield 0.0
            dve.memset(sel, 0.0)
            dve.drain()
            dve.tensor_copy(b.sel[:, k % 2, k * P:W], c.all[:, CHUNKED])
            return

        def halve(x, wanted, place):
            dve.memset(cand, 32768.0)
            for bit in range(15, -1, -1):
                yield place + 0.44 * (15 - bit) / 16
                dve.drain()
                dve.tensor_scalar(seen, x, cand, 0.0, ALU.is_ge, ALU.add, accum_out=count)
                dve.drain()
                dve.tensor_scalar(hit, count, wanted, float(1 << bit), ALU.is_ge, ALU.mult)
                dve.drain()
                dve.scalar_tensor_tensor(out=cand, in0=hit, scalar=-float(1 << bit >> 1) if bit else -1.0, in1=cand,
                                         op0=ALU.add, op1=ALU.add)
            dve.drain()

        yield 0.0
        dve.tensor_scalar(u.bitcast(I32), score.bitcast(I32), 31, -2 ** 31, ALU.arith_shift_right, ALU.bitwise_or)
        dve.drain()
        dve.tensor_tensor(u, u, score.bitcast(U32), ALU.bitwise_xor)
        dve.drain()
        dve.tensor_copy(hi, halves[:, :, 1])
        yield from halve(hi, KEEP, 0.03)
        dve.tensor_copy(top, cand)
        dve.tensor_scalar(seen, hi, cand, 0.0, ALU.is_gt, ALU.add, accum_out=n_hi)
        dve.scalar_tensor_tensor(out=lo, in0=hi, scalar=cand, in1=halves[:, :, 0], op0=ALU.is_equal, op1=ALU.mult)
        dve.drain()
        dve.tensor_scalar(need, n_hi, -1.0, KEEP, ALU.mult, ALU.add)
        dve.drain()
        yield from halve(lo, need, 0.47)
        dve.tensor_scalar(seen, lo, cand, 0.0, ALU.is_gt, ALU.add, accum_out=count)
        dve.tensor_copy(bits.bitcast(U16)[:, 1:2], top)
        dve.tensor_copy(bits.bitcast(U16)[:, 0:1], cand)
        dve.drain()
        dve.tensor_scalar(sign.bitcast(I32), bits.bitcast(I32), 31, -1, ALU.arith_shift_right, ALU.bitwise_xor)
        dve.drain()
        dve.tensor_scalar(sign.bitcast(I32), sign.bitcast(I32), -2 ** 31, None, ALU.bitwise_or)
        dve.drain()
        dve.tensor_tensor(bits.bitcast(U32), bits.bitcast(U32), sign.bitcast(U32), ALU.bitwise_xor)
        dve.tensor_tensor(need, need, count, ALU.subtract)
        dve.drain()
        yield 0.9
        dve.tensor_scalar(eq, score, bits, None, ALU.is_equal)
        dve.drain()
        yield 0.92
        dve.tensor_tensor_scan(sel, eq, eq, 0.0, ALU.add, ALU.max)
        dve.drain()
        yield 0.94
        dve.scalar_tensor_tensor(out=eq, in0=sel, scalar=need, in1=eq, op0=ALU.is_le, op1=ALU.mult)
        dve.drain()
        yield 0.96
        dve.scalar_tensor_tensor(out=sel, in0=score, scalar=bits, in1=eq, op0=ALU.is_gt, op1=ALU.add)
        dve.drain()
        yield 0.98
        dve.tensor_scalar(sel, sel, -1.0, -NEG, ALU.add, ALU.mult)
        dve.drain()
        dve.tensor_tensor(b.sel[:, k % 2, k * P:W], b.sel[:, k % 2, k * P:W], c.all[:, CHUNKED], ALU.add)

    return {"vector": vector}


def attend_buffers(B, cT, ct, uk, uv, bias, sel):
    b = Named()
    b.cT, b.ct, b.uk, b.uv, b.bias, b.sel = cT, ct, uk, uv, bias, sel
    b.q = B.sb("q", [P, 2, 4 * P])
    b.gate = B.sb("gate", [P, 4, P])
    b.qT = B.sb("qT", [P, 4, P])
    b.ql = B.sb("ql", [P, 4, P])
    b.L = B.sb("L", [P, 2, SEQ])
    b.mx = B.sb("mx", [P, 4, 4])
    b.top = B.sb("top", [P, 4])
    b.den = B.sb("den", [P, 4])
    b.pT = B.sb("pT", [P, 2, 4, P])
    return b


def attend_loads(b, sp, arrived, proj, k):
    sp.dma_start(b.q[:, k % 2], proj[k * P:(k + 1) * P, E_Q:E_Q + 4 * P]).then_inc(arrived, 16)
    return 16


def attend(c, b, s, proj, big, k):
    H, R = 4, P
    W = (k + 1) * P
    gate, qT, ql, mx, top, den, pT, bias = b.gate, b.qT, b.ql, b.mx, b.top, b.den, b.pT, b.bias
    q = b.q[:, k % 2]
    oT, y = b.qT, q
    PIECES = [(x, min(512, W - x)) for x in range(0, W, 512)]
    NP = len(PIECES)
    tok = slice(k * P, (k + 1) * P)
    N = 13.1
    at_logits = lambda h, p: (2 + 2 * h + 1.6 * p / NP) / N
    at_exp = lambda h: (3.75 + 2 * h) / N
    at_turn = lambda h, p: (4.15 + 2 * h + 1.6 * (p + 0.5) / NP) / N
    pitch = 1.6 / NP / N
    uses = [("q", (s.q_kept, 1)), ("ql", (s.ql_kept, 1))]
    for h in range(H + 1):
        for p in range(NP):
            if h < H:
                uses.append((("L", h, p), (s.added, h * NP + p + 1)))
            if h:
                uses.append((("T", h - 1, p), (s.kept, (h - 1) * NP + p + 1)))
    uses += [("o", (s.y_done, 1))]
    turns = in_turn([2, 3, 4], uses)

    def bank(*key):
        return turns[key if len(key) > 1 else key[0]][0]

    def take(pe, *key):
        n, before = turns[key if len(key) > 1 else key[0]]
        if before:
            pe.wait_ge(*before)
        return n

    def sync(sp):
        yield 0.002
        sp.dma_start(gate[:].rearrange("p h d -> p (h d)"), proj[tok, E_G:E_G + H * P]).then_inc(s.g_in, 16)
        if k:
            n = attend_loads(b, sp, s.q_ahead, proj, k - 1)
            yield 1.0
            sp.wait_ge(s.q_ahead, n)

    def gpsimd(pool):
        for h in range(H):
            yield 0.0 if h < 2 else (1.65 + 2 * h) / N
            for p, (x, wd) in enumerate(PIECES):
                if h >= 2:
                    pool.wait_ge(s.turned, (h - 2) * NP + p + 1)
                x0 = (TILES - 1 - k) * P + x
                pool.tensor_tensor(b.L[:, h % 2, x:x + wd], b.sel[:, k % 2, x:x + wd], bias[:, h, x0:x0 + wd],
                                   ALU.add).then_inc(s.biased, 1)

    def scalar(act):
        yield 0.0
        act.wait_ge(s.q_turned, 1)
        act.activation(qT[:], big[:, bank("q")].rearrange("p (h t) -> p h t", h=H), ACT.Copy)\
           .then_inc(s.q_kept, 1)
        act.wait_ge(s.ql_ps, 1)
        act.activation(ql[:], big[:, bank("ql")].rearrange("p (h t) -> p h t", h=H), ACT.Copy,
                       scale=P ** -0.5).then_inc(s.ql_kept, 1)
        yield 1.2 / N
        act.wait_ge(s.g_in, 16)
        act.activation(gate[:], gate[:], ACT.Silu).then_inc(s.silus, 1)
        for h in range(H):
            if h:
                yield from keep(act, h - 1)
            yield at_exp(h)
            act.wait_ge(s.maxed, h + 1)
            act.activation(b.L[:, h % 2, 0:W], b.L[:, h % 2, 0:W], ACT.Exp, bias=top[:, h:h + 1],
                           accum_out=den[:, h:h + 1]).then_inc(s.exps, 1)
        yield from keep(act, H - 1)
        yield 12.0 / N
        act.wait_ge(s.weighed, H * NP)
        act.activation(oT[:], big[:, 5].rearrange("p (h t) -> p h t", h=H), ACT.Copy).then_inc(s.o_kept, 1)

    def keep(act, h):
        for p, (x, wd) in enumerate(PIECES):
            n = h * NP + p
            yield at_turn(h, p) + 0.4 * pitch
            act.wait_ge(s.turned, n + 1)
            if n >= 2:
                act.wait_ge(s.weighed, n - 1)
            act.activation(pT[:, n % 2, 0:wd // P],
                           big[:, bank("T", h, p), 0:wd].rearrange("p (b t) -> p b t", t=P), ACT.Copy)\
               .then_inc(s.kept, 1)

    def vector(dve):
        for h in range(H):
            for p, (x, wd) in enumerate(PIECES):
                yield at_logits(h, p) + 0.9 * pitch
                dve.wait_ge(s.biased, h * NP + p + 1)
                dve.wait_ge(s.logits, h * NP + p + 1)
                L = b.L[:, h % 2, x:x + wd]
                dve.tensor_tensor_reduce(L, big[:, bank("L", h, p), 0:wd], L, 1.0, 4 * NEG, ALU.add, ALU.max,
                                         mx[:, h, p:p + 1]).then_inc(s.added, 1)
            yield at_exp(h)
            dve.drain()
            dve.tensor_reduce(top[:, h:h + 1], mx[:, h, 0:NP], AX.X, ALU.max)
            dve.drain()
            dve.tensor_scalar(top[:, h:h + 1], top[:, h:h + 1], -1.0, None, ALU.mult).then_inc(s.maxed, 1)
        yield 12.0 / N
        dve.wait_ge(s.exps, H)
        dve.reciprocal(den[:], den[:])
        dve.wait_ge(s.silus, 1)
        dve.drain()
        dve.tensor_tensor(gate[:], gate[:], spread(den[:], 2, P), ALU.mult)
        dve.drain()
        yield 12.8 / N
        dve.wait_ge(s.o_ps, 1)
        dve.tensor_tensor(y.rearrange("p (h t) -> p h t", h=H),
                          big[:, bank("o")].rearrange("p (h t) -> p h t", h=H), gate[:], ALU.mult)\
           .then_inc(s.y_done, 1)

    def tensor(pe):
        yield 0.0
        n = take(pe, "q")
        for h in range(H):
            m = pe.transpose(big[:, n, h * P:(h + 1) * P], q[:, h * R:(h + 1) * R], c.ident)
        m.then_inc(s.q_turned, 1)
        pe.wait_ge(s.q_kept, 1)
        n = take(pe, "ql")
        for h in range(H):
            m = pe.matmul(big[:, n, h * P:(h + 1) * P], b.uk[:, h], qT[:, h], start=True, stop=True)
        m.then_inc(s.ql_ps, 1)
        for h in range(H + 1):
            for p in range(NP):
                if h < H:
                    yield at_logits(h, p)
                    if h == p == 0:
                        pe.wait_ge(s.ql_kept, 1)
                    logits(pe, h, p)
                if h:
                    yield at_turn(h - 1, p)
                    if p == 0:
                        pe.wait_ge(s.exps, h)
                    turn(pe, h - 1, p)
                    if p:
                        weigh(pe, h - 1, p - 1)
            if h:
                yield at_turn(h - 1, NP - 1) + 0.45 * pitch
                weigh(pe, h - 1, NP - 1)
        yield 12.0 / N
        pe.wait_ge(s.o_kept, 1)
        n = take(pe, "o")
        for h in range(H):
            m = pe.matmul(big[:, n, h * P:(h + 1) * P], oT[:, h], b.uv[:, h], start=True, stop=True)
        m.then_inc(s.o_ps, 1)

    def logits(pe, h, p):
        x, wd = PIECES[p]
        n = take(pe, "L", h, p)
        pe.matmul(big[:, n, 0:wd], ql[:, h], b.cT[:, x:x + wd], start=True, stop=True).then_inc(s.logits, 1)

    def turn(pe, h, p):
        x, wd = PIECES[p]
        n = take(pe, "T", h, p)
        for t in range(wd // P):
            m = pe.transpose(big[:, n, t * P:(t + 1) * P], b.L[:, h % 2, x + t * P:x + (t + 1) * P], c.ident)
        m.then_inc(s.turned, 1)

    def weigh(pe, h, p):
        x, wd = PIECES[p]
        pe.wait_ge(s.kept, h * NP + p + 1)
        for t in range(wd // P):
            m = pe.matmul(big[:, 5, h * P:(h + 1) * P], b.ct[:, x // P + t], pT[:, (h * NP + p) % 2, t],
                          start=(p == 0 and t == 0), stop=(x + (t + 1) * P == W))
        m.then_inc(s.weighed, 1)

    return {"sync": sync, "gpsimd": gpsimd, "vector": vector, "scalar": scalar, "tensor": tensor}


def hgrn_buffers(B, big):
    H = BH
    b = Named()
    b.lb = B.sb("lb", [P, 2, H * BD])
    b.g = B.sb("hg", [P, H * BD])
    b.state = B.sb("state", [P, H, BD])
    b.x = B.sb("x", [P, 3, H * BD])
    b.f = B.sb("f", [P, 2, H * BD])
    b.k = B.sb("k", [P, H * BD])
    b.kT = B.sb("kT", [P, H, P])
    b.hqT = B.sb("hqT", [P, H, P])
    b.bT = B.sb("bT", [P, H, P])
    b.E = B.sb("E", [P, 2, H, P])
    b.A = B.sb("A", [P, H, P])
    b.qe = B.sb("qe", [P, H, P])
    b.ke = B.sb("ke", [P, H, P])
    b.ktok = b.E[:, 1]
    b.dec = B.sb("dec", [P, H])
    b.y = B.sb("y", [P, 2, H, BD])
    b.ss = B.sb("ssq", [P, H])
    b.big = big
    return b


def hgrn_setup(nc, w, b):
    lb, g, E, state = b.lb, b.g, b.E, b.state
    load(nc, "hg_w", [(lb[:, 0], row(w['lb_logits_2'][0])), (lb[:, 1], row(w['lb_logits_2'][1])),
                      (g[:], row(w['hgrn_norm_g_2']))])
    with step(nc, "expd diffd cleared lbd") as (block, s):

        @block.vector
        def _(dve):
            dve.memset(state[:], 0.0).then_inc(s.cleared, 1)
            dve.tensor_tensor(E[:, 0].rearrange("p h t -> p (h t)"), lb[:, 0], lb[:, 1], ALU.max)
            dve.drain()
            for n in range(2):
                dve.tensor_tensor(lb[:, n], lb[:, n], E[:, 0].rearrange("p h t -> p (h t)"), ALU.subtract)
            dve.drain().then_inc(s.diffd, 1)
            dve.wait_ge(s.expd, 1)
            dve.tensor_tensor(lb[:, 1], lb[:, 0], lb[:, 1], ALU.add)
            dve.drain()
            dve.reciprocal(lb[:, 1], lb[:, 1])
            dve.drain()
            dve.tensor_tensor(lb[:, 0], lb[:, 0], lb[:, 1], ALU.mult)
            dve.drain()
            dve.tensor_scalar(lb[:, 1], lb[:, 0], -1.0, 1.0, ALU.mult, ALU.add).then_inc(s.lbd, 1)

        @block.scalar
        def _(act):
            act.wait_ge(s.diffd, 1)
            act.activation(lb[:], lb[:], ACT.Exp).then_inc(s.expd, 1)


def hgrn_loads(b, sp, arrived, proj, i):
    sp.dma_start(b.f[:, i % 2], proj[i * P:(i + 1) * P, H_F:H_F + BH * BD]).then_inc(arrived, 16)
    return 16


def hgrn_chunk(c, b, s, proj, i):
    H = BH
    lb, g, state, x, k, qT, kT, bT, E, A = b.lb, b.g, b.state, b.x, b.k, b.hqT, b.kT, b.bT, b.E, b.A
    qe, ke, ktok, dec, ss, big = b.qe, b.ke, b.ktok, b.dec, b.ss, b.big
    f, y = b.f[:, i % 2], b.y[:, i % 2]
    four = lambda n: big[:, n].rearrange("p (h t) -> p h t", h=H)
    tok = slice(i * P, (i + 1) * P)

    N = 29.0

    def halves(ap, l):
        v = ap.rearrange("p h (n a b) -> p h n a b", a=2, b=1 << l)
        return v[:, :, :, 0], v[:, :, :, 1]

    def joint(l):
        half = 1 << l
        v = bT[:].rearrange("p h (n a b) -> p h n a b", a=2, b=half)[:, :, :, 0, half - 1]
        return spread(v, 3, half)

    def sync(sp):
        yield 0.0
        sp.dma_start(x[:, 0], proj[tok, H_Q:H_Q + H * BD]).then_inc(s.hx_in, 16)
        sp.dma_start(x[:, 1:3].rearrange("p a c -> p (a c)"), proj[tok, H_I:H_I + 2 * H * BD]).then_inc(s.hx_in, 16)
        if i + 1 < TILES:
            n = hgrn_loads(b, sp, s.hf_ahead, proj, i + 1)
            yield 1.0
            sp.wait_ge(s.hf_ahead, n)

    def scalar(act):
        yield 0.0
        act.activation(f, f, ACT.Sigmoid).then_inc(s.sigs, 1)
        yield 2.2 / N
        act.wait_ge(s.hx_in, 32)
        act.activation(x[:, 0], x[:, 0], ACT.Silu)
        act.activation(x[:, 2], x[:, 2], ACT.Silu).then_inc(s.h_silus, 1)
        yield 3 / N
        act.wait_ge(s.f_done, 1)
        act.activation(f, f, ACT.Ln).then_inc(s.logf, 1)
        act.wait_ge(s.turned_hq, 1)
        act.activation(qT[:], four(6), ACT.Copy).then_inc(s.hq_kept, 1)
        act.wait_ge(s.turned_hk, 1)
        act.activation(kT[:], four(7), ACT.Copy).then_inc(s.hk_kept, 1)
        yield 4 / N
        act.wait_ge(s.sums, 1)
        act.activation(bT[:], four(6), ACT.Copy).then_inc(s.b_kept, 1)
        for l in range(LEVELS):
            yield (6.5 + 2 * l) / N
            act.wait_ge(s.diffs, 2 * (l + 1))
            act.activation(E[:, l % 2], E[:, l % 2], ACT.Exp).then_inc(s.h_exps, 1)
            if l == 0:
                yield 7.2 / N
                act.wait_ge(s.e_in, 1)
                act.activation(ke[:], ke[:], ACT.Exp)
                act.drain()
                act.activation(qe[:], bT[:], ACT.Exp)
                act.activation(dec[:], bT[:, :, P - 1], ACT.Exp).then_inc(s.e_out, 1)
        yield 23.5 / N
        act.wait_ge(s.ke_t, 1)
        act.activation(ktok, four(7), ACT.Copy).then_inc(s.ktok_done, 1)
        yield 24.5 / N
        act.wait_ge(s.ho_ps, 1)
        act.activation(y, four(6), ACT.Copy)
        act.drain()
        for h in range(H):
            act.activation(E[:, 0, h], y[:, h], ACT.Square, accum_out=ss[:, h:h + 1])
        act.drain().then_inc(s.sqd, 1)
        rstd(act, c, ss[:], BD).then_inc(s.rs, 1)

    def gpsimd(pool):
        def diffs(l):
            if l >= 2:
                pool.wait_ge(s.pairs, l)
            (e0, e1), (b0, b1) = halves(E[:, l % 2], l), halves(bT[:], l)
            pool.tensor_tensor(e0, joint(l), b0, ALU.subtract).then_inc(s.diffs, 1)
            pool.tensor_tensor(e1, b1, joint(l), ALU.subtract).then_inc(s.diffs, 1)

        def tilde(l):
            e0, e1 = halves(E[:, l % 2], l)
            pool.wait_ge(s.h_exps, l + 1)
            pool.tensor_tensor(e0, e0, halves(kT[:], l)[0], ALU.mult).then_inc(s.tilde, 1)
            pool.tensor_tensor(e1, e1, halves(qT[:], l)[1], ALU.mult).then_inc(s.tilde, 1)

        yield 6 / N
        pool.wait_ge(s.b_kept, 1)
        diffs(0)
        pool.tensor_tensor(ke[:], spread(bT[:, :, P - 1], 2, P), bT[:], ALU.subtract).then_inc(s.e_in, 1)
        for l in range(LEVELS):
            if l + 1 < LEVELS:
                yield (7 + 2 * l) / N
                diffs(l + 1)
            yield (7.5 + 2 * l) / N
            tilde(l)
        yield 20 / N
        pool.wait_ge(s.e_out, 1)
        pool.tensor_tensor(ke[:], ke[:], kT[:], ALU.mult)
        pool.tensor_tensor(qe[:], qe[:], qT[:], ALU.mult)
        pool.drain().then_inc(s.ee_done, 1)
        yield 25 / N
        y2 = y.rearrange("p h d -> p (h d)")
        pool.wait_ge(s.sqd, 1)
        pool.tensor_tensor(y2, y2, g[:], ALU.mult)
        pool.drain()
        pool.tensor_tensor(y2, y2, x[:, 2], ALU.mult)
        pool.wait_ge(s.rs, 1)
        pool.drain()
        pool.tensor_tensor(y, y, spread(ss[:], 2, BD), ALU.mult).then_inc(s.hy_done, 1)

    def vector(dve):
        yield 1.2 / N
        dve.wait_ge(s.sigs, 1)
        dve.tensor_tensor(f, f, lb[:, 1], ALU.mult)
        dve.drain()
        dve.tensor_tensor(f, f, lb[:, 0], ALU.add)
        dve.drain()
        dve.tensor_scalar(k[:], f, -1.0, 1.0, ALU.mult, ALU.add)
        dve.drain().then_inc(s.f_done, 1)

        def pick(l):
            dve.wait_ge(s.pairs, l + 2)
            dve.drain()
            dve.copy_predicated(A[:], spread(c.all[:, LEVEL[l]].bitcast(U32), 1, H), four(6 + l % 2))\
               .then_inc(s.picked, 1)

        yield 6 / N
        dve.wait_ge(s.pairs, 1)
        dve.tensor_tensor(A[:], four(7), spread(c.ident, 1, H), ALU.mult).then_inc(s.own_set, 1)
        for l in range(LEVELS):
            if l:
                yield (9.3 + 2 * l) / N
                pick(l - 1)
        yield 22.9 / N
        pick(LEVELS - 1)
        yield 28 / N
        dve.wait_ge(s.up_ps, 1)
        for h in range(H):
            dve.scalar_tensor_tensor(out=state[:, h], in0=state[:, h], scalar=dec[:, h:h + 1],
                                     in1=big[:, 7, h * BD:(h + 1) * BD], op0=ALU.mult, op1=ALU.add)

    def tensor(pe):
        yield 1.8 / N
        pe.wait_ge(s.f_done, 1)
        for h in range(H):
            m = pe.transpose(big[:, 7, h * P:(h + 1) * P], k[:, h * BD:(h + 1) * BD], c.ident)
        m.then_inc(s.turned_hk, 1)
        yield 2.6 / N
        pe.wait_ge(s.h_silus, 1)
        for h in range(H):
            m = pe.transpose(big[:, 6, h * P:(h + 1) * P], x[:, 0, h * BD:(h + 1) * BD], c.ident)
        m.then_inc(s.turned_hq, 1)
        yield 3.5 / N
        pe.wait_ge(s.logf, 1)
        pe.wait_ge(s.hq_kept, 1)
        for h in range(H):
            m = pe.matmul(big[:, 6, h * P:(h + 1) * P], f[:, h * BD:(h + 1) * BD], c.upto, start=True, stop=True)
        m.then_inc(s.sums, 1)
        yield 5 / N
        pe.wait_ge(s.hk_kept, 1)
        for h in range(H):
            m = pe.matmul(big[:, 7, h * P:(h + 1) * P], kT[:, h], qT[:, h], start=True, stop=True)
        m.then_inc(s.pairs, 1)
        for l in range(LEVELS):
            yield (8.4 + 2 * l) / N
            pe.wait_ge(s.tilde, 2 * (l + 1))
            if l == 0:
                pe.wait_ge(s.b_kept, 1)
            elif l == 1:
                pe.wait_ge(s.own_set, 1)
            else:
                pe.wait_ge(s.picked, l - 1)
            for h in range(H):
                m = pe.matmul(big[:, 6 + l % 2, h * P:(h + 1) * P], E[:, l % 2, h], E[:, l % 2, h],
                              start=True, stop=True)
            m.then_inc(s.pairs, 1)
        yield 23 / N
        pe.wait_ge(s.ee_done, 1)
        pe.wait_ge(s.picked, LEVELS - 1)
        for h in range(H):
            m = pe.transpose(big[:, 7, h * P:(h + 1) * P], ke[:, h], c.ident)
        m.then_inc(s.ke_t, 1)
        yield 24 / N
        pe.wait_ge(s.picked, LEVELS)
        for h in range(H):
            v = x[:, 1, h * BD:(h + 1) * BD]
            pe.matmul(big[:, 6, h * BD:(h + 1) * BD], qe[:, h], state[:, h], start=True, stop=False)
            m = pe.matmul(big[:, 6, h * BD:(h + 1) * BD], A[:, h], v, start=False, stop=True)
        m.then_inc(s.ho_ps, 1)
        yield 25 / N
        pe.wait_ge(s.ktok_done, 1)
        for h in range(H):
            m = pe.matmul(big[:, 7, h * BD:(h + 1) * BD], ktok[:, h], x[:, 1, h * BD:(h + 1) * BD],
                          start=True, stop=True)
        m.then_inc(s.up_ps, 1)

    return {"sync": sync, "gpsimd": gpsimd, "vector": vector, "scalar": scalar, "tensor": tensor}


def second_mixers(nc, c, w, proj, mix, table, onehot):
    H, R, KEEP = 4, 128, float(TOPK)
    with ExitStack() as ctx:
        B = Buffers(nc, ctx, "ds")
        cT = B.sb("cT", [P, SEQ])
        ct = B.sb("ct", [P, TILES, R])
        ikT = B.sb("ikT", [IDX_DIM, SEQ])
        uk = B.sb("uk", [P, H, R])
        uv = B.sb("uv", [P, H, P])
        bias = B.sb("bias", [P, H, SKEW])
        big = B.ps("big", [P, 8, 512])
        with ExitStack() as early:
            E = Buffers(nc, early, "dp")
            g = E.sb("g", [P, R])
            ik = E.sb("ik", [P, TILES, IDX_DIM])
            sq = E.sb("sq", [P, TILES, R])
            ss = E.sb("ss", [P, TILES])
            rb = E.sb("rb", [BUCKETS, H])
            oh = E.sb("oh", [BUCKETS, TAB])
            tb = E.sb("tb", [H, TAB])
            load(nc, "ds_w", [(uk[:], w['w_uk_2'].rearrange("h d r -> d h r")),
                              (uv[:], w['w_uv_2'].rearrange("h r v -> r h v")), (g[:], row(w['kv_norm_g_2'])),
                              (ik[:], proj[:, E_IK:E_IK + IDX_DIM].rearrange("(t p) c -> p t c", p=P)),
                              (ct[:], proj[:, E_C:E_C + R].rearrange("(t p) c -> p t c", p=P)),
                              (rb[:], w['rel_bias_2']), (oh[:], onehot)])
            with step(nc, "squares rs normed turned kept biases bias_kept table_out ik_t ik_kept") as (block, s):

                @block.vector
                def _(dve):
                    dve.tensor_tensor(sq[:], ct[:], ct[:], ALU.mult)
                    dve.drain()
                    dve.tensor_reduce(ss[:], sq[:], AX.X, ALU.add).then_inc(s.squares, 1)
                    dve.tensor_tensor(ct[:], ct[:], spread(g[:], 1, TILES), ALU.mult)
                    dve.wait_ge(s.rs, 1)
                    dve.drain()
                    dve.tensor_tensor(ct[:], ct[:], spread(ss[:], 2, R), ALU.mult).then_inc(s.normed, 1)
                    dve.wait_ge(s.biases, 1)
                    dve.tensor_copy(tb[:].rearrange("h (a b) -> h a b", a=5), big[0:H, 0:5]).then_inc(s.bias_kept, 1)
                    dve.wait_ge(s.turned, 1)
                    dve.tensor_copy(cT[:].rearrange("p (a b) -> p a b", a=4), big[:, 0:4]).then_inc(s.kept, 1)
                    dve.wait_ge(s.ik_t, 1)
                    dve.tensor_copy(ikT[:].rearrange("p (a b) -> p a b", a=4), big[0:IDX_DIM, 4:8])\
                       .then_inc(s.ik_kept, 1)

                @block.scalar
                def _(act):
                    act.wait_ge(s.squares, 1)
                    rstd(act, c, ss[:], R).then_inc(s.rs, 1)

                @block.tensor
                def _(pe):
                    for k in range(5):
                        m = pe.matmul(big[0:H, k], rb[:], oh[:, k * 512:(k + 1) * 512], start=True, stop=True)
                    m.then_inc(s.biases, 1)
                    pe.wait_ge(s.bias_kept, 1)
                    pe.wait_ge(s.normed, 1)
                    for t in range(TILES):
                        m = pe.transpose(big[:, t // 4, (t % 4) * P:(t % 4 + 1) * P], ct[:, t], c.ident)
                    m.then_inc(s.turned, 1)
                    for t in range(TILES):
                        m = pe.transpose(big[0:IDX_DIM, 4 + t // 4, (t % 4) * P:(t % 4 + 1) * P], ik[:, t], c.ident)
                    m.then_inc(s.ik_t, 1)

                @block.sync
                def _(sp):
                    sp.wait_ge(s.bias_kept, 1)
                    sp.dma_start(table, tb[:]).then_inc(s.table_out, 16)
                    sp.wait_ge(s.table_out, 16)

        score = B.sb("score", [P, 2, SEQ])
        sel = B.sb("sel", [P, 2, SEQ])
        ib = index_buffers(B, ikT, score)
        tb = threshold_buffers(B, score, sel)
        ab = attend_buffers(B, cT, ct, uk, uv, bias, sel)
        hb = hgrn_buffers(B, big)
        hgrn_setup(nc, w, hb)
        with step(nc, "arrived") as (block, s):

            @block.sync
            def _(sp):
                n = index_loads(ib, sp, s.arrived, proj, TILES - 1) + attend_loads(ab, sp, s.arrived, proj, TILES - 1)
                n += hgrn_loads(hb, sp, s.arrived, proj, 0)
                sp.wait_ge(s.arrived, n)

        order = list(range(TILES - 1, -1, -1))
        for k in range(TILES + 3):
            names, branches = "stored ", []
            if k < TILES:
                names += INDEX_SIGNALS + HGRN_SIGNALS
            if 2 <= k < TILES + 2:
                names += ATTEND_SIGNALS
            if k < 2:
                names += BIAS_SIGNALS
            with step(nc, names) as (block, s):
                if k == 0:
                    branches.append(bias_load(bias, s, table))
                if k == 1:
                    branches.append(bias_flip(c, bias, s, big))
                if k < TILES:
                    branches.append(index_scores(c, ib, s, proj, big, order[k]))
                if 1 <= k <= TILES:
                    branches.append(select_keys(c, tb, s, order[k - 1]))
                if 2 <= k < TILES + 2:
                    branches.append(attend(c, ab, s, proj, big, order[k - 2]))
                if k < TILES:
                    branches.append(hgrn_chunk(c, hb, s, proj, k))

                @block.sync
                def _(sp):
                    stores = 0
                    if k >= 3:
                        t = order[k - 3]
                        sp.dma_start(mix[t * P:(t + 1) * P, 0:512], ab.q[:, t % 2]).then_inc(s.stored, 16)
                        stores += 1
                    if 1 <= k <= TILES:
                        t = k - 1
                        sp.dma_start(mix[t * P:(t + 1) * P, 512:1024], hb.y[:, t % 2].rearrange("p h d -> p (h d)"))\
                          .then_inc(s.stored, 16)
                        stores += 1
                    if stores:
                        sp.wait_ge(s.stored, 16 * stores)
                    together(sp, "sync", branches)

                @block.gpsimd
                def _(pool):
                    together(pool, "gpsimd", branches)

                @block.scalar
                def _(act):
                    together(act, "scalar", branches)

                @block.vector
                def _(dve):
                    together(dve, "vector", branches)

                @block.tensor
                def _(pe):
                    together(pe, "tensor", branches)


def program(nc, t, consts, onehot, out):
    w = {n: (v[0] if v.shape[0] == 1 else v) for n, v in t.items()}
    out = out[0]

    def scratch(name, shape):
        return nc.dram_tensor(name, shape, F32, kind="Internal").ap()

    proj1, mixed1 = scratch("proj1", [SEQ + PAD, COLS1]), scratch("mixed1", [SEQ, MIX1])
    x2 = scratch("x2", [SEQ, D_MODEL])
    proj2, mixed2 = scratch("proj2", [SEQ, COLS2]), scratch("mixed2", [SEQ, D_MODEL])
    table = scratch("table", [HEADS, TAB])
    with ExitStack() as ctx:
        c = load_constants(nc, ctx, consts)
        with ExitStack() as own:
            zero_rows(nc, proj1)
            hT = Split(Buffers(nc, own, "first"), "hT", [P, KD, SEQ])
            norm_transpose(nc, c, w['x'], w['norm_g'], hT, "n1")
            gemm(nc, c, hT, w['w_in'], proj1, COLS1, "g1", PAD)
        memory_and_mlstm(nc, c, w, proj1, mixed1)
        fox_rwkv_and_gating(nc, c, w, proj1, mixed1)
        with ExitStack() as own:
            hT = Split(Buffers(nc, own, "second"), "hT", [P, KD, SEQ])
            project_out(nc, c, mixed1, w['w_out'], w['x'], x2, "po", turned_out=hT)
            gemm(nc, c, hT, w['w_in_2'], proj2, COLS2, "g2", 0)
        second_mixers(nc, c, w, proj2, mixed2, table, onehot)
        project_out(nc, c, mixed2, w['w_o_2'], x2, out, "pf", ln=(w['ln_g_2'], w['ln_b_2']))


INPUTS = """x mem norm_g w_in w_out sgu_norm_g sgu_w sgu_b fox_q_g fox_k_g fox_f_b mlstm_conv_w mlstm_conv_b
mlstm_i_b mlstm_f_b mlstm_out_g rwkv_mu rwkv_w0 rwkv_w2 rwkv_a0 rwkv_a2 rwkv_k_k rwkv_k_a rwkv_r_k rwkv_ln_g
mem_norm_g mem_w_kv mem_q_g mem_k_g w_in_2 w_uk_2 w_uv_2 kv_norm_g_2 rel_bias_2 lb_logits_2 hgrn_norm_g_2 w_o_2
ln_g_2 ln_b_2""".split()


def kernel(**inputs):
    import concourse.bacc as bacc
    from concourse.bass_utils import run_bass_kernel_spmd

    nc = bacc.Bacc("TRN2", target_bir_lowering=False, num_devices=1)
    arrays, views = {}, {}
    for n in INPUTS:
        a = np.ascontiguousarray(inputs[n])
        arrays[f"in_{n}"] = a
        views[n] = nc.dram_tensor(f"in_{n}", a.shape, F32, kind="ExternalInput").ap()
    made = {"consts": shape_constants(), "onehot": bucket_table()}
    for n, a in made.items():
        arrays[n] = a
        views[n] = nc.dram_tensor(n, a.shape, F32, kind="ExternalInput").ap()
    out = nc.dram_tensor("out", [1, SEQ, D_MODEL], F32, kind="ExternalOutput").ap()
    program(nc, {n: views[n] for n in INPUTS}, views["consts"], views["onehot"], out)
    r = run_bass_kernel_spmd(nc, [arrays], core_ids=[0])
    return r.results[0]["out"]
```
